# Optimizing a Trainium2 kernel written in Bass

```python
import jax, jax.numpy as jnp
from jax import lax
import numpy as np

D_MODEL = 1024
BATCH = 1
SEQ = 512
DEPTH = 2

PLE_DIM = 256
RMS_EPS = 1e-6
LB_FLOOR = 1e-30
HG_HEADS = 4
HG_HEAD_DIM = 128
HG_WIDTH = HG_HEADS * HG_HEAD_DIM
HG_CHUNK = 64
M2_HEADS = 8
M2_HEAD_DIM = 64
M2_INNER = M2_HEADS * M2_HEAD_DIM
M2_GROUPS = 2
M2_STATE = 128
M2_CONV = 5
M2_CHUNK = 128
M2_XBC = M2_INNER + 2 * M2_GROUPS * M2_STATE
EVEN_IN_WIDTH = 5 * HG_WIDTH + M2_INNER + M2_XBC + 2 * M2_HEADS
EVEN_MIX_WIDTH = HG_WIDTH + M2_INNER
S5_GROUP_SIZE = 16
S5_GROUPS = D_MODEL // S5_GROUP_SIZE
S5_STATE = 64
S5_DT_MIN = 1e-3
S5_DT_MAX = 1e-1
D_FF = 3584
N_EXPERTS = 8
TOP_K = 2
MOE_BLOCK = 128

kernel_name = 'hybrid_hgrn2_ssd_s5_moe_encoder'

F32 = jnp.float32

def rmsnorm(x, w):
    xf = x.astype(F32)
    y = xf * lax.rsqrt(jnp.mean(xf * xf, axis=-1, keepdims=True) + RMS_EPS)
    return (y * w.astype(F32)).astype(x.dtype)

def _flip(t):
    return jnp.flip(t, axis=1)

def _masked_exp(mask, t):
    return jnp.where(mask, jnp.exp(jnp.where(mask, t, 0.0)), 0.0)

def _hgrn2_one_direction(q, k, v, logf):
    b, s, h, dk = q.shape
    dv = v.shape[-1]
    nc = s // HG_CHUNK

    def chunks(t):
        return t.reshape(b, nc, HG_CHUNK, h, t.shape[-1]).transpose(1, 0, 3, 2, 4)

    qc, kc, vc = chunks(q), chunks(k), chunks(v)
    bc = jnp.cumsum(chunks(logf), axis=3)
    mask = jnp.tril(jnp.ones((HG_CHUNK, HG_CHUNK), bool))[:, :, None]

    def step(state, inp):
        qi, ki, vi, bi = inp
        diff = bi[:, :, :, None, :] - bi[:, :, None, :, :]
        decay = _masked_exp(mask, diff)
        scores = jnp.einsum('bhtsd,bhsd->bhts', decay * qi[:, :, :, None, :], ki)
        o = (jnp.einsum('bhts,bhsv->bhtv', scores, vi)
             + jnp.einsum('bhtd,bhdv->bhtv', qi * jnp.exp(bi), state))
        b_end = bi[:, :, -1, :]
        k_dec = ki * jnp.exp(b_end[:, :, None, :] - bi)
        state = jnp.exp(b_end)[..., None] * state + jnp.einsum('bhsd,bhsv->bhdv', k_dec, vi)
        return state, o

    state0 = jnp.zeros((b, h, dk, dv), q.dtype)
    _, out = lax.scan(step, state0, (qc, kc, vc, bc))
    return out.transpose(1, 0, 3, 2, 4).reshape(b, s, h, dv)

def hgrn2_mixer(q_pre, ff_pre, fb_pre, i_pre, g_pre, lb, norm_w):
    b, s, _ = q_pre.shape
    shp = (b, s, HG_HEADS, HG_HEAD_DIM)
    q = jax.nn.silu(q_pre.astype(F32)).reshape(shp)
    v = i_pre.astype(F32).reshape(shp)
    lb = lb.astype(F32).reshape(HG_HEADS, HG_HEAD_DIM)
    log_lb, log_1m_lb = jnp.log(jnp.maximum(lb, LB_FLOOR)), jnp.log1p(-lb)

    def forget(f_pre):
        logf = jnp.logaddexp(log_lb, log_1m_lb + jax.nn.log_sigmoid(f_pre.astype(F32).reshape(shp)))
        return logf, -jnp.expm1(logf)

    logf_f, k_f = forget(ff_pre)
    logf_b, k_b = forget(fb_pre)
    o = (_hgrn2_one_direction(q, k_f, v, logf_f)
         + _flip(_hgrn2_one_direction(_flip(q), _flip(k_b), _flip(v), _flip(logf_b))))
    o = o * lax.rsqrt(jnp.mean(o * o, axis=-1, keepdims=True) + RMS_EPS)
    return o.reshape(b, s, HG_WIDTH) * norm_w.astype(F32) * jax.nn.sigmoid(g_pre.astype(F32))

def _centred_depthwise_conv(x, w, bias):
    ch, width = x.shape[-1], w.shape[0]
    y = lax.conv_general_dilated(x, w[:, None, :].astype(x.dtype), window_strides=(1,),
                                 padding=[(width // 2, width // 2)],
                                 dimension_numbers=('NWC', 'WIO', 'NWC'),
                                 feature_group_count=ch)
    return y + bias.astype(x.dtype)

def _ssd_one_direction(x, dt, a, bm, cm):
    b, s, h, p = x.shape
    g, n = bm.shape[2], bm.shape[3]
    hg, l = h // g, M2_CHUNK
    nc = s // l
    xc = x.reshape(b, nc, l, g, hg, p)
    dtc = dt.reshape(b, nc, l, g, hg)
    bc = bm.reshape(b, nc, l, g, n)
    cc = cm.reshape(b, nc, l, g, n)
    acum = jnp.cumsum(dtc * a.reshape(g, hg), axis=2)
    mask = jnp.tril(jnp.ones((l, l), bool))[:, :, None, None]
    seg = acum[:, :, :, None] - acum[:, :, None, :]
    decay = _masked_exp(mask, seg)
    cb = jnp.einsum('bclgn,bcsgn->bclsg', cc, bc)
    w = cb[..., None] * decay * dtc[:, :, None]
    y_diag = jnp.einsum('bclsgh,bcsghp->bclghp', w, xc)
    to_end = jnp.exp(acum[:, :, -1:] - acum) * dtc
    states = jnp.einsum('bclgn,bclghp->bcghpn', bc, to_end[..., None] * xc)
    chunk_decay = jnp.exp(acum[:, :, -1])

    def step(hstate, inp):
        st, dc = inp
        return dc[..., None, None] * hstate + st, hstate

    h0 = jnp.zeros((b, g, hg, p, n), x.dtype)
    _, prev = lax.scan(step, h0, (jnp.moveaxis(states, 1, 0), jnp.moveaxis(chunk_decay, 1, 0)))
    prev = jnp.moveaxis(prev, 0, 1)
    y_off = jnp.einsum('bclgn,bcghpn->bclghp', cc, prev) * jnp.exp(acum)[..., None]
    return (y_diag + y_off).reshape(b, s, h, p)

def mamba2_mixer(z, xbc, dt_raw, conv_w, conv_b, dt_bias, a_log, d_skip, norm_w):
    b, s, _ = z.shape
    xbc = jax.nn.silu(_centred_depthwise_conv(xbc, conv_w, conv_b)).astype(F32)
    nb = M2_GROUPS * M2_STATE
    xs = xbc[..., :M2_INNER].reshape(b, s, M2_HEADS, M2_HEAD_DIM)
    bm = xbc[..., M2_INNER:M2_INNER + nb].reshape(b, s, M2_GROUPS, M2_STATE)
    cm = xbc[..., M2_INNER + nb:].reshape(b, s, M2_GROUPS, M2_STATE)
    dt = jax.nn.softplus(dt_raw.astype(F32).reshape(b, s, 2, M2_HEADS) + dt_bias.astype(F32))
    a = -jnp.exp(a_log.astype(F32))
    y = (_ssd_one_direction(xs, dt[:, :, 0], a[0], bm, cm)
         + _flip(_ssd_one_direction(_flip(xs), _flip(dt[:, :, 1]), a[1], _flip(bm), _flip(cm)))
         + d_skip.astype(F32)[:, None] * xs)
    y = y.reshape(b, s, M2_INNER) * jax.nn.silu(z.astype(F32))
    yg = y.reshape(b, s, M2_GROUPS, M2_INNER // M2_GROUPS)
    yg = yg * lax.rsqrt(jnp.mean(yg * yg, axis=-1, keepdims=True) + RMS_EPS)
    return yg.reshape(b, s, M2_INNER) * norm_w.astype(F32)

def even_mixer(hn, w_in, w_out, lb, hg_norm_w, conv_w, conv_b, dt_bias, a_log, d_skip, m2_norm_w):
    proj = hn @ w_in
    sizes = [HG_WIDTH] * 5 + [M2_INNER, M2_XBC, 2 * M2_HEADS]
    q, ff, fb, i, g, z, xbc, dt_raw = jnp.split(proj, list(np.cumsum(sizes)[:-1]), axis=-1)
    o_a = hgrn2_mixer(q, ff, fb, i, g, lb, hg_norm_w)
    o_b = mamba2_mixer(z, xbc, dt_raw, conv_w, conv_b, dt_bias, a_log, d_skip, m2_norm_w)
    return jnp.concatenate([o_a, o_b], axis=-1).astype(hn.dtype) @ w_out

def _complex_affine_combine(left, right):
    a1r, a1i, b1r, b1i = left
    a2r, a2i, b2r, b2i = right
    return (a2r * a1r - a2i * a1i, a2r * a1i + a2i * a1r,
            a2r * b1r - a2i * b1i + b2r, a2r * b1i + a2i * b1r + b2i)

def _s5_one_direction(ug, a_re, a_im, log_step, b_re, b_im, c_re, c_im):
    delta = jnp.exp(log_step)[:, None]
    mag = jnp.exp(a_re * delta)
    lam_re, lam_im = mag * jnp.cos(a_im * delta), mag * jnp.sin(a_im * delta)
    den = a_re * a_re + a_im * a_im
    num_re = lam_re - 1.0
    coef_re = (num_re * a_re + lam_im * a_im) / den
    coef_im = (lam_im * a_re - num_re * a_im) / den
    bb_re = coef_re[..., None] * b_re - coef_im[..., None] * b_im
    bb_im = coef_re[..., None] * b_im + coef_im[..., None] * b_re
    bu_re = jnp.einsum('bsgc,gnc->bsgn', ug, bb_re)
    bu_im = jnp.einsum('bsgc,gnc->bsgn', ug, bb_im)
    s = ug.shape[1]
    lam_re_s = jnp.broadcast_to(lam_re, (s,) + lam_re.shape)
    lam_im_s = jnp.broadcast_to(lam_im, (s,) + lam_im.shape)

    def scan_seq(br, bi):
        _, _, hr, hi = lax.associative_scan(_complex_affine_combine, (lam_re_s, lam_im_s, br, bi), axis=0)
        return hr, hi

    h_re, h_im = jax.vmap(scan_seq)(bu_re, bu_im)
    return jnp.einsum('bsgn,gcn->bsgc', h_re, c_re) - jnp.einsum('bsgn,gcn->bsgc', h_im, c_im)

def s5_mixer(hn, a_re, a_im, log_step, b_re, b_im, c_re, c_im, d_skip, glu_w):
    b, s, d = hn.shape
    hf = hn.astype(F32)
    u = hf.reshape(b, s, S5_GROUPS, S5_GROUP_SIZE)
    a_re, a_im, log_step = a_re.astype(F32), a_im.astype(F32), log_step.astype(F32)
    b_re, b_im, c_re, c_im = b_re.astype(F32), b_im.astype(F32), c_re.astype(F32), c_im.astype(F32)
    y = (_s5_one_direction(u, a_re[0], a_im[0], log_step[0], b_re, b_im, c_re[0], c_im[0])
         + _flip(_s5_one_direction(_flip(u), a_re[1], a_im[1], log_step[1], b_re, b_im, c_re[1], c_im[1])))
    y = y.reshape(b, s, d) + d_skip.astype(F32) * hf
    out, gate = jnp.split(jax.nn.gelu(y).astype(hn.dtype) @ glu_w, 2, axis=-1)
    return out * jax.nn.sigmoid(gate)

def swiglu(h, w_gu, w_down):
    g, u = jnp.split(h @ w_gu, 2, axis=-1)
    return (jax.nn.silu(g) * u) @ w_down

def moe_swiglu(h, w_router, w_gu, w_down):
    b, s, d = h.shape
    t = b * s
    xt = h.reshape(t, d)
    logits = (xt @ w_router).astype(F32)
    top_logit, top_e = lax.top_k(logits, TOP_K)
    gates = jax.nn.softmax(top_logit, axis=-1).astype(h.dtype)
    n_assign = t * TOP_K
    flat_e = top_e.reshape(-1)
    flat_tok = jnp.repeat(jnp.arange(t, dtype=jnp.int32), TOP_K)
    flat_w = gates.reshape(-1)
    order = jnp.argsort(flat_e)
    se, stok, sw = flat_e[order], flat_tok[order], flat_w[order]
    counts = jnp.bincount(flat_e, length=N_EXPERTS)
    start = jnp.cumsum(counts) - counts
    padded = (counts + MOE_BLOCK - 1) // MOE_BLOCK * MOE_BLOCK
    pend = jnp.cumsum(padded)
    pstart = pend - padded
    dest = pstart[se] + jnp.arange(n_assign, dtype=jnp.int32) - start[se]
    n_rows = (-(-n_assign // MOE_BLOCK) + N_EXPERTS) * MOE_BLOCK
    n_blocks = n_rows // MOE_BLOCK
    x_buf = jnp.zeros((n_rows, d), h.dtype).at[dest].set(xt[stok])
    w_buf = jnp.zeros((n_rows,), h.dtype).at[dest].set(sw)
    tok_buf = jnp.zeros((n_rows,), jnp.int32).at[dest].set(stok)
    blk_e = jnp.minimum(jnp.searchsorted(pend, jnp.arange(n_blocks, dtype=jnp.int32) * MOE_BLOCK, side='right'),
                        N_EXPERTS - 1)

    def expert_block(args):
        xb, e = args
        return swiglu(xb, w_gu[e], w_down[e])

    y_buf = lax.map(expert_block, (x_buf.reshape(n_blocks, MOE_BLOCK, d), blk_e)).reshape(n_rows, d)
    out = jnp.zeros((t, d), h.dtype).at[tok_buf].add(y_buf * w_buf[:, None])
    return out.reshape(b, s, d)

def setup_inputs(seed: int = 0) -> dict:
    key = jax.random.key(seed)
    ks = iter(jax.random.split(key, 48))
    n_even, n_odd = (DEPTH + 1) // 2, DEPTH // 2

    def nrm(shape, scale):
        return scale * jax.random.normal(next(ks), shape, F32)

    def gain(shape):
        return 1.0 + 0.02 * jax.random.normal(next(ks), shape, F32)

    def unif(shape, lo, hi):
        return jax.random.uniform(next(ks), shape, F32, lo, hi)

    dt0 = jnp.exp(unif((n_even, 2, M2_HEADS), float(np.log(1e-3)), float(np.log(1e-1))))
    s5_a_re = -0.5 * jnp.exp(nrm((n_odd, 2, S5_GROUPS, S5_STATE), 0.02))
    s5_a_im = jnp.pi * jnp.arange(S5_STATE, dtype=F32) + nrm((n_odd, 2, S5_GROUPS, S5_STATE), 0.02)
    return {
        'x': nrm((BATCH, SEQ, D_MODEL), 1.0),
        'p': nrm((DEPTH, BATCH, SEQ, PLE_DIM), 1.0),
        'norm_mix': gain((DEPTH, D_MODEL)),
        'norm_ffn': gain((DEPTH, D_MODEL)),
        'norm_ple': gain((DEPTH, D_MODEL)),
        'final_norm': gain((D_MODEL,)),
        'ple_gate': nrm((DEPTH, D_MODEL, D_MODEL), D_MODEL ** -0.5),
        'ple_proj': nrm((DEPTH, PLE_DIM, D_MODEL), PLE_DIM ** -0.5),
        'ev_w_in': nrm((n_even, D_MODEL, EVEN_IN_WIDTH), D_MODEL ** -0.5),
        'ev_w_out': nrm((n_even, EVEN_MIX_WIDTH, D_MODEL), EVEN_MIX_WIDTH ** -0.5),
        'hg_lb_logits': 1.0 + nrm((n_even, HG_WIDTH), 0.1),
        'hg_norm_w': gain((n_even, HG_WIDTH)),
        'm2_conv_w': nrm((n_even, M2_CONV, M2_XBC), M2_CONV ** -0.5),
        'm2_conv_b': nrm((n_even, M2_XBC), 0.01),
        'm2_dt_bias': dt0 + jnp.log(-jnp.expm1(-dt0)),
        'm2_a_log': jnp.log(unif((n_even, 2, M2_HEADS), 1.0, 16.0)),
        'm2_d': gain((n_even, M2_HEADS)),
        'm2_norm_w': gain((n_even, M2_INNER)),
        's5_a_re': s5_a_re,
        's5_a_im': s5_a_im,
        's5_log_step': unif((n_odd, 2, S5_GROUPS), float(np.log(S5_DT_MIN)), float(np.log(S5_DT_MAX))),
        's5_b_re': nrm((n_odd, S5_GROUPS, S5_STATE, S5_GROUP_SIZE), (2 * S5_GROUP_SIZE) ** -0.5),
        's5_b_im': nrm((n_odd, S5_GROUPS, S5_STATE, S5_GROUP_SIZE), (2 * S5_GROUP_SIZE) ** -0.5),
        's5_c_re': nrm((n_odd, 2, S5_GROUPS, S5_GROUP_SIZE, S5_STATE), (2 * S5_STATE) ** -0.5),
        's5_c_im': nrm((n_odd, 2, S5_GROUPS, S5_GROUP_SIZE, S5_STATE), (2 * S5_STATE) ** -0.5),
        's5_d': nrm((n_odd, D_MODEL), 1.0),
        's5_glu_w': nrm((n_odd, D_MODEL, 2 * D_MODEL), D_MODEL ** -0.5),
        'ffn_w_gu': nrm((n_even, D_MODEL, 2 * D_FF), D_MODEL ** -0.5),
        'ffn_w_down': nrm((n_even, D_FF, D_MODEL), D_FF ** -0.5),
        'moe_router': nrm((n_odd, D_MODEL, N_EXPERTS), D_MODEL ** -0.5),
        'moe_w_gu': nrm((n_odd, N_EXPERTS, D_MODEL, 2 * D_FF), D_MODEL ** -0.5),
        'moe_w_down': nrm((n_odd, N_EXPERTS, D_FF, D_MODEL), D_FF ** -0.5),
    }

def reference(x, p, norm_mix, norm_ffn, norm_ple, final_norm, ple_gate, ple_proj, ev_w_in, ev_w_out,
              hg_lb_logits, hg_norm_w, m2_conv_w, m2_conv_b, m2_dt_bias, m2_a_log, m2_d, m2_norm_w,
              s5_a_re, s5_a_im, s5_log_step, s5_b_re, s5_b_im, s5_c_re, s5_c_im, s5_d, s5_glu_w,
              ffn_w_gu, ffn_w_down, moe_router, moe_w_gu, moe_w_down):
    lb_soft = jax.nn.softmax(hg_lb_logits.astype(F32), axis=0)
    hg_lb = jnp.cumsum(lb_soft, axis=0) - lb_soft[0]
    h = x
    for layer in range(DEPTH):
        j = layer // 2
        hn = rmsnorm(h, norm_mix[layer])
        if layer % 2 == 0:
            h = h + even_mixer(hn, ev_w_in[j], ev_w_out[j], hg_lb[j], hg_norm_w[j], m2_conv_w[j], m2_conv_b[j],
                               m2_dt_bias[j], m2_a_log[j], m2_d[j], m2_norm_w[j])
            h = h + swiglu(rmsnorm(h, norm_ffn[layer]), ffn_w_gu[j], ffn_w_down[j])
        else:
            h = h + s5_mixer(hn, s5_a_re[j], s5_a_im[j], s5_log_step[j], s5_b_re[j], s5_b_im[j],
                             s5_c_re[j], s5_c_im[j], s5_d[j], s5_glu_w[j])
            h = h + moe_swiglu(rmsnorm(h, norm_ffn[layer]), moe_router[j], moe_w_gu[j], moe_w_down[j])
        gate = jax.nn.sigmoid(rmsnorm(h, norm_ple[layer]) @ ple_gate[layer])
        h = h + gate * (p[layer] @ ple_proj[layer])
    return rmsnorm(h, final_norm)


_drawn_inputs = setup_inputs


def setup_inputs(seed=0):
    import zlib

    import numpy as np

    out = dict(_drawn_inputs(seed))
    spreads = {}
    factors = {'norm_ple': 200.0,
     'final_norm': 26.911,
     'hg_norm_w': 16.34,
     'm2_conv_b': 3.35,
     'm2_d': 12.776,
     'm2_norm_w': 9.551,
     's5_a_re': 200.0,
     'norm_ffn': 3.751,
     's5_a_im': 53.912,
     's5_log_step': 49.816,
     's5_b_re': 64.0,
     's5_b_im': 64.0,
     's5_c_re': 64.0,
     's5_c_im': 64.0}
    for name, (base, spread) in spreads.items():
        noise = np.random.default_rng([zlib.crc32(name.encode()), seed]).standard_normal(out[name].shape)
        drawn = base * np.exp(spread * noise) if base else spread * noise
        out[name] = __import__('jax').numpy.asarray(drawn.astype(out[name].dtype))
    for name, factor in factors.items():
        out[name] = (out[name] * factor).astype(out[name].dtype)
    return out
```

```python
from contextlib import ExitStack

import concourse.bass as bass
from concourse import mybir

F32 = mybir.dt.float32
I32 = mybir.dt.int32
U32 = mybir.dt.uint32
U8 = mybir.dt.uint8
ALU = mybir.AluOpType
ACT = mybir.ActivationFunctionType
AX_X = mybir.AxisListType.X

P = 128
RING = 6
TILE = 2048


TWO_PI = 6.283185307179586
PI_PARTS = (6.28125, 0.0019350051879882812, 3.0199159795074593e-07)
PI_MAX = 3.1415925
ROUND = 12582912.0


class Arena:

    def __init__(self, tensor, start, end):
        self.tensor, self.at, self.end = tensor, start, end

    def take(self, n):
        a = self.at
        self.at += n
        assert self.at <= self.end, (self.at, self.end)
        return self.tensor[:, a:a + n]


class Chain:

    def __init__(self, eng, sem):
        self.eng, self.sem, self.n = eng, sem, 0

    def link(self, ins):
        self.n += 1
        ins.then_inc(self.sem, 1)

    def settle(self):
        self.eng.wait_ge(self.sem, self.n)


def build_program(nc, I, out, dbg=None):
    x, p_in = I["x"], I["p"]
    _, T, D = x.shape
    TC = T // P
    KB = D // P
    EPS = 1e-6
    LB_FLOOR = 1e-30
    LN_SPLIT = 2.0 ** -60
    HG = I["hg_norm_w"].shape[1]
    HEADS = HG // P
    INNER = I["m2_norm_w"].shape[1]
    MH = I["m2_d"].shape[1]
    MP = INNER // MH
    GROUPS = 2
    HPG = MH // GROUPS
    CONV = I["m2_conv_w"].shape[1]
    XBC = I["m2_conv_w"].shape[2]
    CB = XBC // P
    W_IN = I["ev_w_in"].shape[2]
    FF = I["ffn_w_down"].shape[1]
    FJ = FF // 512
    LEVELS = 9
    assert T == 1 << LEVELS and KB == 8 and TC == 4 and CB == 8 and HEADS == 4

    w_in = I["ev_w_in"][0]
    w_out = I["ev_w_out"][0]

    ctx = ExitStack()
    with ctx:
        def sem(name):
            return ctx.enter_context(nc.semaphore(name))

        words = nc.sbuf_bytes_remaining() // 4 - 64 if callable(nc.sbuf_bytes_remaining) else nc.sbuf_bytes_remaining // 4 - 64
        sbuf = ctx.enter_context(nc.sbuf_tensor("sbuf", [P, words], F32))
        psum = ctx.enter_context(nc.psum_tensor("psum", [P, 8, 512], F32))
        whole = Arena(sbuf, 0, words)
        ring = whole.take(RING * TILE).rearrange("p (s n) -> p s n", s=RING)
        h = whole.take(TC * D).rearrange("p (c n) -> p c n", c=TC)
        hnT = whole.take(KB * T).rearrange("p (k t) -> p k t", k=KB)
        mixT = whole.take(KB * T).rearrange("p (k t) -> p k t", k=KB)
        ident, ones, LE, GE, GT, LT = [whole.take(P) for _ in range(6)]
        masks = whole.take(14 * P // 4).bitcast(U8).rearrange("p (m t) -> p m t", m=14)
        parT = whole.take(68)
        parR = whole.take(P)
        nw = whole.take(2 * D).rearrange("p (b n) -> p b n", b=2)
        stat = whole.take(7 * 4 * 3).rearrange("p (k a c) -> p k a c", k=7, a=3)
        eps = whole.take(1)
        hgc = whole.take(32).rearrange("p (a k) -> p a k", k=4)
        tokp = whole.take(56)
        dtb, alog, dskip, aneg = tokp[:, 0:16], tokp[:, 16:32], tokp[:, 32:40], tokp[:, 40:56]
        base = whole.at
        pe_words = words

        c_q, c_ff, c_fb, c_v, c_g, c_z = [HG * n for n in range(6)]
        c_xs = c_z + INNER
        c_bc = c_xs + INNER
        c_dt = c_bc + XBC - INNER

        stream = []
        release, n_used = [], [0]

        def add_tiles(w, col, width):
            for g in range(2):
                stream.append((w[g * 512:(g + 1) * 512, col:col + width].rearrange("(k p) n -> p k n", p=P), width))

        groups = []

        def add_group(name, w, col, width, layout, drain):
            if w is None:
                groups.append((name, layout, width, drain, None))
                return
            add_tiles(w, col, width)
            groups.append((name, layout, width, drain, len(stream) - 2))
            release.append(("used", n_used[0] + 1))
            release.append(("group", 4 * len(groups)))
            n_used[0] += 1

        add_group("q", w_in, c_q, 512, "T", "A")
        add_group("ff", w_in, c_ff, 512, "T", "A")
        add_group("fb", w_in, c_fb, 512, "T", "A")
        add_group("v", w_in, c_v, 512, "tok", "D")
        add_group("g", w_in, c_g, 512, "T", "A")
        add_group("z", w_in, c_z, 512, "tok", "A")
        add_group("xs", w_in, c_xs, 512, "T", "D")
        add_group("bc", w_in, c_bc, 512, "T", "D")
        add_group("dt", w_in, c_dt, 16, "tok", "D")
        add_group("o0", w_out, 0, 512, "tok", "D")
        add_group("o1", w_out, 512, 512, "tok", "D")
        gu, down = I["ffn_w_gu"][0], I["ffn_w_down"][0]
        for j in range(FJ):
            add_group(f"fg{j}", gu, 512 * j, 512, "T", "A")
            add_group(f"fu{j}", gu, FF + 512 * j, 512, "T", "D")
        down_tile0 = len(stream)
        for j in range(FJ):
            for half in range(2):
                stream.append((down[512 * j:512 * (j + 1), 512 * half:512 * (half + 1)].rearrange("(k p) n -> p k n", p=P), 512))
                n_used[0] += j < FJ - 1
                release.append(("down", 4 * half + 4) if j == FJ - 1 else ("used", n_used[0]))
        ple_tile = len(stream)
        stream.append((I["ple_proj"][0].rearrange("(k p) n -> p k n", p=P), -1))
        release.append(("proj", 8))
        for j in range(2):
            add_group(f"pg0{j}", I["ple_gate"][0], 512 * j, 512, "tok", "A")
        glu = I["s5_glu_w"][0]
        for j in range(2):
            add_group(f"gg{j}", glu, D + 512 * j, 512, "tok", "A")
            add_group(f"go{j}", glu, 512 * j, 512, "tok", "D")
        for j in range(2):
            add_group(f"pg1{j}", None, 512 * j, 512, "tok", "A")
        gidx = {g[0]: n for n, g in enumerate(groups)}
        cumA, cumD = [], []
        for g in groups:
            cumA.append((cumA[-1] if cumA else 0) + (4 if g[3] == "A" else 0))
            cumD.append((cumD[-1] if cumD else 0) + (4 if g[3] == "D" else 0))

        s_ring = [sem(f"ring_full{i}") for i in range(RING)]
        s_used = sem("ring_tile_used")
        s_x = sem("x_loaded")
        s_par = sem("params_loaded")
        s_tokp = sem("token_params_loaded")
        s_nw = [sem(f"norm_weight_loaded{i}") for i in range(2)]
        s_const = sem("constants_built")
        s_parT = sem("params_transposed")
        s_parTd = sem("params_in_sbuf")
        s_lb = sem("hg_bounds_ready")
        s_lbc = sem("hg_bounds_exp")
        s_sq = sem("square_sums")
        s_rms = sem("rms_ready")
        s_hn = sem("hn_ready")
        s_tp = sem("hn_transposed")
        s_hA = sem("hnT_by_act")
        s_hD = sem("hnT_by_dve")
        s_grp = sem("dense_bank_done")
        s_drA = sem("dense_bank_drained_act")
        s_drD = sem("dense_bank_drained_dve")
        s_vc = sem("dve_chain")
        s_ac = sem("act_chain")
        s_pc = sem("pool_chain")
        s_lf = sem("log_forget_ready")
        s_k = sem("key_ready")
        s_lnin = sem("ln_inputs_ready")
        s_lnout = sem("ln_outputs_ready")
        s_rz = sem("suffix_zeroed")
        s_exp = sem("decay_exp_ready")
        s_X = sem("scaled_qk_ready")
        s_upd = sem("prefix_updated")
        s_gram = sem("gram_done")
        s_gdr = sem("gram_drained")
        s_ks = sem("key_sum_ready")
        s_dg = sem("diag_gram_done")
        s_sd = sem("diag_scores_ready")
        s_o = sem("hg_out_done")
        s_osq = sem("hg_out_squared")
        s_oss = sem("hg_square_sum_done")
        s_orms = sem("hg_rms_ready")
        s_mix = sem("hg_mix_ready")
        s_diag = sem("conv_diag_ready")
        s_pad = sem("conv_pad_zeroed")
        s_conv = sem("conv_done")
        s_cact = sem("conv_activated")
        s_sp = sem("softplus_parts")
        s_dt = sem("dt_ready")
        s_xt = sem("xs_transposed")
        s_xtd = sem("xs_in_sbuf")
        s_cum = sem("cumsums_done")
        s_ex = sem("cumsum_exp_ready")
        s_te = sem("to_end_ready")
        s_xe = sem("x_to_end_ready")
        s_st = sem("chunk_state_done")
        s_H = sem("state_ready")
        s_cb = sem("cb_done")
        s_cbm = sem("cb_masked")
        s_dtau = sem("dta_masked")
        s_seg = sem("segment_sums_done")
        s_E = sem("segment_exp_ready")
        s_w = sem("ssd_weights_ready")
        s_xdt = sem("x_dt_ready")
        s_y = sem("ssd_y_done")
        s_yd = sem("ssd_y_drained")
        s_yz = sem("ssd_gated")
        s_ysq = sem("ssd_square_sums")
        s_yrms = sem("ssd_rms")
        s_yn = sem("ssd_normed")
        s_yt = sem("ssd_transposed")
        s_ym = sem("ssd_mix_ready")
        s_ffd = sem("ffn_down_done")
        s_fd = sem("ffn_down_drained")
        s_ph = sem("ple_added")
        s_p = sem("ple_input_loaded")
        s_pT = sem("ple_input_transposed")
        s_pTd = sem("ple_input_in_sbuf")
        s_pp = sem("ple_proj_done")
        s_ppd = sem("ple_proj_drained")
        s_out = sem("out_stored")

        s_rtr = sem("router_loaded")
        s_pw = sem("ple_proj_weights_loaded")
        s_gw = sem("ple_gate_weights_loaded")
        s_lg = sem("router_logits_done")
        s_top = sem("router_logit_gap_ready")
        s_gexp = sem("router_gap_exp")
        s_hot = sem("expert_one_hot_ready")
        s_rank = sem("expert_ranks_done")
        s_slot = sem("slot_one_hot_ready")
        s_tok = sem("slot_tokens_done")
        s_plan = sem("block_plan_ready")
        s_hnm = sem("moe_rows_in_dram")
        s_ix = sem("slot_tokens_copied")
        s_xg = sem("block_rows_loaded")
        s_xtp = sem("block_rows_transposed")
        s_xtA = sem("block_xT_by_act")
        s_xtD = sem("block_xT_by_dve")
        s_mt = sem("moe_tile_used")
        s_msl = sem("expert_silu_ready")
        s_mh = sem("expert_hidden_ready")
        s_mht = sem("expert_hidden_transposed")
        s_mhc = sem("expert_hiddenT_ready")
        s_myd = sem("block_y_in_sbuf")
        s_mys = sem("block_y_in_dram")
        s_yg = [sem(f"token_y_gathered{c}") for c in range(TC)]
        s_mc = sem("moe_combined")

        s_s5in = sem("s5_params_loaded")
        s_sin = sem("s5_sin_ready")
        s_ang = sem("s5_angle_ready")
        s_rowt = sem("s5_row_tables_ready")
        s_rt = sem("s5_rows_transposed")
        s_tabD = sem("s5_tables_by_dve")
        s_hnd = sem("hn_in_dram")
        s_un = sem("s5_inputs_by_chunk")
        s_up = sem("s5_inputs_by_group")
        s_ut = sem("s5_inputs_transposed")
        s_u = sem("s5_inputs_ready")
        s_t2 = sem("s5_pool_product")
        s_bp = sem("s5_b_powers")
        s_bt = sem("s5_b_transposed")
        s_bigA = sem("s5_b_by_act")
        s_bigD = sem("s5_b_by_dve")
        s_v = sem("s5_chunk_inputs_done")
        s_vd = sem("s5_chunk_inputs_ready")
        s_zf = sem("s5_forward_states")
        s_zb = sem("s5_backward_states")
        s_cp = sem("s5_c_powers")
        s_kk = sem("s5_kernels_done")
        s_kj = sem("s5_kernels_in_sbuf")
        s_kb = sem("s5_toeplitz_built")
        s_yy = sem("s5_y_done")
        s_yb = sem("s5_y_in_sbuf")
        s_ydr = sem("s5_y_in_dram")
        s_yin = sem("s5_y_loaded")
        s_dw = sem("s5_skip_loaded")
        s_gin = sem("gelu_input_ready")
        s_gl = sem("gelu_ready")
        s_glt = sem("gelu_transposed")
        s_glA = sem("gelu_by_act")
        s_glD = sem("gelu_by_dve")
        s_z0 = sem("s5_zero_states")
        s_cst = sem("s5_c_transposed")

        hga = Arena(sbuf, base, pe_words)
        v4 = "p (a t) -> p a t"
        qT = hga.take(4 * T).rearrange(v4, a=4)
        kT = [hga.take(4 * T).rearrange(v4, a=4) for _ in range(2)]
        vtok = hga.take(4 * 512).rearrange(v4, a=4)
        gT = hga.take(4 * T).rearrange(v4, a=4)
        lf = [hga.take(4 * T).rearrange(v4, a=4) for _ in range(2)]
        Rs = [[hga.take(T) for _ in range(2)] for _ in range(2)]
        Xb = [hga.take(T) for _ in range(4)]
        S_flat = hga.take(5 * T)
        S_main = S_flat[:, 0:4 * T].rearrange("p (c t) -> p c t", c=4)
        S_diag = S_flat.rearrange("p (c x) -> p c x", x=T + P)[:, :, 0:P]
        ksum = hga.take(T)
        osq = hga.take(T)
        orms = hga.take(T)
        hn_at = pe_words - 4 * D
        hn = sbuf[:, hn_at:hn_at + 4 * D].rearrange("p (c n) -> p c n", c=4)
        lnb = hn

        mtmp = hnT.rearrange("p k t -> p (k t)")[:, 0:14 * P].rearrange("p (m t) -> p m t", m=14)

        ssa = Arena(sbuf, base, pe_words)
        zs = ssa.take(4 * 512).rearrange(v4, a=4)
        dtr = ssa.take(64).rearrange("p (d c k) -> p d c k", d=2, c=4)
        dts = ssa.take(64).rearrange("p (d c k) -> p d c k", d=2, c=4)
        dta = ssa.take(64).rearrange("p (d c k) -> p d c k", d=2, c=4)
        dtt = ssa.take(64).rearrange("p (d c k) -> p d c k", d=2, c=4)
        toend = ssa.take(64).rearrange("p (d c k) -> p d c k", d=2, c=4)
        ex = ssa.take(192)
        xc = ssa.take(8 * T).rearrange(v4, a=8)
        xst = ssa.take(4 * 512).rearrange(v4, a=4)
        btok = ssa.take(4 * 256).rearrange(v4, a=4)
        Hst = [ssa.take(3 * 512).rearrange(v4, a=3) for _ in range(2)]
        yst_flat = ssa.take(4 * 512)
        yst = yst_flat.rearrange(v4, a=4)
        ytmp = ssa.take(512)
        ssy = ssa.take(24).rearrange("p (a k) -> p a k", a=3)
        cbm = ssa.take(512).rearrange("p (d g t) -> p d g t", d=2, g=2)
        xdt = ssa.take(1024).rearrange("p (d n) -> p d n", d=2)
        xe = ssa.take(1024).rearrange("p (d n) -> p d n", d=2)
        shared = ssa.at
        raw = ssa.take(8 * (T + 4)).rearrange(v4, a=8)
        diag = yst_flat[:, 0:2 * CONV * P].rearrange("p (b k n) -> p b k n", b=2, k=CONV)
        ssa.at = shared
        Ew = ssa.take(2048).rearrange("p (d n t) -> p d n t", d=2, t=P)
        dtaU = ssa.take(2048).rearrange("p (d n t) -> p d n t", d=2, t=P)

        ffa = Arena(sbuf, base, hn_at)
        hT = ffa.take(FJ * 4 * T).rearrange("p (f t) -> p f t", t=T)
        silT = mixT[:, 0:4, :]
        pla = Arena(sbuf, base, hn_at)
        ptok = pla.take(4 * 256).rearrange(v4, a=4)
        pT = pla.take(2 * T).rearrange(v4, a=2)
        pp = pla.take(4 * D).rearrange(v4, a=4)
        pgate = mixT

        NE = I["moe_router"].shape[2]
        MAXB = TC * 2 + NE - 1
        EJ = I["moe_w_down"].shape[2] // 512
        PER = 6 * EJ
        assert PER % RING == 0 and NE == 8
        N0 = len(stream)
        moa = Arena(sbuf, base, hn_at)
        pp1 = moa.take(4 * D).rearrange(v4, a=4)
        gw = moa.take(8 * D).rearrange("p (j k n) -> p j k n", j=2, k=8)
        xblk = moa.take(D)
        xbT = moa.take(D).rearrange("p (k t) -> p k t", k=8)
        esil = moa.take(2 * 512).rearrange(v4, a=2)
        ehid = moa.take(2 * 512).rearrange(v4, a=2)
        ehT = moa.take(2 * 512).rearrange("p (b k t) -> p b k t", b=2, k=4)
        yblk = moa.take(D)
        router = moa.take(8 * NE).rearrange("p (k e) -> p k e", k=8)
        lg = moa.take(TC * NE).rearrange("p (c e) -> p c e", c=TC)
        top = moa.take(TC * 8).rearrange("p (c e) -> p c e", c=TC)
        topi = moa.take(TC * 8).bitcast(U32).rearrange("p (c e) -> p c e", c=TC)
        topf = moa.take(TC * 2).rearrange("p (c k) -> p c k", c=TC)
        gate = moa.take(TC * 3).rearrange("p (a c) -> p a c", a=3)
        hot = moa.take(TC * 3 * NE).rearrange("p (k c e) -> p k c e", k=3, c=TC)
        rowi = moa.take(P)
        parti = moa.take(TC)
        rk = moa.take(TC * NE).rearrange("p (c e) -> p c e", c=TC)
        rq = moa.take(TC * NE).rearrange("p (c e) -> p c e", c=TC)
        rtmp = moa.take(2 * TC * NE).rearrange("p (k c e) -> p k c e", k=2, c=TC)
        cnt = moa.take(NE)
        nblk = moa.take(NE)
        ends = moa.take(2 * NE).rearrange("p (a e) -> p a e", a=2)
        bsel = moa.take(2 * TC).rearrange("p (k c) -> p k c", k=2)
        rsel = moa.take(2 * TC).rearrange("p (k c) -> p k c", k=2)
        destf = moa.take(2 * TC).rearrange("p (k c) -> p k c", k=2)
        desti = moa.take(2 * TC).bitcast(I32).rearrange("p (k c) -> p k c", k=2)
        ecmp = moa.take((MAXB + 1) * NE).rearrange("p (b e) -> p b e", e=NE)
        ef = moa.take(MAXB + 1)
        plan = moa.take(MAXB + 2).bitcast(I32)
        slot_tok = moa.take(MAXB + 1).bitcast(I32)
        slot_now = moa.take(1).bitcast(I32)
        slot_junk = moa.take(4)
        moe_hotR = mixT.rearrange("p k t -> p (k t)")[:, 0:8 * P].rearrange("p (k c t) -> p k c t", k=2, c=TC)
        moe_hotB = mixT.rearrange("p k t -> p (k t)")[:, 8 * P:8 * P + 8 * 16].rearrange("p (k c b) -> p k c b", k=2, c=TC)
        ptok1 = mixT.rearrange("p k t -> p (k t)")[:, 0:1024].rearrange(v4, a=4)
        pT1 = mixT.rearrange("p k t -> p (k t)")[:, 1024:2048].rearrange(v4, a=2)
        pw1 = mixT.rearrange("p k t -> p (k t)")[:, 2048:4096].rearrange("p (k n) -> p k n", k=2)
        yg = [r_.rearrange("p k t -> p (k t)").rearrange("p (c n) -> p c n", c=TC) for r_ in (hnT, mixT)]
        y_rows = nc.dram_tensor("expert_rows", (MAXB * P, D), F32, kind="Internal").ap()
        w_egu, w_edn = I["moe_w_gu"][0], I["moe_w_down"][0]
        moe_dram = nc.dram_tensor("moe_rows_by_token", (T, D), F32, kind="Internal").ap()

        def gu_at(j):
            return 4 * j + 2 * max(j - 1, 0)

        def down_at(j):
            return min(6 * j + 8, PER - 2)

        def tiles_done(i, n):
            return i * PER + (RING + n)

        def moe_sources(e):
            def src(w, r0, col):
                return w[bass.ds(e, 1), r0:r0 + 512, col:col + 512].rearrange("a (k p) n -> p (a k) n", p=P)
            down_ = lambda j: [src(w_edn, 512 * j, 512 * hf) for hf in range(2)]
            tiles = []
            for j in range(EJ):
                tiles += [src(w_egu, 512 * kk, 512 * j) for kk in range(2)]
                tiles += [src(w_egu, 512 * kk, EJ * 512 + 512 * j) for kk in range(2)]
                if j:
                    tiles += down_(j - 1)
            return tiles + down_(EJ - 1)

        block = ctx.enter_context(nc.Block())
        norm_w = [I["norm_mix"][0], I["norm_ffn"][0], I["norm_ple"][0], I["norm_mix"][1], I["norm_ffn"][1],
                  I["norm_ple"][1], I["final_norm"]]

        def row(v):
            return v.rearrange("(a n) -> a n", a=1)

        def half(ap, n, side):
            return ap.rearrange("p (b two n) -> p b two n", two=2, n=n)[:, :, side, :]

        G5, NS, GC = I["s5_b_re"].shape[1:]
        L5 = 8
        NC5 = T // L5
        HALF = G5 // 2
        BG = 4
        BATCHES = G5 // BG
        M5 = L5 + 1
        s5a = Arena(sbuf, base, pe_words)
        WA, WB = [s5a.take(2 * G5 * L5).rearrange("p (d g m) -> p d g m", d=2, g=G5) for _ in range(2)]
        PA, PB = [s5a.take(2 * G5 * M5).rearrange("p (d g m) -> p d g m", d=2, g=G5) for _ in range(2)]
        LR = s5a.take(2 * G5).rearrange("p (d g) -> p d g", d=2)
        LI = s5a.take(4 * G5).rearrange("p (d e g) -> p d e g", d=2, e=2)
        Bst, Bsw = [s5a.take(G5 * GC).rearrange("p (g c) -> p g c", g=G5) for _ in range(2)]
        s5_work = s5a.at
        ZS = 2 * HALF
        z_at = [s5a.at, s5a.at + (NC5 + 1) * ZS]
        Z = [s5a.take((NC5 + 1) * ZS) for _ in range(2)]
        BBk = s5a.take(HALF * 2 * GC).rearrange("p (d g c) -> p d g c", d=2, g=HALF)
        W1, W2 = [s5a.take(2 * BG * M5 * GC) for _ in range(2)]
        BP = W1[:, 0:2 * BG * L5 * GC].rearrange("p (d g m c) -> p d g (m c)", d=2, g=BG, m=L5)
        BQ = W2[:, 0:2 * BG * L5 * GC].rearrange("p (d g m c) -> p d g (m c)", d=2, g=BG, m=L5)
        CP = W1.rearrange("p (d g m c) -> p d g (m c)", d=2, g=BG, m=M5)
        CQ = W2.rearrange("p (d g m c) -> p d g (m c)", d=2, g=BG, m=M5)
        big_at = s5a.at
        BigB = s5a.take(2 * BG * 192).rearrange("p (d g n) -> p d g n", d=2, g=BG)
        s5a.at = big_at
        KJ = s5a.take(BG * 15 * GC).rearrange("p (g j c) -> p g j c", g=BG, j=15)
        Kbig = s5a.take(BG * P).rearrange("p (g n) -> p g n", g=BG)
        s5a.at = max(s5a.at, big_at + 2 * BG * 192)
        Yb = s5a.take(L5 * BG * GC).rearrange("p (t n) -> p t n", t=L5)
        UN = sbuf[0:NC5, s5_work:s5_work + L5 * D].rearrange("p (t n) -> p t n", t=L5)
        UP = (W1, W2)
        U = hnT.rearrange("p k t -> p (k t)").rearrange("p (g n) -> p g n", g=G5)
        Cst, Csw = [mixT.rearrange("p k t -> p (k t)")[:, 2048 * n:2048 * (n + 1)].rearrange("p (d g c) -> p d g c", d=2, g=G5)
                    for n in range(2)]
        rwa = Arena(sbuf, s5_work, pe_words)
        srow = lambda n: rwa.take(n)
        r_are, r_aim, r_x, r_th, r_k, r_r, r_s, r_c, r_den, r_t0, r_t1, r_nr, r_cr, r_ci = [srow(NS) for _ in range(14)]
        r_ls = srow(1)
        PR, PI = [rwa.take(M5 * NS).rearrange("p (m n) -> p m n", m=M5) for _ in range(2)]
        WR, WI = [rwa.take(L5 * NS).rearrange("p (m n) -> p m n", m=L5) for _ in range(2)]
        rowt = rwa.take(6 * 2 * NS * M5).rearrange("p (k m q n) -> p k m q n", k=6, m=M5, q=2)
        crow = mixT_free = None
        C3 = s5a.tensor[:, s5_work + 14 * NS + 1 + 4 * M5 * NS + 12 * NS * M5:][:, 0:16 * 3 * NS].rearrange(
            "p (b q n) -> p b q n", b=16, q=3)
        ytok = sbuf[:, base:base + 4 * D].rearrange("p (c n) -> p c n", c=4)
        skip_w = sbuf[:, base + 4 * D:base + 5 * D]
        gtmp = sbuf[:, base + 5 * D:base + 5 * D + 2048].rearrange(v4, a=4)
        hn_dram = nc.dram_tensor("hn_by_token", (T, D), F32, kind="Internal").ap()
        y_dram = nc.dram_tensor("s5_y_by_token", (T, D), F32, kind="Internal").ap()


        lnb4 = lnb.rearrange("p c n -> p (c n)")[:, 0:4 * T].rearrange(v4, a=4)
        h_ready = {
            0: lambda e, c: e.wait_ge(s_x, 16),
            1: lambda e, c: e.wait_ge(s_drD, cumD[gidx["o1"]] - 3 + c),
            2: lambda e, c: e.wait_ge(s_fd, 2 * (c + 1)),
            3: lambda e, c: e.wait_ge(s_ph, c + 1),
            4: lambda e, c: e.wait_ge(s_drD, cumD[gidx["go1"]] - 3 + c),
            5: lambda e, c: e.wait_ge(s_mc, c + 1),
            6: lambda e, c: e.wait_ge(s_ph, 4 + c + 1),
        }

        def ssd_squares(act, c):
            act.wait_ge(s_yz, c + 1)
            for g in range(GROUPS):
                m = act.activation(zs[:, c, g * 256:(g + 1) * 256], yst[:, c, g * 256:(g + 1) * 256], ACT.Square,
                                   accum_out=ssy[:, 0, 2 * c + g:2 * c + g + 1])
            m.then_inc(s_ysq, 1)

        SSD_STATES = [(0, 0), (1, 3), (0, 1), (1, 2), (0, 2), (1, 1)]
        LE_, GE_, GT_, LT_ = LE, GE, GT, LT
        def scan(eng, chain, d, half_, done):
            scratch = (W1, W2)[d]
            a = scratch[:, 0:ZS]
            b = scratch[:, ZS:2 * ZS]
            g0 = HALF * half_
            LRv = LR[:, d, g0:g0 + HALF].unsqueeze(1).broadcast_to([P, 2, HALF])
            LIv = LI[:, d, :, g0:g0 + HALF]
            kinds = lambda ap: ap.rearrange("p (e g) -> p e g", e=2)
            for n in range(NC5):
                last, new = (n, n + 1) if d == 0 else (NC5 - n, NC5 - 1 - n)
                at = last * ZS
                old = Z[d][:, at:at + ZS]
                swapped = bass.AP(sbuf, z_at[d] + at + HALF, [[words, P], [-HALF, 2], [1, HALF]])
                chain.link(eng.tensor_tensor(kinds(a), kinds(old), LRv, ALU.mult))
                chain.link(eng.tensor_tensor(kinds(b), swapped, LIv, ALU.mult))
                v = Z[d][:, new * ZS:(new + 1) * ZS]
                eng.wait_ge(chain.sem, chain.n - 1)
                chain.link(eng.tensor_tensor(a, a, v, ALU.add))
                chain.settle()
                m = eng.tensor_tensor(v, a, b, ALU.add)
                if n < NC5 - 1:
                    chain.link(m)
                    chain.settle()
                else:
                    m.then_inc(done, 1)
            eng.wait_ge(done, half_ + 1)

        TURN = {0: 0, 1: 1, 2: 2, 4: 3, 5: 4}
        ROW_TABLES = [(k, m) for k in range(4) for m in range(M5 if k < 2 else L5)] + [(4, 0), (5, 0)]
        s5_tile0 = groups[gidx["gg0"]][4]

        def s5_moves(sp):
            for c in range(TC):
                sp.wait_ge(s_hn, 12 + c + 1)
                sp.dma_start(hn_dram[c * P:(c + 1) * P, :], hn[:, c, :]).then_inc(s_hnd, 16)
            sp.wait_ge(s_hnd, 64)
            sp.wait_ge(s_tabD, 1)
            sp.dma_start(UN, hn_dram.rearrange("(n t) d -> n t d", t=L5)).then_inc(s_un, 16)
            for b in range(BATCHES):
                sp.wait_ge(s_kj, b + 1)
                if b:
                    sp.wait_ge(s_yy, b)
                for t in range(L5):
                    sp.dma_start(Kbig[GC * t:GC * (t + 1), :, :],
                                 KJ[0:GC, :, :, :].rearrange("p g j c -> p g (j c)")[:, :, GC * (L5 - 1 - t):GC * (2 * L5 - 1 - t)]
                                 ).then_inc(s_kb, 16)
                sp.wait_ge(s_yb, b + 1)
                sp.dma_start(y_dram.rearrange("(n t) d -> n t d", t=L5)[:, :, BG * GC * b:BG * GC * (b + 1)],
                             Yb[0:NC5, :, :]).then_inc(s_ydr, 16)
            sp.wait_ge(s_ydr, 16 * BATCHES)
            sp.dma_start(ytok, y_dram.rearrange("(c p) d -> p c d", p=P)).then_inc(s_yin, 16)

        releases = dict(used=s_used, group=s_grp, down=s_ffd, proj=s_pp)

        @block.sync
        def _(sp):
            sp.dma_start(h, x[0].rearrange("(c p) n -> p c n", p=P)).then_inc(s_x, 16)
            for src, r0, n in ((I["m2_conv_w"][0], 0, CONV * CB), (I["m2_conv_b"], 40, CB), (I["hg_norm_w"], 48, 4),
                               (I["hg_lb_logits"], 52, 4), (I["m2_norm_w"], 56, 4), (I["s5_d"], 60, 8)):
                sp.dma_start(parR[r0:r0 + n, :], src.rearrange("a (b n) -> (a b) n", n=P)).then_inc(s_par, 16)
            for n, (src, width) in enumerate(stream):
                if n == s5_tile0 + RING:
                    s5_moves(sp)
                if n >= RING:
                    what, count = release[n - RING]
                    sp.wait_ge(releases[what], count)
                dst = ring[:, n % RING, :]
                if width == -1:
                    dst = dst.rearrange("p (k n) -> p k n", k=2)
                else:
                    dst = dst.rearrange("p (k n) -> p k n", k=4)[:, :, 0:width]
                sp.dma_start(dst, src).then_inc(s_ring[n % RING], 16)
            for c in range(TC):
                sp.wait_ge(s_hn, 16 + c + 1)
                sp.dma_start(moe_dram[c * P:(c + 1) * P, :], hn[:, c, :]).then_inc(s_hnm, 16)
            for n in range(N0 - RING, N0):
                what, count = release[n]
                sp.wait_ge(releases[what], count)
            sp.wait_ge(s_plan, 1)
            blocks_sp = sp.value_load(plan[0:1, MAXB:MAXB + 1], min_val=2 * TC, max_val=MAXB)
            with sp.Fori(0, MAXB) as i:
                with sp.If(i < blocks_sp):
                    e = sp.value_load(plan[0:1, bass.ds(i, 1)], min_val=0, max_val=NE - 1)
                    for jj, src in enumerate(moe_sources(e)):
                        sp.wait_ge(s_mt, PER * i + jj + 1)
                        slot = (N0 + jj) % RING
                        sp.dma_start(ring[:, slot, :].rearrange("p (k n) -> p k n", k=4), src).then_inc(s_ring[slot], 16)
            for c in range(TC):
                sp.wait_ge(s_hn, 24 + c + 1)
                sp.dma_start(out[0, c * P:(c + 1) * P, :], hn[:, c, :]).then_inc(s_out, 16)
            sp.wait_ge(s_out, 16 * TC)

        @block.gpsimd
        def _(pool):
            chain = Chain(pool, s_pc)
            for n, v in enumerate((I["m2_dt_bias"][0].rearrange("a b -> (a b)"), I["m2_a_log"][0].rearrange("a b -> (a b)"),
                                   I["m2_d"][0])):
                dst = (dtb, alog, dskip)[n]
                pool.dma_start(dst, row(v).broadcast_to([P, v.shape[0]])).then_inc(s_tokp, 16)
            for k in range(2):
                pool.dma_start(nw[:, k, :], row(norm_w[k]).broadcast_to([P, D])).then_inc(s_nw[k], 16)
            chain.link(pool.memset(ones, 1.0))
            chain.link(pool.memset(eps, EPS))
            chain.settle()
            for m, op, sign in ((ident, ALU.is_equal, 1), (LE, ALU.is_ge, -1), (GE, ALU.is_ge, 1), (GT, ALU.is_gt, 1),
                                (LT, ALU.is_gt, -1)):
                pool.affine_select(out=m, in_=ones, compare_op=op, fill=0.0, base=0, pattern=[[-sign, P]],
                                   channel_multiplier=sign).then_inc(s_const, 1)

            chain.link(pool.memset(mtmp, 0.0))
            chain.settle()
            for l in range(7):
                n = 1 << l
                for d in range(2):
                    m = mtmp[:, 2 * l + d, :]
                    view = half(m, n, 1 - d)
                    blocks, lo = [[-2 * n, P // (2 * n)], [0, n]], n * d
                    chain.link(pool.memset(view, 1.0))
                    chain.settle()
                    chain.link(pool.affine_select(out=view, in_=view, compare_op=ALU.is_ge, fill=0.0, base=-lo,
                                                  pattern=blocks, channel_multiplier=1))
                    chain.settle()
                    chain.link(pool.affine_select(out=view, in_=view, compare_op=ALU.is_gt, fill=0.0, base=lo + n,
                                                  pattern=[[2 * n, P // (2 * n)], [0, n]], channel_multiplier=-1))
            chain.settle()
            pool.tensor_copy(masks, mtmp).then_inc(s_const, 1)

            def zero_suffix(hd):
                if hd >= 2:
                    pool.wait_ge(s_exp, 18 * (hd - 1))
                for d in range(2):
                    m = pool.memset(Rs[hd % 2][d], 0.0)
                m.then_inc(s_rz, 1)

            pool.wait_ge(s_hn, 4)
            for r0 in range(2 * TC * P, MAXB * P, T):
                n = min(T, MAXB * P - r0)
                pool.dma_start(y_rows[r0:r0 + n, :], x[0, 0:n, :]).then_inc(s_mys, 16)
            pool.wait_ge(s_tp, 8)
            pool.wait_ge(s_k, 8)
            pool.wait_ge(s_lf, 2)
            for hd in range(HEADS):
                zero_suffix(hd)
                if hd >= 1:
                    pool.wait_ge(s_dg, hd)
                pool.tensor_tensor(ksum, kT[0][:, hd, :], kT[1][:, hd, :], ALU.add).then_inc(s_ks, 1)
                pool.wait_ge(s_lf, 2)
                pool.wait_ge(s_rz, hd + 1)
                for l in range(LEVELS - 1):
                    for d in range(2):
                        n = hd * 18 + 2 * l + d
                        pool.wait_ge(s_exp, n + 1)
                        if l:
                            pool.wait_ge(s_upd, hd * 16 + 2 * (l - 1) + d + 1)
                        Pd, Rd = lf[d][:, hd, :], Rs[hd % 2][d]
                        hs = 1 << l
                        near, far = (0, 1) if d == 0 else (1, 0)
                        edge = hs - 1 if d == 0 else 0
                        shape = [P, T // (2 * hs), hs]
                        chain.link(pool.tensor_tensor(half(Rd, hs, near), half(Rd, hs, near),
                                                      half(Pd, hs, far)[:, :, edge:edge + 1].broadcast_to(shape), ALU.add))
                        chain.settle()
                        pool.tensor_tensor(half(Pd, hs, far), half(Pd, hs, far),
                                           half(Pd, hs, near)[:, :, edge:edge + 1].broadcast_to(shape),
                                           ALU.add).then_inc(s_upd, 1)

            pool.wait_ge(s_mix, HEADS)
            for c in (0, T + 2):
                m = pool.memset(raw[:, :, c:c + 2], 0.0)
            m.then_inc(s_pad, 1)
            pool.wait_ge(s_parTd, 1)
            for cb in range(CB):
                if cb >= 2:
                    pool.wait_ge(s_conv, cb - 1)
                for k in range(CONV):
                    m = pool.tensor_scalar(diag[:, cb % 2, k, :], ident, parT[:, k * CB + cb:k * CB + cb + 1], None, ALU.mult)
                m.then_inc(s_diag, 1)
            pool.wait_ge(s_dt, 1)
            pool.wait_ge(s_ex, 1)
            R = ex[:, 64:128].rearrange("p (d c k) -> p d c k", d=2, c=4)
            pool.tensor_tensor(toend.rearrange("p d c k -> p (d c k)"), ex[:, 64:128], dts.rearrange("p d c k -> p (d c k)"),
                               ALU.mult).then_inc(s_te, 1)
            pool.wait_ge(s_te, 1)
            for m, (d, c) in enumerate(SSD_STATES):
                pool.wait_ge(s_xtd, c + 1)
                if m >= 2:
                    pool.wait_ge(s_st, m - 1)
                pool.tensor_tensor(xe[:, m % 2, :].rearrange("p (k n) -> p k n", k=MH),
                                   xst[:, c, :].rearrange("p (k n) -> p k n", k=MH),
                                   toend[:, d, c, :].unsqueeze(2).broadcast_to([P, MH, MP]), ALU.mult).then_inc(s_xe, 1)
            for c in range(TC):
                if c >= 1:
                    pool.wait_ge(s_seg, c)
                for d in range(2):
                    m = pool.tensor_tensor(dtaU[:, d, :, :], (LE_, GE_)[d].unsqueeze(1).broadcast_to([P, MH, P]),
                                           dta[:, d, c, :].unsqueeze(2).broadcast_to([P, MH, P]), ALU.mult)
                m.then_inc(s_dtau, 1)
                if c >= 1:
                    pool.wait_ge(s_y, c)
                for d in range(2):
                    m = pool.tensor_tensor(xdt[:, d, :].rearrange("p (k n) -> p k n", k=MH),
                                           xst[:, c, :].rearrange("p (k n) -> p k n", k=MH),
                                           dts[:, d, c, :].unsqueeze(2).broadcast_to([P, MH, MP]), ALU.mult)
                m.then_inc(s_xdt, 1)
            for k in range(2, 4):
                pool.wait_ge(s_hn, 4 * (k - 1))
                pool.dma_start(nw[:, k % 2, :], row(norm_w[k]).broadcast_to([P, D])).then_inc(s_nw[k % 2], 16)
                if k == 2:
                    pool.wait_ge(s_ffd, 8)
                    pool.dma_start(ptok, p_in[0, 0].rearrange("(c p) n -> p c n", p=P)).then_inc(s_p, 16)
            pool.wait_ge(s_ph, 4)
            pool.dma_start(nw[:, 0, :], row(norm_w[4]).broadcast_to([P, D])).then_inc(s_nw[0], 16)
            for v, dst in ((I["s5_a_re"], r_are), (I["s5_a_im"], r_aim)):
                pool.dma_start(dst, v[0].rearrange("d g n -> (d g) n")).then_inc(s_s5in, 16)
            pool.dma_start(r_ls, I["s5_log_step"][0].rearrange("d (g a) -> (d g) a", a=1)).then_inc(s_s5in, 16)
            for n, v in enumerate((I["s5_c_re"], I["s5_c_im"], I["s5_c_re"])):
                pool.dma_start(C3[:, :, n, :], v[0].rearrange("d (b g) c n -> (g c) (d b) n", b=8)).then_inc(s_s5in, 16)
            for dst, top, low in ((Bst, I["s5_b_re"], I["s5_b_im"]), (Bsw, I["s5_b_im"], I["s5_b_re"])):
                for q, v in ((0, top), (1, low)):
                    pool.dma_start(dst[NS * q:NS * (q + 1), :, :], v[0].rearrange("g n c -> n g c")).then_inc(s_s5in, 16)
            pool.wait_ge(s_u, 8)
            pool.dma_start(nw[:, 1, :], row(norm_w[5]).broadcast_to([P, D])).then_inc(s_nw[1], 16)
            for hf in range(2):
                for b in range(8 * hf, 8 * hf + 8):
                    if b % 8:
                        pool.wait_ge(s_bp, b)
                    elif b:
                        pool.wait_ge(s_cp, b)
                    for d in range(2):
                        m = pool.tensor_tensor(BQ[:, d, :, :].rearrange("p g (m c) -> p g m c", m=L5),
                                               Bsw[:, BG * b:BG * (b + 1), :].unsqueeze(2).broadcast_to([P, BG, L5, GC]),
                                               WB[:, d, BG * b:BG * (b + 1), :].unsqueeze(3).broadcast_to([P, BG, L5, GC]),
                                               ALU.mult)
                    m.then_inc(s_t2, 1)
                pool.wait_ge(s_vd, 8 * (hf + 1))
                pool.wait_ge(s_z0, hf + 1)
                scan(pool, chain, 1, hf, s_zb)
                for b in range(8 * hf, 8 * hf + 8):
                    if b % 8:
                        pool.wait_ge(s_cp, b)
                    else:
                        pool.wait_ge(s_bp, 8 * (hf + 1))
                    for d in range(2):
                        m = pool.tensor_tensor(CQ[:, d, :, :].rearrange("p g (m c) -> p g m c", m=M5),
                                               Csw[:, d, BG * b:BG * (b + 1), :].unsqueeze(2).broadcast_to([P, BG, M5, GC]),
                                               PB[:, d, BG * b:BG * (b + 1), :].unsqueeze(3).broadcast_to([P, BG, M5, GC]),
                                               ALU.mult)
                    m.then_inc(s_t2, 1)
            pool.wait_ge(s_yy, BATCHES)
            pool.dma_start(skip_w, row(I["s5_d"][0]).broadcast_to([P, D])).then_inc(s_dw, 16)
            pool.dma_start(ptok1, p_in[1, 0].rearrange("(c p) n -> p c n", p=P)).then_inc(s_p, 16)
            pool.dma_start(pw1, I["ple_proj"][1].rearrange("(k p) n -> p k n", p=P)).then_inc(s_pw, 16)

            pool.wait_ge(s_drD, cumD[gidx["go1"]])
            pool.dma_start(router, I["moe_router"][0].rearrange("(k p) e -> p k e", p=P)).then_inc(s_rtr, 16)
            pool.wait_ge(s_hn, 20)
            pool.dma_start(nw[:, 0, :], row(norm_w[6]).broadcast_to([P, D])).then_inc(s_nw[0], 16)
            pool.wait_ge(s_mys, 16 * 2)
            pool.wait_ge(s_plan, 1)
            pool.wait_ge(s_hnm, 16 * TC)

            def hold(n):
                return pool.tensor_tensor(slot_junk[:, n:n + 1], ident[:, 0:1], ident[:, 1:2], ALU.add)

            def gather_block(column, count):
                pool.tensor_copy(slot_now, column).then_inc(s_ix, 1)
                pool.wait_ge(s_ix, count)
                hold(1).then_inc(s_ix, 1)
                pool.indirect_dma_start(xblk, None, moe_dram, bass.IndirectOffsetOnAxis(slot_now, 0)).then_inc(s_xg, 16)

            gather_block(slot_tok[:, 0:1], 1)
            for j in range(2):
                pool.dma_start(gw[:, j, :, :], I["ple_gate"][1][:, 512 * j:512 * (j + 1)].rearrange("(k p) n -> p k n", p=P)
                               ).then_inc(s_gw, 16)
            blocks_pool = pool.value_load(plan[0:1, MAXB:MAXB + 1], min_val=2 * TC, max_val=MAXB)
            with pool.Fori(0, MAXB) as i:
                with pool.If(i < blocks_pool):
                    pool.wait_ge(s_xtp, 2 * i + 2)
                    hold(0).then_inc(s_ix, 1)
                    gather_block(slot_tok[:, bass.ds(i + 1, 1)], 4 * i + 4)
                    pool.wait_ge(s_myd, i + 2)
                    hold(2).then_inc(s_ix, 1)
                    pool.dma_start(y_rows[bass.ds(i * P, P), :], yblk).then_inc(s_mys, 16)
            pool.wait_ge(s_mys, blocks_pool * 16 + 32)
            pool.wait_ge(s_xg, blocks_pool * 16 + 16)
            hold(3)
            for c in range(TC):
                for k in range(2):
                    pool.indirect_dma_start(yg[k][:, c, :], None, y_rows,
                                            bass.IndirectOffsetOnAxis(desti[:, k, c:c + 1], 0)).then_inc(s_yg[c], 16)


        @block.tensor
        def _(pe):
            def tile(n):
                pe.wait_ge(s_ring[n % RING], 16 * (n // RING + 1))
                return ring[:, n % RING, :].rearrange("p (k n) -> p k n", k=2 if stream[n][1] == -1 else 4)

            def all_drained(name):
                g = gidx[name]
                if cumA[g]:
                    pe.wait_ge(s_drA, cumA[g])
                if cumD[g]:
                    pe.wait_ge(s_drD, cumD[g])

            def transpose_norm(k):
                for c in range(TC):
                    pe.wait_ge(s_hn, 4 * k + c + 1)
                    for g in range(2):
                        for q in range(4):
                            m = pe.transpose(psum[:, 2 * c + g, q * P:(q + 1) * P],
                                             hn[:, c, (4 * g + q) * P:(4 * g + q + 1) * P], ident)
                        m.then_inc(s_tp, 1)
                pe.wait_ge(s_hA, 4 * (TURN[k] + 1))
                pe.wait_ge(s_hD, 4 * (TURN[k] + 1))

            def dense(name, act):
                g = gidx[name]
                _, layout, width, _, t0 = groups[g]
                if t0 is None:
                    pe.wait_ge(s_gw, 32)
                b0 = 4 * (g % 2)
                if g >= 2:
                    all_drained(groups[g - 2][0])
                for kk in range(2):
                    w = gw[:, int(name[-1]), 4 * kk:4 * kk + 4, :] if t0 is None else tile(t0 + kk)
                    for b in range(4):
                        for k in range(4):
                            at = dict(start=kk == 0 and k == 0, stop=kk == 1 and k == 3, skip_group_check=True)
                            if layout == "T":
                                m = pe.matmul(psum[:, b0 + b, :], w[:, k, b * P:(b + 1) * P], act[:, 4 * kk + k, :], **at)
                            else:
                                m = pe.matmul(psum[:, b0 + b, 0:width], act[:, 4 * kk + k, b * P:(b + 1) * P],
                                              w[:, k, 0:width], **at)
                        if kk == 1:
                            m.then_inc(s_grp, 1)
                    if kk == 0 and t0 is not None:
                        m.then_inc(s_used, 1)

            pe.wait_ge(s_const, 6)
            pe.wait_ge(s_par, 16 * 6)
            pe.transpose(psum[:, 7, 0:68], parR[0:68, :], ident[0:68, 0:68]).then_inc(s_parT, 1)
            pe.wait_ge(s_parTd, 1)
            transpose_norm(0)
            for name in ("q", "ff", "fb", "v", "g"):
                dense(name, hnT)

            def hg_out(hd):
                pe.wait_ge(s_gdr, 18 * (hd + 1))
                if hd >= 2:
                    pe.wait_ge(s_mix, hd - 1)
                for c in range(TC):
                    m = pe.matmul(psum[:, 5 + hd % 2, :], vtok[:, c, hd * P:(hd + 1) * P], S_main[:, c, :],
                                  start=c == 0, stop=c == TC - 1)
                m.then_inc(s_o, 1)

            def hg_squares(hd):
                pe.wait_ge(s_osq, hd + 1)
                if hd >= 1:
                    pe.wait_ge(s_orms, hd)
                pe.matmul(psum[:, 7, :], ones, osq, start=True, stop=True).then_inc(s_oss, 1)

            all_drained("g")
            for hd in range(HEADS):
                pe.wait_ge(s_ks, hd + 1)
                if hd >= 1:
                    pe.wait_ge(s_sd, hd)
                for c in range(TC):
                    at = slice(c * P, (c + 1) * P)
                    m = pe.matmul(psum[:, 4, at], ksum[:, at], qT[:, hd, at], start=True, stop=True)
                m.then_inc(s_dg, 1)
                for j in range(18):
                    n, l, d = hd * 18 + j, j // 2, j % 2
                    X, bank = Xb[n % 4], psum[:, n % 4, :]
                    pe.wait_ge(s_X, n + 1)
                    if n >= 4:
                        pe.wait_ge(s_gdr, n - 3)
                    if l < 7:
                        for c in range(TC):
                            at = slice(c * P, (c + 1) * P)
                            m = pe.matmul(bank[:, at], X[:, at], X[:, at], start=True, stop=True)
                    elif l == 7:
                        for i in range(2):
                            s0, t0 = (2 * i, 2 * i + 1) if d == 0 else (2 * i + 1, 2 * i)
                            m = pe.matmul(bank[:, i * P:(i + 1) * P], X[:, s0 * P:(s0 + 1) * P],
                                          X[:, t0 * P:(t0 + 1) * P], start=True, stop=True)
                    else:
                        for i in range(2):
                            s0, t0 = (i, 2) if d == 0 else (2 + i, 0)
                            m = pe.matmul(bank[:, i * 256:(i + 1) * 256], X[:, s0 * P:(s0 + 1) * P],
                                          X[:, t0 * P:(t0 + 2) * P], start=True, stop=True)
                    m.then_inc(s_gram, 1)
                    if hd and j == 2:
                        hg_out(hd - 1)
                    if hd and j == 6:
                        hg_squares(hd - 1)
            hg_out(HEADS - 1)
            hg_squares(HEADS - 1)

            pe.wait_ge(s_mix, HEADS)
            pe.wait_ge(s_gdr, 18 * HEADS)
            for name in ("z", "xs", "bc", "dt"):
                dense(name, hnT)
            all_drained("dt")
            for cb in range(CB):
                pe.wait_ge(s_diag, cb + 1)
                if cb >= 2:
                    pe.wait_ge(s_cact, cb - 1)
                for k in range(CONV):
                    m = pe.matmul(psum[:, cb % 2, :], diag[:, cb % 2, k, :], raw[:, cb, k:k + T], start=k == 0,
                                  stop=k == CONV - 1)
                m.then_inc(s_conv, 1)
            pe.wait_ge(s_cact, CB)
            for c in range(TC):
                b = 4 + 2 * (c % 2)
                if c >= 2:
                    pe.wait_ge(s_xtd, c - 1)
                for q in range(6):
                    m = pe.transpose(psum[:, b + q // 4, (q % 4) * P:(q % 4 + 1) * P], xc[:, q, c * P:(c + 1) * P], ident)
                m.then_inc(s_xt, 1)
            pe.wait_ge(s_dt, 1)
            df = [dta[:, d, :, :].rearrange("p c k -> p (c k)") for d in range(2)]
            for n, (w, d) in enumerate(((LE_, 0), (GE_, 1), (GT_, 0), (LT_, 1))):
                pe.matmul(psum[:, 3, 32 * n:32 * n + 32], w, df[d], start=True, stop=True)
            pe.matmul(psum[:, 3, 128:192], ones, dta.rearrange("p d c k -> p (d c k)"), start=True,
                      stop=True).then_inc(s_cum, 1)
            for m_, (d, c) in enumerate(SSD_STATES):
                pe.wait_ge(s_xe, m_ + 1)
                if m_ >= 2:
                    pe.wait_ge(s_H, m_ - 1)
                for g in range(GROUPS):
                    m = pe.matmul(psum[:, m_ % 2, g * 256:(g + 1) * 256], btok[:, c, g * P:(g + 1) * P],
                                  xe[:, m_ % 2, g * 256:(g + 1) * 256], start=True, stop=True)
                m.then_inc(s_st, 1)
            pe.wait_ge(s_H, 6)
            pe.wait_ge(s_xtd, TC)
            pe.wait_ge(s_ex, 1)
            for c in range(TC):
                at = slice(c * P, (c + 1) * P)
                if c >= 1:
                    pe.wait_ge(s_cbm, c)
                for g in range(GROUPS):
                    m = pe.matmul(psum[:, 2, g * P:(g + 1) * P], xc[:, 4 + g, at], xc[:, 6 + g, at], start=True, stop=True)
                m.then_inc(s_cb, 1)
                pe.wait_ge(s_dtau, c + 1)
                if c >= 1:
                    pe.wait_ge(s_E, c)
                for n in range(4):
                    d = n // 2
                    m = pe.matmul(psum[:, 4 + n, :], (GT_, LT_)[d],
                                  dtaU[:, d, 4 * (n % 2):4 * (n % 2) + 4, :].rearrange("p k t -> p (k t)"),
                                  start=True, stop=True)
                m.then_inc(s_seg, 1)
                pe.wait_ge(s_w, c + 1)
                pe.wait_ge(s_xdt, c + 1)
                if c >= 1:
                    pe.wait_ge(s_yd, c)
                for k in range(MH):
                    for d in range(2):
                        m = pe.matmul(psum[:, 3, k * MP:(k + 1) * MP], Ew[:, d, k, :], xdt[:, d, k * MP:(k + 1) * MP],
                                      start=d == 0, stop=d == 1, skip_group_check=True)
                for d in range(2):
                    if c == (0, TC - 1)[d]:
                        continue
                    for g in range(GROUPS):
                        m = pe.matmul(psum[:, d, g * 256:(g + 1) * 256], xc[:, 6 + g, at],
                                      Hst[d][:, c - 1 + d, g * 256:(g + 1) * 256], start=True, stop=True)
                m.then_inc(s_y, 1)
            for c in range(TC):
                pe.wait_ge(s_yn, c + 1)
                if c >= 2:
                    pe.wait_ge(s_ym, c - 1)
                for q in range(4):
                    m = pe.transpose(psum[:, 4 + c % 2, q * P:(q + 1) * P], yst[:, c, q * P:(q + 1) * P], ident)
                m.then_inc(s_yt, 1)
            pe.wait_ge(s_ym, TC)
            dense("o0", mixT)
            dense("o1", mixT)

            all_drained("o1")
            transpose_norm(1)
            for j in range(FJ):
                dense(f"fg{j}", hnT)
                dense(f"fu{j}", hnT)
            all_drained(f"fu{FJ - 1}")
            for j in range(FJ):
                for hf in range(2):
                    n = down_tile0 + 2 * j + hf
                    w = tile(n)
                    for c in range(TC):
                        for k in range(4):
                            m = pe.matmul(psum[:, 2 * c + hf, :], hT[:, 4 * j + k, c * P:(c + 1) * P], w[:, k, :],
                                          start=j == 0 and k == 0, stop=j == FJ - 1 and k == 3, skip_group_check=True)
                        if j == FJ - 1:
                            m.then_inc(s_ffd, 1)
                    if j < FJ - 1:
                        m.then_inc(s_used, 1)

            def embed(layer):
                ptok_, pT_ = ((ptok, pT), (ptok1, pT1))[layer]
                pe.wait_ge(s_p, 16 * (layer + 1))
                for c in range(TC):
                    for q in range(2):
                        m = pe.transpose(psum[:, 0, c * P:(c + 1) * P] if q == 0 else psum[:, 1, c * P:(c + 1) * P],
                                         ptok_[:, c, q * P:(q + 1) * P], ident)
                m.then_inc(s_pT, 1)
                pe.wait_ge(s_pTd, layer + 1)
                if layer:
                    pe.wait_ge(s_pw, 16)
                w = pw1 if layer else tile(ple_tile)
                for c in range(TC):
                    for hf in range(2):
                        for k in range(2):
                            m = pe.matmul(psum[:, 2 * c + hf, :], pT_[:, k, c * P:(c + 1) * P],
                                          w[:, k, hf * 512:(hf + 1) * 512], start=k == 0, stop=k == 1)
                        m.then_inc(s_pp, 1)
                pe.wait_ge(s_ppd, 8 * (layer + 1))

            pe.wait_ge(s_fd, 8)
            embed(0)
            transpose_norm(2)
            dense("pg00", hnT)
            dense("pg01", hnT)

            all_drained("pg01")
            pe.wait_ge(s_s5in, 16 * 10)
            for n in range(16):
                if n >= 4:
                    pe.wait_ge(s_cst, n - 3)
                for v in range(2):
                    m = pe.transpose(psum[:, n % 4, v * P:(v + 1) * P], C3[:, n, v:v + 2, :].rearrange("p q n -> p (q n)"), ident)
                m.then_inc(s_rt, 1)
            pe.wait_ge(s_rowt, 1)
            for n, (k, m_) in enumerate(ROW_TABLES):
                if n >= 4:
                    pe.wait_ge(s_cst, 16 + n - 3)
                m = pe.transpose(psum[:, 4 + n % 4, 0:P], rowt[:, k, m_, :, :].rearrange("p q n -> p (q n)"), ident)
                m.then_inc(s_rt, 1)
            pe.wait_ge(s_cst, 16 + len(ROW_TABLES))
            pe.wait_ge(s_un, 16)
            for n in range(8):
                pe.wait_ge(s_up, n + 1)
                for q in range(8):
                    m = pe.transpose(psum[:, n, NC5 * q:NC5 * (q + 1)], UP[n % 2][0:NC5, P * q:P * (q + 1)], ident[0:NC5, 0:NC5])
                m.then_inc(s_ut, 1)
            pe.wait_ge(s_u, 8)
            for hf in range(2):
                for b in range(8 * hf, 8 * hf + 8):
                    pe.wait_ge(s_bp, b + 1)
                    for d in range(2):
                        for g in range(BG):
                            m = pe.transpose(psum[:, d, g * P:(g + 1) * P], BP[:, d, g, :], ident)
                    m.then_inc(s_bt, 1)
                    pe.wait_ge(s_bigA, b + 1)
                    pe.wait_ge(s_bigD, b + 1)
                    if b % 8:
                        pe.wait_ge(s_vd, b)
                    for d in range(2):
                        for e in range(2):
                            for g in range(BG):
                                m = pe.matmul(psum[:, 2 + d, (e * BG + g) * NC5:(e * BG + g + 1) * NC5],
                                              BigB[:, d, g, NS - NS * e:NS - NS * e + P], U[:, BG * b + g, :],
                                              start=True, stop=True)
                    m.then_inc(s_v, 1)
                pe.wait_ge(s_vd, 8 * (hf + 1))
                for b in range(8 * hf, 8 * hf + 8):
                    gl = BG * (b - 8 * hf)
                    pe.wait_ge(s_cp, b + 1)
                    for d in range(2):
                        for g in range(BG):
                            m = pe.matmul(psum[0:GC, 4 + d, g * P:(g + 1) * P], BBk[:, d, gl + g, :],
                                          CP[:, d, g, GC * d:GC * d + P], start=True, stop=True)
                    m.then_inc(s_kk, 1)
                    if b % 8 == 0:
                        pe.wait_ge(s_zf, hf + 1)
                        pe.wait_ge(s_zb, hf + 1)
                    pe.wait_ge(s_kb, 16 * L5 * (b + 1))
                    if b:
                        pe.wait_ge(s_yb, b)
                    for g in range(BG):
                        o = psum[0:NC5, 6, g * P:(g + 1) * P]
                        pe.matmul(o, U[:, BG * b + g, :], Kbig[:, g, :], start=True, stop=False, skip_group_check=True)
                        for d in range(2):
                            first = z_at[d] + d * ZS + gl + g
                            states = bass.AP(sbuf, first, [[words, P], [ZS, NC5]])
                            m = pe.matmul(o, states, CP[:, d, g, GC * (1 - d):GC * (1 - d) + P], start=False, stop=d == 1,
                                          skip_group_check=True)
                    m.then_inc(s_yy, 1)
            pe.wait_ge(s_yb, BATCHES)
            for c in range(TC):
                pe.wait_ge(s_gl, c + 1)
                for g in range(2):
                    for q in range(4):
                        m = pe.transpose(psum[:, 2 * c + g, q * P:(q + 1) * P],
                                         ytok[:, c, (4 * g + q) * P:(4 * g + q + 1) * P], ident)
                    m.then_inc(s_glt, 1)
            pe.wait_ge(s_glA, 4)
            pe.wait_ge(s_glD, 4)
            for j in range(2):
                dense(f"gg{j}", hnT)
                dense(f"go{j}", hnT)

            all_drained("go1")
            embed(1)
            transpose_norm(4)
            pe.matmul(psum[:, 1, 128:256], ones, LT, start=True, stop=True)
            pe.matmul(psum[:, 1, 64:65], LT, ones[:, 0:1], start=True, stop=True)
            pe.wait_ge(s_rtr, 16)
            for c in range(TC):
                for k in range(8):
                    m = pe.matmul(psum[:, 0, NE * c:NE * (c + 1)], hnT[:, k, c * P:(c + 1) * P], router[:, k, :],
                                  start=k == 0, stop=k == 7)
                    if (c, k) == (0, 0):
                        m.then_inc(s_mt, RING)
            m.then_inc(s_lg, 1)
            pe.wait_ge(s_hot, 1)
            for c in range(TC):
                for c0 in range(c + 1):
                    pe.matmul(psum[:, 1, NE * c:NE * (c + 1)], LT if c0 == c else ones, hot[:, 2, c0, :], start=c0 == 0,
                              stop=c0 == c, skip_group_check=True)
            for c in range(TC):
                m = pe.matmul(psum[:, 1, 32:32 + NE], ones, hot[:, 2, c, :], start=c == 0, stop=c == TC - 1,
                              skip_group_check=True)
            m.then_inc(s_rank, 1)
            pe.wait_ge(s_slot, 1)
            for n in range(2 * TC):
                k, c = n // TC, n % TC
                m = pe.matmul(psum[:, 2, 0:MAXB + 1], moe_hotR[:, k, c, :], moe_hotB[:, k, c, :], start=n == 0,
                              stop=n == 2 * TC - 1)
            m.then_inc(s_tok, 1)
            pe.wait_ge(s_plan, 1)
            blocks_pe = pe.value_load(plan[0:1, MAXB:MAXB + 1], min_val=2 * TC, max_val=MAXB)
            with pe.Fori(0, MAXB) as i:
                with pe.If(i < blocks_pe):
                    def moe_tile(jj):
                        slot = (N0 + jj) % RING
                        pe.wait_ge(s_ring[slot], i * (16 * PER // RING) + 16 * ((N0 + jj) // RING + 1))
                        return ring[:, slot, :].rearrange("p (k n) -> p k n", k=4)

                    def expert_down(j):
                        pe.wait_ge(s_mhc, EJ * i + j + 1)
                        if j == 0:
                            pe.wait_ge(s_myd, i + 1)
                        for hf in range(2):
                            w = moe_tile(down_at(j) + hf)
                            for k in range(4):
                                m = pe.matmul(psum[:, 6 + hf, :], ehT[:, j % 2, k, :], w[:, k, :],
                                              start=j == 0 and k == 0, stop=j == EJ - 1 and k == 3, skip_group_check=True)
                            m.then_inc(s_mt, 1)

                    def expert_turn(j):
                        pe.wait_ge(s_mh, EJ * i + j + 1)
                        for q in range(4):
                            m = pe.transpose(psum[:, 4 + j % 2, q * P:(q + 1) * P], ehid[:, j % 2, q * P:(q + 1) * P], ident)
                        m.then_inc(s_mht, 1)

                    pe.wait_ge(s_xg, 16 * i + 16)
                    for g in range(2):
                        for q in range(4):
                            m = pe.transpose(psum[:, 4 + g, q * P:(q + 1) * P], xblk[:, (4 * g + q) * P:(4 * g + q + 1) * P], ident)
                        m.then_inc(s_xtp, 1)
                    pe.wait_ge(s_xtA, i + 1)
                    pe.wait_ge(s_xtD, i + 1)
                    for j in range(EJ):
                        for part in range(2):
                            for kk in range(2):
                                w = moe_tile(gu_at(j) + 2 * part + kk)
                                for k in range(4):
                                    m = pe.matmul(psum[:, 2 * part + j % 2, :], xbT[:, 4 * kk + k, :], w[:, k, :],
                                                  start=kk == 0 and k == 0, stop=kk == 1 and k == 3, skip_group_check=True)
                                m.then_inc(s_mt, 1)
                            if part == 0 and j:
                                expert_turn(j - 1)
                        if j:
                            expert_down(j - 1)
                    expert_turn(EJ - 1)
                    expert_down(EJ - 1)
            transpose_norm(5)
            dense("pg10", hnT)
            dense("pg11", hnT)

        @block.scalar
        def _(act):
            def norm(k, ready, turn=True):
                for c in range(TC):
                    ready(act, c)
                    act.activation(hn[:, c, :], h[:, c, :], ACT.Square, accum_out=stat[:, k, 0, c:c + 1]).then_inc(s_sq, 1)
                act.wait_ge(s_sq, 4 * (k + 1))
                act.activation(stat[:, k, 1, :], stat[:, k, 0, :], ACT.Sqrt, bias=eps, scale=1.0 / D).then_inc(s_rms, 1)
                for c in range(TC if turn else 0):
                    act.wait_ge(s_tp, 8 * TURN[k] + 2 * c + 1)
                    act.activation(hnT[:, 0:4, c * P:(c + 1) * P], psum[:, 2 * c, :].rearrange("p (q t) -> p q t", q=4),
                                   ACT.Copy).then_inc(s_hA, 1)

            def drain(name, out_of, func):
                g = gidx[name]
                for b in range(4):
                    act.wait_ge(s_grp, 4 * g + b + 1)
                    act.activation(out_of(b), psum[:, 4 * (g % 2) + b, :], func).then_inc(s_drA, 1)

            act.wait_ge(s_const, 1)
            norm(0, h_ready[0])
            act.wait_ge(s_lb, 1)
            act.activation(hgc[:, 1, :], hgc[:, 0, :], ACT.Exp).then_inc(s_lbc, 1)
            drain("q", lambda b: qT[:, b, :], ACT.Silu)
            for name, d in (("ff", 0), ("fb", 1)):
                g = gidx[name]
                for b in range(4):
                    bank = psum[:, 4 * (g % 2) + b, :]
                    act.wait_ge(s_grp, 4 * g + b + 1)
                    act.activation(lf[d][:, b, :], bank, ACT.Sigmoid)
                    act.activation(kT[d][:, b, :], bank, ACT.Sigmoid, scale=-1.0).then_inc(s_drA, 1)
            drain("g", lambda b: gT[:, b, :], ACT.Sigmoid)
            for d in range(2):
                act.wait_ge(s_lnin, d + 1)
                act.activation(lf[d], lf[d], ACT.Ln)
                act.activation(lnb4, lnb4, ACT.Ln).then_inc(s_lnout, 1)

            def hg_square(hd):
                act.wait_ge(s_o, hd + 1)
                if hd == HEADS - 1:
                    pass
                act.activation(osq, psum[:, 5 + hd % 2, :], ACT.Square).then_inc(s_osq, 1)

            def hg_rms(hd):
                act.wait_ge(s_oss, hd + 1)
                if hd:
                    act.wait_ge(s_mix, hd)
                act.activation(orms, psum[:, 7, :], ACT.Sqrt, bias=eps, scale=1.0 / P).then_inc(s_orms, 1)

            act.wait_ge(s_lf, 2)
            for hd in range(HEADS):
                act.wait_ge(s_rz, hd + 1)
                for j in range(18):
                    n, l, d = hd * 18 + j, j // 2, j % 2
                    if n >= 4:
                        act.wait_ge(s_gram, n - 3)
                    if l:
                        act.wait_ge(s_upd, hd * 16 + 2 * (l - 1) + d + 1)
                    hs = 1 << l
                    near, far = (0, 1) if d == 0 else (1, 0)
                    act.activation(half(Xb[n % 4], hs, far), half(lf[d][:, hd, :], hs, far), ACT.Exp)
                    act.activation(half(Xb[n % 4], hs, near), half(Rs[hd % 2][d], hs, near), ACT.Exp).then_inc(s_exp, 1)
                    if hd and j == 5:
                        hg_square(hd - 1)
                    if hd and j == 9:
                        hg_rms(hd - 1)
            hg_square(HEADS - 1)
            hg_rms(HEADS - 1)

            act.wait_ge(s_mix, HEADS)
            drain("z", lambda b: zs[:, b, :], ACT.Silu)
            act.wait_ge(s_parTd, 1)
            for cb in range(CB):
                act.wait_ge(s_conv, cb + 1)
                act.activation(xc[:, cb, :], psum[:, cb % 2, :], ACT.Silu, bias=parT[:, 40 + cb:41 + cb]).then_inc(s_cact, 1)
            act.wait_ge(s_sp, 2)
            act.activation(dtt, dtt, ACT.Exp, scale=-1.0).then_inc(s_ac, 1)
            act.wait_ge(s_ac, 1)
            act.activation(dtt, dtt, ACT.Ln, bias=1.0).then_inc(s_ac, 1)
            act.activation(aneg, alog, ACT.Exp).then_inc(s_ac, 1)
            act.wait_ge(s_cum, 1)
            act.activation(ex, psum[:, 3, 0:192], ACT.Exp).then_inc(s_ex, 1)
            for c in range(TC):
                act.wait_ge(s_seg, c + 1)
                if c:
                    act.wait_ge(s_y, c)
                act.activation(Ew.rearrange("p d k t -> p (d k t)"), psum[:, 4:8, :].rearrange("p b n -> p (b n)"),
                               ACT.Exp).then_inc(s_E, 1)
                if c:
                    ssd_squares(act, c - 1)
            ssd_squares(act, TC - 1)
            act.wait_ge(s_ysq, TC)
            act.activation(ssy[:, 1, :], ssy[:, 0, :], ACT.Sqrt, bias=eps, scale=1.0 / (INNER // GROUPS)).then_inc(s_yrms, 1)

            norm(1, h_ready[1])
            for j in range(FJ):
                g = gidx[f"fg{j}"]
                for b in range(4):
                    act.wait_ge(s_grp, 4 * g + b + 1)
                    if j:
                        act.wait_ge(s_drD, cumD[gidx[f"fu{j - 1}"]] - 3 + b)
                    act.activation(silT[:, b, :], psum[:, 4 * (g % 2) + b, :], ACT.Silu).then_inc(s_drA, 1)
            act.wait_ge(s_pT, 1)
            act.activation(pT[:, 0, :], psum[:, 0, :], ACT.Copy).then_inc(s_ac, 1)
            norm(2, h_ready[2])

            def gate_ple(layer):
                gates = pgate.rearrange("p k t -> p (k t)").rearrange("p (c n) -> p c n", c=4)
                for j in range(2):
                    g = gidx[f"pg{layer}{j}"]
                    for b in range(4):
                        act.wait_ge(s_grp, 4 * g + b + 1)
                        act.activation(gates[:, b, 512 * j:512 * (j + 1)], psum[:, 4 * (g % 2) + b, :],
                                       ACT.Sigmoid).then_inc(s_drA, 1)

            gate_ple(0)

            act.wait_ge(s_s5in, 16 * 10)
            act.activation(r_ls, r_ls, ACT.Exp).then_inc(s_sin, 1)
            act.wait_ge(s_ang, 1)
            act.activation(r_x, r_x, ACT.Exp).then_inc(s_sin, 1)
            act.wait_ge(s_ang, 2)
            act.activation(r_s, r_r, ACT.Sin)
            act.activation(r_c, r_r, ACT.Sin, scale=0.5).then_inc(s_sin, 1)
            norm(3, h_ready[3], False)
            act.wait_ge(s_un, 16)
            for n in range(8):
                if n >= 2:
                    act.wait_ge(s_ut, n - 1)
                act.activation(UP[n % 2][0:NC5, 0:8 * P].rearrange("p (g t c) -> p t g c", g=8, t=L5),
                               UN[:, :, P * n:P * (n + 1)].rearrange("p t (g c) -> p t g c", g=8), ACT.Copy).then_inc(s_up, 1)
            for b in range(BATCHES):
                act.wait_ge(s_bt, b + 1)
                if b % 8:
                    act.wait_ge(s_v, b)
                src = psum[:, 0, :].rearrange("p (g n) -> p g n", g=BG)
                act.activation(BigB[:, 0, :, NS:192], src, ACT.Copy)
                act.activation(BigB[:, 0, :, 0:NS], src[:, :, NS:P], ACT.Copy, scale=-1.0).then_inc(s_bigA, 1)
                if b % 8 == 7:
                    for bb in range(b - 7, b + 1):
                        act.wait_ge(s_yy, bb + 1)
                        if bb:
                            act.wait_ge(s_ydr, 16 * bb)
                        for g in range(BG):
                            m = act.activation(Yb[0:NC5, :, GC * g:GC * (g + 1)],
                                               psum[0:NC5, 6, g * P:(g + 1) * P].rearrange("p (t c) -> p t c", t=L5), ACT.Copy)
                        m.then_inc(s_yb, 1)
            for c in range(TC):
                act.wait_ge(s_gin, c + 1)
                act.activation(ytok[:, c, :], ytok[:, c, :], ACT.Gelu_apprx_tanh).then_inc(s_gl, 1)
            for c in range(TC):
                act.wait_ge(s_glt, 2 * c + 1)
                act.activation(hnT[:, 0:4, c * P:(c + 1) * P], psum[:, 2 * c, :].rearrange("p (q t) -> p q t", q=4),
                               ACT.Copy).then_inc(s_glA, 1)
            for j in range(2):
                g = gidx[f"gg{j}"]
                for b in range(4):
                    act.wait_ge(s_grp, 4 * g + b + 1)
                    if j:
                        act.wait_ge(s_drD, cumD[gidx[f"go{j - 1}"]] - 3 + b)
                    act.activation(gtmp[:, b, :], psum[:, 4 * (g % 2) + b, :], ACT.Sigmoid).then_inc(s_drA, 1)

            act.wait_ge(s_pT, 2)
            act.activation(pT1[:, 0, :], psum[:, 0, :], ACT.Copy).then_inc(s_ac, 1)
            norm(4, h_ready[4])
            act.wait_ge(s_top, 1)
            act.activation(gate[:, 2, :], gate[:, 0, :], ACT.Exp).then_inc(s_gexp, 1)
            act.wait_ge(s_plan, 1)
            blocks_act = act.value_load(plan[0:1, MAXB:MAXB + 1], min_val=2 * TC, max_val=MAXB)
            with act.Fori(0, MAXB) as i:
                with act.If(i < blocks_act):
                    act.wait_ge(s_xtp, 2 * i + 1)
                    act.activation(xbT[:, 0:4, :], psum[:, 4, :].rearrange("p (q t) -> p q t", q=4), ACT.Copy).then_inc(s_xtA, 1)
                    for j in range(EJ):
                        act.wait_ge(s_mt, tiles_done(i, gu_at(j) + 2))
                        act.activation(esil[:, j % 2, :], psum[:, j % 2, :], ACT.Silu).then_inc(s_msl, 1)
                        if j:
                            act.wait_ge(s_mht, EJ * i + j)
                            act.activation(ehT[:, (j - 1) % 2, :, :], psum[:, 4 + (j - 1) % 2, :].rearrange("p (q t) -> p q t", q=4),
                                           ACT.Copy).then_inc(s_mhc, 1)
                    act.wait_ge(s_mht, EJ * i + EJ)
                    act.activation(ehT[:, (EJ - 1) % 2, :, :], psum[:, 4 + (EJ - 1) % 2, :].rearrange("p (q t) -> p q t", q=4),
                                   ACT.Copy).then_inc(s_mhc, 1)
            norm(5, h_ready[5])
            gate_ple(1)
            norm(6, h_ready[6], False)

        @block.vector
        def _(dve):
            chain = Chain(dve, s_vc)

            def norm(k, turn=True):
                dve.wait_ge(s_rms, k + 1)
                chain.link(dve.reciprocal(stat[:, k, 2, :], stat[:, k, 1, :]))
                chain.settle()
                dve.wait_ge(s_nw[k % 2], 16 * (k // 2 + 1))
                for c in range(TC):
                    dve.scalar_tensor_tensor(out=hn[:, c, :], in0=h[:, c, :], scalar=stat[:, k, 2, c:c + 1],
                                             in1=nw[:, k % 2, :], op0=ALU.mult, op1=ALU.mult).then_inc(s_hn, 1)
                for c in range(TC if turn else 0):
                    dve.wait_ge(s_tp, 8 * TURN[k] + 2 * c + 2)
                    dve.tensor_copy(hnT[:, 4:8, c * P:(c + 1) * P],
                                    psum[:, 2 * c + 1, :].rearrange("p (q t) -> p q t", q=4)).then_inc(s_hD, 1)

            def drain(name, out_of):
                g = gidx[name]
                width = groups[g][2]
                for b in range(4):
                    dve.wait_ge(s_grp, 4 * g + b + 1)
                    dve.tensor_copy(out_of(b), psum[:, 4 * (g % 2) + b, 0:width]).then_inc(s_drD, 1)

            dve.wait_ge(s_parT, 1)
            dve.tensor_copy(parT, psum[:, 7, 0:68]).then_inc(s_parTd, 1)
            norm(0)
            lbl = parT[:, 52:56]
            chain.settle()
            dve.wait_ge(s_parTd, 1)
            dve.tensor_tensor(hgc[:, 0, :], lbl, lbl, ALU.subtract).then_inc(s_lb, 1)
            dve.wait_ge(s_lbc, 1)
            chain.link(dve.reciprocal(hgc[:, 2, :], hgc[:, 1, :]))
            chain.settle()
            chain.link(dve.tensor_tensor(hgc[:, 3, :], hgc[:, 1, :], hgc[:, 2, :], ALU.mult))
            chain.settle()
            chain.link(dve.tensor_tensor(hgc[:, 4, :], hgc[:, 3, :], hgc[:, 3, :], ALU.subtract))
            chain.settle()
            chain.link(dve.tensor_scalar(hgc[:, 5, :], hgc[:, 4, :], LB_FLOOR, None, ALU.max))
            chain.link(dve.tensor_scalar(hgc[:, 6, :], hgc[:, 4, :], -1.0, 1.0, ALU.mult, ALU.add))
            chain.settle()
            chain.link(dve.tensor_tensor(hgc[:, 7, :], hgc[:, 4, :], hgc[:, 5, :], ALU.subtract))
            chain.settle()
            drain_v = lambda: drain("v", lambda b: vtok[:, b, :])
            drain_v()
            for d, name in enumerate(("ff", "fb")):
                dve.wait_ge(s_drA, cumA[gidx[name]])
                for b in range(4):
                    dve.tensor_scalar(kT[d][:, b, :], kT[d][:, b, :], hgc[:, 6, b:b + 1], hgc[:, 7, b:b + 1],
                                      ALU.mult, ALU.add).then_inc(s_k, 1)
                    chain.link(dve.tensor_scalar(lf[d][:, b, :], lf[d][:, b, :], hgc[:, 6, b:b + 1], hgc[:, 5, b:b + 1],
                                                 ALU.mult, ALU.add))
                chain.settle()
                chain.link(dve.tensor_scalar(lnb4, lf[d], 1.0 / LN_SPLIT, 1.0, ALU.mult, ALU.min))
                chain.settle()
                dve.tensor_scalar(lf[d], lf[d], LN_SPLIT, None, ALU.max).then_inc(s_lnin, 1)
                dve.wait_ge(s_lnout, d + 1)
                dve.tensor_tensor(lf[d], lf[d], lnb4, ALU.add).then_inc(s_lf, 1)

            def scores(n):
                hd, l, d = n // 18, (n % 18) // 2, n % 2
                dve.wait_ge(s_gram, n + 1)
                bank = psum[:, n % 4, :]
                if l < 7:
                    if (l, d) == (0, 0):
                        dve.wait_ge(s_sd, hd + 1)
                    else:
                        dve.wait_ge(s_gdr, n)
                    m = dve.copy_predicated(S_diag, masks[:, 2 * l + d, :].unsqueeze(1).broadcast_to([P, TC, P]),
                                            bank.rearrange("p (c t) -> p c t", c=TC))
                elif l == 7:
                    out_ = S_main.rearrange("p (i s) (a e t) -> p i s a e t", s=2, a=2, e=2)
                    for i in range(2):
                        s0, t0 = (2 * i, 2 * i + 1) if d == 0 else (2 * i + 1, 2 * i)
                        m = dve.tensor_copy(S_main[:, s0, t0 * P:(t0 + 1) * P], bank[:, i * P:(i + 1) * P])
                else:
                    s0, t0 = (0, 2) if d == 0 else (2, 0)
                    m = dve.tensor_copy(S_main[:, s0:s0 + 2, t0 * P:(t0 + 2) * P], bank.rearrange("p (i t) -> p i t", i=2))
                m.then_inc(s_gdr, 1)

            def hg_finish(hd):
                dve.wait_ge(s_orms, hd + 1)
                chain.link(dve.reciprocal(orms, orms))
                chain.settle()
                chain.link(dve.tensor_tensor(orms, psum[:, 5 + hd % 2, :], orms, ALU.mult))
                chain.settle()
                dve.scalar_tensor_tensor(out=mixT[:, hd, :], in0=orms, scalar=parT[:, 48 + hd:49 + hd], in1=gT[:, hd, :],
                                         op0=ALU.mult, op1=ALU.mult).then_inc(s_mix, 1)

            dve.wait_ge(s_drA, cumA[gidx["g"]])
            for hd in range(HEADS):
                for j in range(18):
                    n, l, d = hd * 18 + j, j // 2, j % 2
                    hs = 1 << l
                    near, far = (0, 1) if d == 0 else (1, 0)
                    X = Xb[n % 4]
                    dve.wait_ge(s_exp, n + 1)
                    dve.tensor_tensor(half(X, hs, far), half(X, hs, far), half(qT[:, hd, :], hs, far), ALU.mult)
                    dve.tensor_tensor(half(X, hs, near), half(X, hs, near), half(kT[d][:, hd, :], hs, near),
                                      ALU.mult).then_inc(s_X, 1)
                    if j == 2:
                        dve.wait_ge(s_dg, hd + 1)
                        if hd:
                            dve.wait_ge(s_o, hd)
                        dve.tensor_tensor(S_diag, psum[:, 4, :].rearrange("p (c t) -> p c t", c=TC),
                                          ident.unsqueeze(1).broadcast_to([P, TC, P]), ALU.mult).then_inc(s_sd, 1)
                    if j >= 3:
                        scores(n - 3)
                    if hd and j == 13:
                        hg_finish(hd - 1)
                for n in range(hd * 18 + 15, hd * 18 + 18):
                    scores(n)
            hg_finish(HEADS - 1)

            dve.wait_ge(s_pad, 1)
            drain("xs", lambda b: raw[:, b, 2:2 + T])
            drain("bc", lambda b: raw[:, 4 + b, 2:2 + T])
            drain("dt", lambda b: dtr[:, :, b, :])
            dve.wait_ge(s_tokp, 48)
            dve.wait_ge(s_drD, cumD[gidx["dt"]])
            chain.link(dve.tensor_tensor(dtr, dtr, dtb.rearrange("p (d k) -> p d k", d=2).unsqueeze(2).broadcast_to([P, 2, 4, 8]),
                                         ALU.add))
            chain.settle()
            chain.link(dve.tensor_scalar(dts, dtr, -1.0, None, ALU.mult))
            chain.settle()
            dve.tensor_tensor(dtt, dtr, dts, ALU.max).then_inc(s_sp, 1)
            dve.tensor_scalar(dtr, dtr, 0.0, None, ALU.max).then_inc(s_sp, 1)
            dve.wait_ge(s_ac, 3)
            dve.wait_ge(s_sp, 2)
            chain.link(dve.tensor_tensor(dts, dtr, dtt, ALU.add))
            chain.settle()
            chain.link(dve.tensor_tensor(dta, dts, aneg.rearrange("p (d k) -> p d k", d=2).unsqueeze(2).broadcast_to([P, 2, 4, 8]),
                                         ALU.mult))
            chain.settle()
            dve.tensor_scalar(dta, dta, -1.0, None, ALU.mult).then_inc(s_dt, 1)
            for c in range(TC):
                b = 4 + 2 * (c % 2)
                dve.wait_ge(s_xt, c + 1)
                dve.tensor_copy(xst[:, c, :], psum[:, b, :])
                dve.tensor_copy(btok[:, c, :], psum[:, b + 1, 0:256]).then_inc(s_xtd, 1)
            dve.wait_ge(s_ex, 1)
            exA = ex[:, 0:64].rearrange("p (d c k) -> p d c k", d=2, c=4)
            tot = ex[:, 128:192].rearrange("p (d c k) -> p d c k", d=2, c=4)
            heads = lambda ap: ap.rearrange("p (k n) -> p k n", k=MH)
            for m_, (d, c) in enumerate(SSD_STATES):
                dve.wait_ge(s_st, m_ + 1)
                bank = psum[:, m_ % 2, :]
                slot = c if d == 0 else c - 1
                new = Hst[d][:, slot, :]
                if m_ < 2:
                    dve.tensor_copy(new, bank).then_inc(s_H, 1)
                else:
                    old = Hst[d][:, slot - 1 if d == 0 else slot + 1, :]
                    dve.wait_ge(s_H, m_ - 1)
                    chain.link(dve.tensor_tensor(heads(new), heads(old), tot[:, d, c, :].unsqueeze(2).broadcast_to([P, MH, MP]), ALU.mult))
                    chain.settle()
                    dve.tensor_tensor(new, new, bank, ALU.add).then_inc(s_H, 1)
            for c in range(TC):
                dve.wait_ge(s_cb, c + 1)
                for d in range(2):
                    m = dve.tensor_tensor(cbm[:, d, :, :], psum[:, 2, 0:256].rearrange("p (g t) -> p g t", g=2),
                                          (LE_, GE_)[d].unsqueeze(1).broadcast_to([P, GROUPS, P]), ALU.mult)
                m.then_inc(s_cbm, 1)
                dve.wait_ge(s_cbm, c + 1)
                dve.wait_ge(s_E, c + 1)
                for d in range(2):
                    for g in range(GROUPS):
                        e = Ew[:, d, HPG * g:HPG * (g + 1), :]
                        m = dve.tensor_tensor(e, e, cbm[:, d, g, :].unsqueeze(1).broadcast_to([P, HPG, P]), ALU.mult)
                m.then_inc(s_w, 1)
                y = yst[:, c, :]
                dve.wait_ge(s_xtd, c + 1)
                chain.link(dve.tensor_tensor(heads(y), heads(xst[:, c, :]), dskip.unsqueeze(2).broadcast_to([P, MH, MP]), ALU.mult))
                dve.wait_ge(s_y, c + 1)
                dirs = [d for d in range(2) if c != (0, TC - 1)[d]]
                for d in dirs:
                    chain.settle()
                    chain.link(dve.tensor_tensor(heads(ytmp), heads(psum[:, d, :]), exA[:, d, c, :].unsqueeze(2).broadcast_to([P, MH, MP]), ALU.mult))
                    chain.settle()
                    chain.link(dve.tensor_tensor(y, y, ytmp, ALU.add))
                chain.settle()
                dve.tensor_tensor(y, y, psum[:, 3, :], ALU.add).then_inc(s_yd, 1)
                dve.wait_ge(s_yd, c + 1)
                dve.wait_ge(s_drA, cumA[gidx["z"]])
                dve.tensor_tensor(y, y, zs[:, c, :], ALU.mult).then_inc(s_yz, 1)
            dve.wait_ge(s_yrms, 1)
            chain.link(dve.reciprocal(ssy[:, 2, :], ssy[:, 1, :]))
            chain.settle()
            for c in range(TC):
                for g in range(GROUPS):
                    y = yst[:, c, g * 256:(g + 1) * 256]
                    m = dve.tensor_scalar(y, y, ssy[:, 2, 2 * c + g:2 * c + g + 1], None, ALU.mult)
                m.then_inc(s_yn, 1)
            for c in range(TC):
                dve.wait_ge(s_yt, c + 1)
                dve.tensor_tensor(mixT[:, 4:8, c * P:(c + 1) * P], psum[:, 4 + c % 2, :].rearrange("p (q t) -> p q t", q=4),
                                  parT[:, 56:60].unsqueeze(2).broadcast_to([P, 4, P]), ALU.mult).then_inc(s_ym, 1)

            def add_to_h(name, half_):
                g = gidx[name]
                for b in range(4):
                    dve.wait_ge(s_grp, 4 * g + b + 1)
                    hh = h[:, b, 512 * half_:512 * (half_ + 1)]
                    dve.tensor_tensor(hh, hh, psum[:, 4 * (g % 2) + b, :], ALU.add).then_inc(s_drD, 1)

            add_to_h("o0", 0)
            add_to_h("o1", 1)
            norm(1)
            for j in range(FJ):
                g = gidx[f"fu{j}"]
                for b in range(4):
                    dve.wait_ge(s_grp, 4 * g + b + 1)
                    dve.wait_ge(s_drA, cumA[gidx[f"fg{j}"]] - 3 + b)
                    dve.tensor_tensor(hT[:, 4 * j + b, :], silT[:, b, :], psum[:, 4 * (g % 2) + b, :],
                                      ALU.mult).then_inc(s_drD, 1)
            for c in range(TC):
                for hf in range(2):
                    dve.wait_ge(s_ffd, 4 * hf + c + 1)
                    hh = h[:, c, 512 * hf:512 * (hf + 1)]
                    dve.tensor_tensor(hh, hh, psum[:, 2 * c + hf, :], ALU.add).then_inc(s_fd, 1)

            def embed_parts(layer):
                pT_, pp_ = ((pT, pp), (pT1, pp1))[layer]
                dve.wait_ge(s_pT, layer + 1)
                dve.wait_ge(s_ac, 4 + layer)
                dve.tensor_copy(pT_[:, 1, :], psum[:, 1, :]).then_inc(s_pTd, 1)
                for c in range(TC):
                    for hf in range(2):
                        dve.wait_ge(s_pp, 8 * layer + 2 * c + hf + 1)
                        dve.tensor_copy(pp_[:, c, 512 * hf:512 * (hf + 1)], psum[:, 2 * c + hf, :]).then_inc(s_ppd, 1)

            def embed_add(layer):
                pp_ = (pp, pp1)[layer]
                gates = pgate.rearrange("p k t -> p (k t)").rearrange("p (c n) -> p c n", c=4)
                for c in range(TC):
                    dve.wait_ge(s_drA, cumA[gidx[f"pg{layer}1"]] - 3 + c)
                    dve.wait_ge(s_ppd, 8 * (layer + 1))
                    chain.link(dve.tensor_tensor(pp_[:, c, :], pp_[:, c, :], gates[:, c, :], ALU.mult))
                    chain.settle()
                    dve.tensor_tensor(h[:, c, :], h[:, c, :], pp_[:, c, :], ALU.add).then_inc(s_ph, 1)

            embed_parts(0)
            norm(2)
            embed_add(0)

            tt = lambda o, a, b, op: chain.link(dve.tensor_tensor(o, a, b, op))
            ts = lambda o, a, s1, s2, op0, op1=ALU.bypass: chain.link(dve.tensor_scalar(o, a, s1, s2, op0, op1))
            dve.wait_ge(s_s5in, 16 * 10)
            dve.wait_ge(s_sin, 1)
            dve.tensor_scalar(r_x, r_are, r_ls, None, ALU.mult).then_inc(s_ang, 1)
            ts(r_th, r_aim, r_ls, None, ALU.mult)
            chain.settle()
            ts(r_k, r_th, 1.0 / TWO_PI, ROUND, ALU.mult, ALU.add)
            chain.settle()
            ts(r_k, r_k, ROUND, None, ALU.subtract)
            chain.settle()
            r = r_th
            for part in PI_PARTS:
                chain.link(dve.scalar_tensor_tensor(out=r_r, in0=r_k, scalar=-part, in1=r, op0=ALU.mult, op1=ALU.add))
                chain.settle()
                r = r_r
            dve.tensor_scalar(r_r, r_r, PI_MAX, -PI_MAX, ALU.min, ALU.max).then_inc(s_ang, 1)
            dve.wait_ge(s_sin, 3)
            tt(r_t0, r_c, r_c, ALU.mult)
            chain.settle()
            ts(r_t0, r_t0, -2.0, 1.0, ALU.mult, ALU.add)
            chain.settle()
            chain.link(dve.memset(PR[:, 0, :], 1.0))
            chain.link(dve.memset(PI[:, 0, :], 0.0))
            tt(PR[:, 1, :], r_x, r_t0, ALU.mult)
            tt(PI[:, 1, :], r_x, r_s, ALU.mult)
            tt(r_den, r_are, r_are, ALU.mult)
            tt(r_t1, r_aim, r_aim, ALU.mult)
            chain.settle()
            tt(r_den, r_den, r_t1, ALU.add)
            ts(r_nr, PR[:, 1, :], -1.0, None, ALU.add)
            chain.settle()
            chain.link(dve.reciprocal(r_den, r_den))
            for o, u1, w1, u2, w2, op in ((r_cr, r_nr, r_are, PI[:, 1, :], r_aim, ALU.add),
                                          (r_ci, PI[:, 1, :], r_are, r_nr, r_aim, ALU.subtract)):
                tt(r_t0, u1, w1, ALU.mult)
                tt(r_t1, u2, w2, ALU.mult)
                chain.settle()
                tt(o, r_t0, r_t1, op)
                chain.settle()
                tt(o, o, r_den, ALU.mult)
                chain.settle()

            def complex_product(zr, zi, ar, ai, br, bi, s0, s1):
                tt(s0, ar, br, ALU.mult)
                tt(s1, ai, bi, ALU.mult)
                chain.settle()
                tt(zr, s0, s1, ALU.subtract)
                chain.settle()
                tt(s0, ar, bi, ALU.mult)
                tt(s1, ai, br, ALU.mult)
                chain.settle()
                tt(zi, s0, s1, ALU.add)
                chain.settle()

            s0, s1 = WR, WI
            for n in (1, 2, 4):
                many = lambda ap: ap[:, n:n + 1, :].broadcast_to([P, n, NS])
                complex_product(PR[:, n + 1:2 * n + 1, :], PI[:, n + 1:2 * n + 1, :], PR[:, 1:n + 1, :], PI[:, 1:n + 1, :],
                                many(PR), many(PI), s0[:, 0:n, :], s1[:, 0:n, :])
            scr = rowt.rearrange("p k m q n -> p (k m q n)")
            sc = [scr[:, n * L5 * NS:(n + 1) * L5 * NS].rearrange("p (m n) -> p m n", m=L5) for n in range(2)]
            rows = lambda ap: ap.unsqueeze(1).broadcast_to([P, L5, NS])
            complex_product(WR, WI, PR[:, 0:L5, :], PI[:, 0:L5, :], rows(r_cr), rows(r_ci), sc[0], sc[1])
            for k, (src, sign0, sign1, m) in enumerate(((PR, 1, -1, M5), (PI, -1, -1, M5), (WR, 1, 1, L5), (WI, -1, 1, L5))):
                for q, sign in enumerate((sign0, sign1)):
                    ts(rowt[:, k, 0:m, q, :], src[:, 0:m, :], float(sign), None, ALU.mult)
            for q in range(2):
                ts(rowt[:, 4, 0, q, :], PR[:, L5, :], 1.0, None, ALU.mult)
                ts(rowt[:, 5, 0, q, :], PI[:, L5, :], 1.0, None, ALU.mult)
            chain.settle()
            dve.tensor_copy(r_t0, r_t1).then_inc(s_rowt, 1)
            for n in range(16):
                dve.wait_ge(s_rt, n + 1)
                d, b = n // 8, n % 8
                bank = psum[:, n % 4, :]
                dve.tensor_copy(Cst[:, d, 8 * b:8 * b + 8, :], bank[:, 0:P].rearrange("p (g c) -> p g c", g=8))
                dve.tensor_copy(Csw[:, d, 8 * b:8 * b + 8, :], bank[:, P:2 * P].rearrange("p (g c) -> p g c", g=8)).then_inc(s_cst, 1)
            for n, (k, m_) in enumerate(ROW_TABLES):
                dve.wait_ge(s_rt, 16 + n + 1)
                bank = psum[:, 4 + n % 4, 0:P]
                fwd, bwd = bank[:, 0:G5], bank[:, G5:2 * G5]
                if k < 4:
                    table = (PA, PB, WA, WB)[k]
                    mf, mb = (m_, L5 - m_) if k < 2 else (L5 - 1 - m_, m_)
                    dve.tensor_copy(table[:, 0, :, mf], fwd)
                    m = dve.tensor_copy(table[:, 1, :, mb], bwd)
                elif k == 4:
                    m = dve.tensor_copy(LR.rearrange("p d g -> p (d g)"), bank)
                else:
                    pair = bank.rearrange("p (d g) -> p d g", d=2)
                    dve.tensor_copy(LI[:, :, 0, :], pair)
                    m = dve.tensor_scalar(LI[:, :, 1, :], pair, -1.0, None, ALU.mult)
                m.then_inc(s_cst, 1)
            norm(3, False)
            dve.wait_ge(s_cst, 16 + len(ROW_TABLES))
            chain.settle()
            dve.tensor_copy(stat[:, 3, 1, 0:1], stat[:, 3, 2, 0:1]).then_inc(s_tabD, 1)
            for n in range(8):
                dve.wait_ge(s_ut, n + 1)
                dve.tensor_copy(U[:, 8 * n:8 * n + 8, :], psum[:, n, :].rearrange("p (g n) -> p g n", g=8)).then_inc(s_u, 1)
            dve.wait_ge(s_ut, 8)
            for hf in range(2):
                if hf:
                    dve.wait_ge(s_yy, 8)
                dve.memset(Z[0][:, 0:ZS], 0.0)
                dve.memset(Z[1][:, NC5 * ZS:], 0.0).then_inc(s_z0, 1)
                for b in range(8 * hf, 8 * hf + 8):
                    g0 = BG * b
                    if b % 8:
                        dve.wait_ge(s_bt, b)
                    for d in range(2):
                        chain.link(dve.tensor_tensor(BP[:, d, :, :].rearrange("p g (m c) -> p g m c", m=L5),
                                                     Bst[:, g0:g0 + BG, :].unsqueeze(2).broadcast_to([P, BG, L5, GC]),
                                                     WA[:, d, g0:g0 + BG, :].unsqueeze(3).broadcast_to([P, BG, L5, GC]), ALU.mult))
                    chain.settle()
                    dve.wait_ge(s_t2, 16 * hf + (b - 8 * hf) + 1)
                    dve.tensor_tensor(BP, BP, BQ, ALU.add).then_inc(s_bp, 1)
                    dve.wait_ge(s_bp, b + 1)
                    gl = g0 - HALF * hf
                    for d in range(2):
                        at = GC * (L5 - 1) * (1 - d)
                        dve.tensor_copy(BBk[:, d, gl:gl + BG, :], BP[:, d, :, at:at + GC])
                    dve.wait_ge(s_bt, b + 1)
                    if b % 8:
                        dve.wait_ge(s_v, b)
                    src = psum[:, 1, :].rearrange("p (g n) -> p g n", g=BG)
                    dve.tensor_copy(BigB[:, 1, :, NS:192], src)
                    dve.tensor_scalar(BigB[:, 1, :, 0:NS], src[:, :, NS:P], -1.0, None, ALU.mult).then_inc(s_bigD, 1)
                    dve.wait_ge(s_v, b + 1)
                    for d in range(2):
                        z = Z[d][:, (1 - d) * ZS:(1 - d) * ZS + NC5 * ZS].rearrange("p (n e g) -> p n e g", e=2, g=HALF)
                        for e in range(2):
                            m = dve.tensor_copy(z[:, :, e, gl:gl + BG],
                                                psum[:, 2 + d, e * 256:(e + 1) * 256].rearrange("p (g n) -> p n g", g=BG))
                    m.then_inc(s_vd, 1)
                dve.wait_ge(s_vd, 8 * (hf + 1))
                dve.wait_ge(s_z0, hf + 1)
                dve.wait_ge(s_bt, 8 * (hf + 1))
                scan(dve, chain, 0, hf, s_zf)
                for b in range(8 * hf, 8 * hf + 8):
                    g0 = BG * b
                    if b % 8:
                        dve.wait_ge(s_yy, b)
                    for d in range(2):
                        chain.link(dve.tensor_tensor(CP[:, d, :, :].rearrange("p g (m c) -> p g m c", m=M5),
                                                     Cst[:, d, g0:g0 + BG, :].unsqueeze(2).broadcast_to([P, BG, M5, GC]),
                                                     PA[:, d, g0:g0 + BG, :].unsqueeze(3).broadcast_to([P, BG, M5, GC]), ALU.mult))
                    chain.settle()
                    dve.wait_ge(s_t2, 16 * hf + 8 + (b - 8 * hf) + 1)
                    dve.tensor_tensor(CP, CP, CQ, ALU.add).then_inc(s_cp, 1)
                    dve.wait_ge(s_kk, b + 1)
                    if b % 8:
                        dve.wait_ge(s_kb, 16 * L5 * b)
                    kf = psum[0:GC, 4, :].rearrange("p (g j c) -> p g j c", g=BG, j=L5)
                    kb = psum[0:GC, 5, :].rearrange("p (g j c) -> p g j c", g=BG, j=L5)
                    KJ_ = KJ[0:GC, :, :, :]
                    chain.link(dve.tensor_copy(KJ_[:, :, L5 - 1:2 * L5 - 1, :], kf))
                    dve.tensor_copy(KJ_[:, :, 0:L5 - 1, :], kb[:, :, 0:L5 - 1, :])
                    chain.settle()
                    dve.tensor_tensor(KJ_[:, :, L5 - 1, :], KJ_[:, :, L5 - 1, :], kb[:, :, L5 - 1, :], ALU.add).then_inc(s_kj, 1)
            dve.wait_ge(s_yin, 16)
            dve.wait_ge(s_dw, 16)
            for c in range(TC):
                chain.link(dve.tensor_tensor(hn[:, c, :], hn[:, c, :], skip_w, ALU.mult))
                chain.settle()
                dve.tensor_tensor(ytok[:, c, :], ytok[:, c, :], hn[:, c, :], ALU.add).then_inc(s_gin, 1)
            for c in range(TC):
                dve.wait_ge(s_glt, 2 * c + 2)
                dve.tensor_copy(hnT[:, 4:8, c * P:(c + 1) * P],
                                psum[:, 2 * c + 1, :].rearrange("p (q t) -> p q t", q=4)).then_inc(s_glD, 1)
            for j in range(2):
                g = gidx[f"go{j}"]
                for b in range(4):
                    dve.wait_ge(s_grp, 4 * g + b + 1)
                    dve.wait_ge(s_drA, cumA[gidx[f"gg{j}"]] - 3 + b)
                    chain.link(dve.tensor_tensor(gtmp[:, b, :], gtmp[:, b, :], psum[:, 4 * (g % 2) + b, :], ALU.mult))
                    chain.settle()
                    hh = h[:, b, 512 * j:512 * (j + 1)]
                    dve.tensor_tensor(hh, hh, gtmp[:, b, :], ALU.add).then_inc(s_drD, 1)

            embed_parts(1)
            norm(4)
            dve.wait_ge(s_lg, 1)
            chain.link(dve.tensor_copy(lg.rearrange("p c e -> p (c e)"), psum[:, 0, 0:TC * NE]))
            chain.settle()
            for c in range(TC):
                chain.link(dve.max(out=top[:, c, :], in_=lg[:, c, :]))
            chain.settle()
            dve.tensor_tensor(gate[:, 0, :], top[:, :, 1], top[:, :, 0], ALU.subtract).then_inc(s_top, 1)
            for c in range(TC):
                chain.link(dve.max_index(out=topi[:, c, :], in_max=top[:, c, :], in_values=lg[:, c, :]))
            chain.link(dve.tensor_copy(rowi, psum[:, 1, 128:256]))
            for c in range(TC):
                chain.link(dve.tensor_scalar(parti[:, c:c + 1], psum[:, 1, 64:65], float(c * P), None, ALU.add))
            chain.settle()
            chain.link(dve.tensor_copy(topf, topi[:, :, 0:2]))
            chain.settle()
            for k in range(2):
                chain.link(dve.tensor_tensor(hot[:, k, :, :], rowi[:, 0:NE].unsqueeze(1).broadcast_to([P, TC, NE]),
                                             topf[:, :, k:k + 1].broadcast_to([P, TC, NE]), ALU.is_equal))
            chain.settle()
            dve.tensor_tensor(hot[:, 2, :, :], hot[:, 0, :, :], hot[:, 1, :, :], ALU.add).then_inc(s_hot, 1)
            dve.wait_ge(s_gexp, 1)
            chain.link(dve.tensor_scalar(gate[:, 1, :], gate[:, 2, :], 1.0, None, ALU.add))
            chain.settle()
            chain.link(dve.reciprocal(gate[:, 0, :], gate[:, 1, :]))
            chain.settle()
            chain.link(dve.tensor_tensor(gate[:, 1, :], gate[:, 0, :], gate[:, 2, :], ALU.mult))
            dve.wait_ge(s_rank, 1)
            chain.link(dve.tensor_copy(rk.rearrange("p c e -> p (c e)"), psum[:, 1, 0:TC * NE]))
            chain.link(dve.tensor_copy(cnt, psum[:, 1, 32:32 + NE]))
            chain.settle()

            def blocks_above(out_, in_, op):
                first = 0 if op == ALU.is_gt else 1
                chain.link(dve.tensor_scalar(out_, in_, float(first * P), None, op))
                chain.settle()
                for m_ in range(first + 1, TC):
                    chain.link(dve.scalar_tensor_tensor(out=out_, in0=in_, scalar=float(m_ * P), in1=out_, op0=op, op1=ALU.add))
                    chain.settle()

            blocks_above(nblk, cnt, ALU.is_gt)
            blocks_above(rq, rk, ALU.is_ge)
            a, b = nblk, ends[:, 0, :]
            for step in (1, 2, 4):
                chain.link(dve.tensor_copy(b[:, 0:step], a[:, 0:step]))
                chain.link(dve.tensor_tensor(b[:, step:NE], a[:, step:NE], a[:, 0:NE - step], ALU.add))
                chain.settle()
                a, b = b, ends[:, 1 if step == 1 else 0, :]
            end = a
            chain.link(dve.scalar_tensor_tensor(out=rk, in0=rq, scalar=-float(P), in1=rk, op0=ALU.mult, op1=ALU.add))
            chain.link(dve.tensor_tensor(nblk, end, nblk, ALU.subtract))
            chain.settle()
            chain.link(dve.tensor_tensor(rq, rq, nblk.unsqueeze(1).broadcast_to([P, TC, NE]), ALU.add))
            chain.settle()
            for src, dst in ((rq, bsel), (rk, rsel)):
                for k in range(2):
                    chain.link(dve.tensor_tensor(rtmp[:, k, :, :], hot[:, k, :, :], src, ALU.mult))
                chain.settle()
                chain.link(dve.tensor_reduce(out=dst, in_=rtmp, axis=AX_X, op=ALU.add))
                chain.settle()
            for k in range(2):
                for c in range(TC):
                    chain.link(dve.tensor_scalar(moe_hotR[:, k, c, :], rowi, rsel[:, k, c:c + 1], None, ALU.is_equal))
                    m = dve.tensor_scalar(moe_hotB[:, k, c, :], rowi[:, 0:MAXB + 1], bsel[:, k, c:c + 1], parti[:, c:c + 1],
                                          ALU.is_equal, ALU.mult)
            m.then_inc(s_slot, 1)
            chain.link(dve.scalar_tensor_tensor(out=destf, in0=bsel, scalar=float(P), in1=rsel, op0=ALU.mult, op1=ALU.add))
            chain.settle()
            dve.tensor_copy(desti, destf).then_inc(s_myd, 1)
            chain.link(dve.tensor_tensor(ecmp, rowi[:, 0:MAXB + 1].unsqueeze(2).broadcast_to([P, MAXB + 1, NE]),
                                         end.unsqueeze(1).broadcast_to([P, MAXB + 1, NE]), ALU.is_ge))
            chain.settle()
            chain.link(dve.tensor_reduce(out=ef, in_=ecmp, axis=AX_X, op=ALU.add))
            chain.settle()
            chain.link(dve.tensor_scalar(ef, ef, float(NE - 1), None, ALU.min))
            chain.settle()
            chain.link(dve.tensor_copy(plan[:, 0:MAXB], ef[:, 0:MAXB]))
            chain.link(dve.tensor_copy(plan[:, MAXB:MAXB + 1], end[:, NE - 1:NE]))
            chain.settle()
            dve.wait_ge(s_tok, 1)
            dve.tensor_copy(slot_tok, psum[:, 2, 0:MAXB + 1]).then_inc(s_plan, 1)
            dve.wait_ge(s_plan, 1)
            blocks_dve = dve.value_load(plan[0:1, MAXB:MAXB + 1], min_val=2 * TC, max_val=MAXB)
            with dve.Fori(0, MAXB) as i:
                with dve.If(i < blocks_dve):
                    dve.wait_ge(s_xtp, 2 * i + 2)
                    dve.tensor_copy(xbT[:, 4:8, :], psum[:, 5, :].rearrange("p (q t) -> p q t", q=4)).then_inc(s_xtD, 1)
                    for j in range(EJ):
                        dve.wait_ge(s_mt, tiles_done(i, gu_at(j) + 4))
                        dve.wait_ge(s_msl, EJ * i + j + 1)
                        dve.tensor_tensor(ehid[:, j % 2, :], esil[:, j % 2, :], psum[:, 2 + j % 2, :], ALU.mult).then_inc(s_mh, 1)
                    dve.wait_ge(s_mt, tiles_done(i, PER))
                    dve.wait_ge(s_mys, 16 * i + 32)
                    dve.tensor_copy(yblk, psum[:, 6:8, :].rearrange("p b n -> p (b n)")).then_inc(s_myd, 1)
            for c in range(TC):
                dve.wait_ge(s_yg[c], 32)
                for k in range(2):
                    m = dve.scalar_tensor_tensor(out=h[:, c, :], in0=yg[k][:, c, :], scalar=gate[:, k, c:c + 1],
                                                 in1=h[:, c, :], op0=ALU.mult, op1=ALU.add)
                    if k:
                        m.then_inc(s_mc, 1)
                    else:
                        chain.link(m)
                        chain.settle()
            norm(5)
            embed_add(1)
            norm(6, False)

    return None


def kernel(**inputs):
    import numpy as _np
    import concourse.bacc as _bacc
    from concourse import mybir as _mybir
    from concourse.bass_utils import run_bass_kernel_spmd as _run

    nc = _bacc.Bacc("TRN2", target_bir_lowering=False, num_devices=1)
    arrays, args = {}, {}
    for name, v in inputs.items():
        a = _np.ascontiguousarray(v)
        arrays[f"in_{name}_dram"] = a
        args[name] = nc.dram_tensor(f"in_{name}_dram", a.shape, _mybir.dt.from_np(a.dtype), kind="ExternalInput").ap()
    out = nc.dram_tensor("out_0_dram", inputs["x"].shape, _mybir.dt.float32, kind="ExternalOutput").ap()
    build_program(nc, args, out)
    r = _run(nc, [arrays], core_ids=[0])
    return r.results[0]["out_0_dram"]
```

```python
from contextlib import ExitStack

import concourse.bass as bass
from concourse import mybir

F32 = mybir.dt.float32
I32 = mybir.dt.int32
U32 = mybir.dt.uint32
U8 = mybir.dt.uint8
F32R = mybir.dt.float32r
ALU = mybir.AluOpType
ACT = mybir.ActivationFunctionType
AX_X = mybir.AxisListType.X

P = 128
RING = 6
HIGH_BITS = -4096
TILE = 2048


TWO_PI = 6.283185307179586
PI_PARTS = (6.28125, 0.0019350051879882812, 3.0199159795074593e-07)
PI_MAX = 3.1415925
ROUND = 12582912.0


class Arena:

    def __init__(self, tensor, start, end):
        self.tensor, self.at, self.end = tensor, start, end

    def take(self, n):
        a = self.at
        self.at += n
        assert self.at <= self.end, (self.at, self.end)
        return self.tensor[:, a:a + n]


class Chain:

    def __init__(self, eng, sem):
        self.eng, self.sem, self.n = eng, sem, 0

    def link(self, ins):
        self.n += 1
        ins.then_inc(self.sem, 1)

    def settle(self):
        self.eng.wait_ge(self.sem, self.n)


def build_program(nc, I, out, dbg=None):
    x, p_in = I["x"], I["p"]
    _, T, D = x.shape
    TC = T // P
    KB = D // P
    EPS = 1e-6
    LB_FLOOR = 1e-30
    LN_SPLIT = 2.0 ** -60
    HG = I["hg_norm_w"].shape[1]
    HEADS = HG // P
    INNER = I["m2_norm_w"].shape[1]
    MH = I["m2_d"].shape[1]
    MP = INNER // MH
    GROUPS = 2
    HPG = MH // GROUPS
    CONV = I["m2_conv_w"].shape[1]
    XBC = I["m2_conv_w"].shape[2]
    CB = XBC // P
    W_IN = I["ev_w_in"].shape[2]
    FF = I["ffn_w_down"].shape[1]
    FJ = FF // 512
    LEVELS = 9
    assert T == 1 << LEVELS and KB == 8 and TC == 4 and CB == 8 and HEADS == 4

    w_in = I["ev_w_in"][0]
    w_out = I["ev_w_out"][0]

    ctx = ExitStack()
    with ctx:
        def sem(name):
            return ctx.enter_context(nc.semaphore(name))

        words = nc.sbuf_bytes_remaining() // 4 - 64 if callable(nc.sbuf_bytes_remaining) else nc.sbuf_bytes_remaining // 4 - 64
        kept_words = RING * TILE + TC * D + 6 * P + 14 * P // 4 + 68 + P + 2 * D + 7 * 12 + 1 + 32 + 56 + 1024
        kept_mem = ctx.enter_context(nc.sbuf_tensor("kept", [P, kept_words], F32))
        words -= kept_words
        r_words = 2 * KB * T + 5 * TILE
        with nc.sbuf_tensor("stages_r", [P, r_words], F32R) as sbuf_r:
            pass
        sbuf = ctx.enter_context(nc.sbuf_tensor("stages", [P, words], F32))
        psum = ctx.enter_context(nc.psum_tensor("psum", [P, 8, 512], F32))
        kept = Arena(kept_mem, 0, kept_words)
        ring = kept.take(RING * TILE).rearrange("p (s n) -> p s n", s=RING)
        h = kept.take(TC * D).rearrange("p (c n) -> p c n", c=TC)
        ident, ones, LE, GE, GT, LT = [kept.take(P) for _ in range(6)]
        masks = kept.take(14 * P // 4).bitcast(U8).rearrange("p (m t) -> p m t", m=14)
        parT = kept.take(68)
        parR = kept.take(P)
        nw = kept.take(2 * D).rearrange("p (b n) -> p b n", b=2)
        stat = kept.take(7 * 4 * 3).rearrange("p (k a c) -> p k a c", k=7, a=3)
        eps = kept.take(1)
        hgc = kept.take(32).rearrange("p (a k) -> p a k", k=4)
        tokp = kept.take(56)
        dtb, alog, dskip, aneg = tokp[:, 0:16], tokp[:, 16:32], tokp[:, 32:40], tokp[:, 40:56]
        ehid = kept.take(2 * 512).rearrange("p (b f t) -> p b f t", b=2, f=2)
        shared = Arena(sbuf, 0, words)
        hnT = shared.take(KB * T).rearrange("p (k t) -> p k t", k=KB)
        mixT = shared.take(KB * T).rearrange("p (k t) -> p k t", k=KB)
        base = shared.at
        pe_words = words

        c_q, c_ff, c_fb, c_v, c_g, c_z = [HG * n for n in range(6)]
        c_xs = c_z + INNER
        c_bc = c_xs + INNER
        c_dt = c_bc + XBC - INNER

        stream = []
        release, n_used = [], [0]

        def add_tiles(w, col, width):
            for g in range(2):
                stream.append((w[g * 512:(g + 1) * 512, col:col + width].rearrange("(k p) n -> p k n", p=P), width))

        groups = []

        def add_group(name, w, col, width, layout, drain):
            if w is None:
                groups.append((name, layout, width, drain, None))
                return
            add_tiles(w, col, width)
            groups.append((name, layout, width, drain, len(stream) - 2))
            release.append(("used", n_used[0] + 1))
            release.append(("group", 4 * len(groups)))
            n_used[0] += 1

        add_group("q", w_in, c_q, 512, "T", "A")
        add_group("ff", w_in, c_ff, 512, "T", "A")
        add_group("fb", w_in, c_fb, 512, "T", "A")
        add_group("v", w_in, c_v, 512, "tok", "D")
        add_group("g", w_in, c_g, 512, "T", "A")
        add_group("z", w_in, c_z, 512, "tok", "A")
        add_group("xs", w_in, c_xs, 512, "T", "D")
        add_group("bc", w_in, c_bc, 512, "T", "D")
        add_group("dt", w_in, c_dt, 16, "tok", "D")
        add_group("o0", w_out, 0, 512, "tok", "D")
        add_group("o1", w_out, 512, 512, "tok", "D")
        gu, down = I["ffn_w_gu"][0], I["ffn_w_down"][0]
        for j in range(FJ):
            add_group(f"fg{j}", gu, 512 * j, 512, "T", "A")
            add_group(f"fu{j}", gu, FF + 512 * j, 512, "T", "D")
        down_tile0 = len(stream)
        for j in range(FJ):
            for half in range(2):
                stream.append((down[512 * j:512 * (j + 1), 512 * half:512 * (half + 1)].rearrange("(k p) n -> p k n", p=P), 512))
                n_used[0] += j < FJ - 1
                release.append(("down", 4 * half + 4) if j == FJ - 1 else ("used", n_used[0]))
        ple_tile = len(stream)
        stream.append((I["ple_proj"][0].rearrange("(k p) n -> p k n", p=P), -1))
        release.append(("proj", 8))
        for j in range(2):
            add_group(f"pg0{j}", I["ple_gate"][0], 512 * j, 512, "tok", "A")
        glu = I["s5_glu_w"][0]
        for j in range(2):
            add_group(f"gg{j}", glu, D + 512 * j, 512, "tok", "A")
            add_group(f"go{j}", glu, 512 * j, 512, "tok", "D")
        for j in range(2):
            add_group(f"pg1{j}", None, 512 * j, 512, "tok", "A")
        gidx = {g[0]: n for n, g in enumerate(groups)}
        cumA, cumD = [], []
        for g in groups:
            cumA.append((cumA[-1] if cumA else 0) + (4 if g[3] == "A" else 0))
            cumD.append((cumD[-1] if cumD else 0) + (4 if g[3] == "D" else 0))

        s_ring = [sem(f"ring_full{i}") for i in range(RING)]
        s_used = sem("ring_tile_used")
        s_x = sem("x_loaded")
        s_par = sem("params_loaded")
        s_tokp = sem("token_params_loaded")
        s_nw = [sem(f"norm_weight_loaded{i}") for i in range(2)]
        s_const = sem("constants_built")
        s_parT = sem("params_transposed")
        s_parTd = sem("params_in_sbuf")
        s_lb = sem("hg_bounds_ready")
        s_lbc = sem("hg_bounds_exp")
        s_sq = sem("square_sums")
        s_rms = sem("rms_ready")
        s_hn = sem("hn_ready")
        s_tp = sem("hn_transposed")
        s_hA = sem("hnT_by_act")
        s_hD = sem("hnT_by_dve")
        s_grp = sem("dense_bank_done")
        s_drA = sem("dense_bank_drained_act")
        s_drD = sem("dense_bank_drained_dve")
        s_vc = sem("dve_chain")
        s_ac = sem("act_chain")
        s_pc = sem("pool_chain")
        s_lf = sem("log_forget_ready")
        s_k = sem("key_ready")
        s_lnin = sem("ln_inputs_ready")
        s_lnout = sem("ln_outputs_ready")
        s_rz = sem("suffix_zeroed")
        s_exp = sem("decay_exp_ready")
        s_X = sem("scaled_qk_ready")
        s_upd = sem("prefix_updated")
        s_gram = sem("gram_done")
        s_gdr = sem("gram_drained")
        s_ks = sem("key_sum_ready")
        s_dg = sem("diag_gram_done")
        s_sd = sem("diag_scores_ready")
        s_o = sem("hg_out_done")
        s_osq = sem("hg_out_squared")
        s_oss = sem("hg_square_sum_done")
        s_orms = sem("hg_rms_ready")
        s_mix = sem("hg_mix_ready")
        s_diag = sem("conv_diag_ready")
        s_pad = sem("conv_pad_zeroed")
        s_conv = sem("conv_done")
        s_cact = sem("conv_activated")
        s_sp = sem("softplus_parts")
        s_dt = sem("dt_ready")
        s_xt = sem("xs_transposed")
        s_xtd = sem("xs_in_sbuf")
        s_cum = sem("cumsums_done")
        s_ex = sem("cumsum_exp_ready")
        s_te = sem("to_end_ready")
        s_xe = sem("x_to_end_ready")
        s_st = sem("chunk_state_done")
        s_H = sem("state_ready")
        s_cb = sem("cb_done")
        s_cbm = sem("cb_masked")
        s_dtau = sem("dta_masked")
        s_seg = sem("segment_sums_done")
        s_E = sem("segment_exp_ready")
        s_w = sem("ssd_weights_ready")
        s_xdt = sem("x_dt_ready")
        s_y = sem("ssd_y_done")
        s_yd = sem("ssd_y_drained")
        s_yz = sem("ssd_gated")
        s_ysq = sem("ssd_square_sums")
        s_yrms = sem("ssd_rms")
        s_yn = sem("ssd_normed")
        s_yt = sem("ssd_transposed")
        s_ym = sem("ssd_mix_ready")
        s_ffd = sem("ffn_down_done")
        s_fd = sem("ffn_down_drained")
        s_ph = sem("ple_added")
        s_p = sem("ple_input_loaded")
        s_pT = sem("ple_input_transposed")
        s_pTd = sem("ple_input_in_sbuf")
        s_pp = sem("ple_proj_done")
        s_ppd = sem("ple_proj_drained")
        s_out = sem("out_stored")

        s_rtr = sem("router_loaded")
        s_pw = sem("ple_proj_weights_loaded")
        s_gw = sem("ple_gate_weights_loaded")
        s_lg = sem("router_logits_done")
        s_top = sem("router_logit_gap_ready")
        s_gexp = sem("router_gap_exp")
        s_hot = sem("expert_one_hot_ready")
        s_rank = sem("expert_ranks_done")
        s_slot = sem("slot_one_hot_ready")
        s_tok = sem("slot_tokens_done")
        s_plan = sem("block_plan_ready")
        s_hnm = sem("moe_rows_in_dram")
        s_ix = sem("slot_tokens_copied")
        s_xg = sem("block_rows_loaded")
        s_xtp = sem("block_rows_transposed")
        s_xtA = sem("block_xT_by_act")
        s_xtD = sem("block_xT_by_dve")
        s_mt = sem("moe_tile_used")
        s_msl = sem("expert_silu_ready")
        s_mh = sem("expert_hidden_ready")
        s_wh = sem("weights_high_part")
        s_ws = sem("weights_split")
        s_myA = sem("first_block_y_in_sbuf")
        s_myd = sem("block_y_in_sbuf")
        s_mys = sem("block_y_in_dram")
        s_yg = [sem(f"token_y_gathered{c}") for c in range(TC)]
        s_mc = sem("moe_combined")

        s_s5in = sem("s5_params_loaded")
        s_sin = sem("s5_sin_ready")
        s_ang = sem("s5_angle_ready")
        s_rowt = sem("s5_row_tables_ready")
        s_rt = sem("s5_rows_transposed")
        s_tabD = sem("s5_tables_by_dve")
        s_hnd = sem("hn_in_dram")
        s_un = sem("s5_inputs_by_chunk")
        s_up = sem("s5_inputs_by_group")
        s_ut = sem("s5_inputs_transposed")
        s_u = sem("s5_inputs_ready")
        s_t2 = sem("s5_pool_product")
        s_bp = sem("s5_b_powers")
        s_bt = sem("s5_b_transposed")
        s_bigA = sem("s5_b_by_act")
        s_bigD = sem("s5_b_by_dve")
        s_v = sem("s5_chunk_inputs_done")
        s_vd = sem("s5_chunk_inputs_ready")
        s_zf = sem("s5_forward_states")
        s_zb = sem("s5_backward_states")
        s_cp = sem("s5_c_powers")
        s_kk = sem("s5_kernels_done")
        s_kj = sem("s5_kernels_in_sbuf")
        s_kb = sem("s5_toeplitz_built")
        s_yy = sem("s5_y_done")
        s_yb = sem("s5_y_in_sbuf")
        s_ydr = sem("s5_y_in_dram")
        s_yin = sem("s5_y_loaded")
        s_dw = sem("s5_skip_loaded")
        s_gin = sem("gelu_input_ready")
        s_gl = sem("gelu_ready")
        s_glt = sem("gelu_transposed")
        s_glA = sem("gelu_by_act")
        s_glD = sem("gelu_by_dve")
        s_z0 = sem("s5_zero_states")
        s_cst = sem("s5_c_transposed")

        hga = Arena(sbuf, base, pe_words)
        v4 = "p (a t) -> p a t"
        qT = hga.take(4 * T).rearrange(v4, a=4)
        kT = [hga.take(4 * T).rearrange(v4, a=4) for _ in range(2)]
        vtok = hga.take(4 * 512).rearrange(v4, a=4)
        gT = hga.take(4 * T).rearrange(v4, a=4)
        lf = [hga.take(4 * T).rearrange(v4, a=4) for _ in range(2)]
        Rs = [[hga.take(T) for _ in range(2)] for _ in range(2)]
        Xb = [hga.take(T) for _ in range(4)]
        S_flat = hga.take(5 * T)
        S_main = S_flat[:, 0:4 * T].rearrange("p (c t) -> p c t", c=4)
        S_diag = S_flat.rearrange("p (c x) -> p c x", x=T + P)[:, :, 0:P]
        ksum = hga.take(T)
        osq = hga.take(T)
        orms = hga.take(T)
        hn_at = pe_words - 4 * D
        hn = sbuf[:, hn_at:hn_at + 4 * D].rearrange("p (c n) -> p c n", c=4)
        lnb = hn

        mtmp = hnT.rearrange("p k t -> p (k t)")[:, 0:14 * P].rearrange("p (m t) -> p m t", m=14)

        ssa = Arena(sbuf, base, pe_words)
        zs = ssa.take(4 * 512).rearrange(v4, a=4)
        dtr = ssa.take(64).rearrange("p (d c k) -> p d c k", d=2, c=4)
        dts = ssa.take(64).rearrange("p (d c k) -> p d c k", d=2, c=4)
        dta = ssa.take(64).rearrange("p (d c k) -> p d c k", d=2, c=4)
        dtt = ssa.take(64).rearrange("p (d c k) -> p d c k", d=2, c=4)
        toend = ssa.take(64).rearrange("p (d c k) -> p d c k", d=2, c=4)
        ex = ssa.take(192)
        xc = ssa.take(8 * T).rearrange(v4, a=8)
        xst = ssa.take(4 * 512).rearrange(v4, a=4)
        btok = ssa.take(4 * 256).rearrange(v4, a=4)
        Hst = [ssa.take(3 * 512).rearrange(v4, a=3) for _ in range(2)]
        yst_flat = ssa.take(4 * 512)
        yst = yst_flat.rearrange(v4, a=4)
        ytmp = ssa.take(512)
        ssy = ssa.take(24).rearrange("p (a k) -> p a k", a=3)
        cbm = ssa.take(512).rearrange("p (d g t) -> p d g t", d=2, g=2)
        xdt = ssa.take(1024).rearrange("p (d n) -> p d n", d=2)
        xe = ssa.take(1024).rearrange("p (d n) -> p d n", d=2)
        shared = ssa.at
        raw = ssa.take(8 * (T + 4)).rearrange(v4, a=8)
        diag = yst_flat[:, 0:2 * CONV * P].rearrange("p (b k n) -> p b k n", b=2, k=CONV)
        ssa.at = shared
        Ew = ssa.take(2048).rearrange("p (d n t) -> p d n t", d=2, t=P)
        dtaU = ssa.take(2048).rearrange("p (d n t) -> p d n t", d=2, t=P)

        ffa = Arena(sbuf, base, hn_at)
        hT = ffa.take(FJ * 4 * T).rearrange("p (f t) -> p f t", t=T)
        silT = mixT[:, 0:4, :]
        pla = Arena(sbuf, base, hn_at)
        ptok = pla.take(4 * 256).rearrange(v4, a=4)
        pT = pla.take(2 * T).rearrange(v4, a=2)
        pp = pla.take(4 * D).rearrange(v4, a=4)
        pgate = mixT

        NE = I["moe_router"].shape[2]
        MAXB = TC * 2 + NE - 1
        MAXU = NE + (2 * T - NE) // (2 * P)
        EF = 256
        STEPS = I["moe_w_down"].shape[2] // EF
        PER = 3 * STEPS
        WSLOTS = 3
        assert PER % RING == 0 and PER % WSLOTS == 0 and NE == 8
        N0 = len(stream)
        moa = Arena(sbuf, base, hn_at)
        gw = kept_mem[:, 0:8 * D].rearrange("p (j k n) -> p j k n", j=2, k=8)

        def both(n):
            a = moa.at
            moa.take(n)
            assert a + n <= r_words
            return sbuf[:, a:a + n], sbuf_r[:, a:a + n]

        xbT, xbH = [ap.rearrange("p (k t) -> p k t", k=8) for ap in both(16 * P)]
        xbL = both(16 * P)[1].rearrange("p (k t) -> p k t", k=8)
        ehH, ehL = [both(2 * 512)[1].rearrange("p (b f t) -> p b f t", b=2, f=2) for _ in range(2)]
        more = both(2 * TILE)[1]
        w_slots = [sbuf_r[:, TILE * n:TILE * (n + 1)] for n in range(4)] + [more[:, TILE * n:TILE * (n + 1)] for n in range(2)]
        w_high, w_low = w_slots[0:3], w_slots[3:6]
        esil = moa.take(2 * 512).rearrange("p (b f t) -> p b f t", b=2, f=2)
        pp1 = moa.take(4 * D).rearrange(v4, a=4)
        xblk = sbuf[:, hn_at:hn_at + 2 * D].rearrange("p (a n) -> p a n", a=2)
        yblk = sbuf[:, hn_at + 2 * D:hn_at + 4 * D].rearrange("p (a n) -> p a n", a=2)
        router = moa.take(8 * NE).rearrange("p (k e) -> p k e", k=8)
        lg = moa.take(TC * NE).rearrange("p (c e) -> p c e", c=TC)
        top = moa.take(TC * 8).rearrange("p (c e) -> p c e", c=TC)
        topi = moa.take(TC * 8).bitcast(U32).rearrange("p (c e) -> p c e", c=TC)
        topf = moa.take(TC * 2).rearrange("p (c k) -> p c k", c=TC)
        gate = moa.take(TC * 3).rearrange("p (a c) -> p a c", a=3)
        hot = moa.take(TC * 3 * NE).rearrange("p (k c e) -> p k c e", k=3, c=TC)
        rowi = moa.take(P)
        parti = moa.take(TC)
        rk = moa.take(TC * NE).rearrange("p (c e) -> p c e", c=TC)
        rq = moa.take(TC * NE).rearrange("p (c e) -> p c e", c=TC)
        rtmp = moa.take(2 * TC * NE).rearrange("p (k c e) -> p k c e", k=2, c=TC)
        cnt = moa.take(NE)
        nblk = moa.take(NE)
        ends = moa.take(2 * NE).rearrange("p (a e) -> p a e", a=2)
        bsel = moa.take(2 * TC).rearrange("p (k c) -> p k c", k=2)
        rsel = moa.take(2 * TC).rearrange("p (k c) -> p k c", k=2)
        destf = moa.take(2 * TC).rearrange("p (k c) -> p k c", k=2)
        desti = moa.take(2 * TC).bitcast(I32).rearrange("p (k c) -> p k c", k=2)
        ecmp = moa.take((MAXB + 1) * NE).rearrange("p (b e) -> p b e", e=NE)
        ef = moa.take(MAXB + 1)
        eown = moa.take((MAXU + 1) * NE).rearrange("p (u e) -> p u e", e=NE)
        SLOTC = MAXB + 2
        plan = moa.take(3 * (MAXU + 1) + 1).bitcast(I32)
        plan_e, plan_b, plan_n = [plan[:, n * (MAXU + 1):(n + 1) * (MAXU + 1)] for n in range(3)]
        plan_u = plan[:, 3 * (MAXU + 1):3 * (MAXU + 1) + 1]
        uend = moa.take(2 * NE).rearrange("p (a e) -> p a e", a=2)
        nun = moa.take(NE)
        usel = moa.take(NE)
        ublk = moa.take(3 * (MAXU + 1)).rearrange("p (a u) -> p a u", a=3)
        slot_tok = moa.take(SLOTC).bitcast(I32)
        slot_now = moa.take(2).bitcast(I32)
        slot_junk = moa.take(8)
        spare = moa.take(2)
        moe_hotR = mixT.rearrange("p k t -> p (k t)")[:, 0:8 * P].rearrange("p (k c t) -> p k c t", k=2, c=TC)
        moe_hotB = mixT.rearrange("p k t -> p (k t)")[:, 8 * P:8 * P + 8 * SLOTC].rearrange("p (k c b) -> p k c b", k=2, c=TC)
        ptok1 = mixT.rearrange("p k t -> p (k t)")[:, 0:1024].rearrange(v4, a=4)
        pT1 = mixT.rearrange("p k t -> p (k t)")[:, 1024:2048].rearrange(v4, a=2)
        pw1 = mixT.rearrange("p k t -> p (k t)")[:, 2048:4096].rearrange("p (k n) -> p k n", k=2)
        yg = [r_.rearrange("p k t -> p (k t)").rearrange("p (c n) -> p c n", c=TC) for r_ in (hnT, mixT)]
        y_rows = nc.dram_tensor("expert_rows", ((MAXB + 1) * P, D), F32, kind="Internal").ap()
        w_egu, w_edn = I["moe_w_gu"][0], I["moe_w_down"][0]
        moe_dram = nc.dram_tensor("moe_rows_by_token", (T, D), F32, kind="Internal").ap()

        def gate_at(s_):
            return max(3 * s_ - 1, 0)

        def down_at(s_):
            return min(3 * s_ + 4, PER - 1)

        def tiles_done(u, n):
            return u * PER + (RING + n)

        def tile_wait(eng, u, n):
            slot = (N0 + n) % RING
            eng.wait_ge(s_ring[slot], u * (16 * PER // RING) + 16 * ((N0 + n) // RING + 1))

        def unit_tile(n):
            return ring[:, (N0 + n) % RING, :]

        def moe_sources(e):
            def up(col):
                return w_egu[bass.ds(e, 1), :, col:col + EF].rearrange("a (k p) n -> p (a k) n", p=P)

            def dn(s_):
                return w_edn[bass.ds(e, 1), EF * s_:EF * (s_ + 1), :].rearrange("a (k p) n -> p (a k) n", p=P)

            tiles = []
            for s_ in range(STEPS):
                tiles += [up(EF * s_), up(EF * (STEPS + s_))]
                if s_:
                    tiles.append(dn(s_ - 1))
            return tiles + [dn(STEPS - 1)]

        block = ctx.enter_context(nc.Block())
        norm_w = [I["norm_mix"][0], I["norm_ffn"][0], I["norm_ple"][0], I["norm_mix"][1], I["norm_ffn"][1],
                  I["norm_ple"][1], I["final_norm"]]

        def row(v):
            return v.rearrange("(a n) -> a n", a=1)

        def half(ap, n, side):
            return ap.rearrange("p (b two n) -> p b two n", two=2, n=n)[:, :, side, :]

        G5, NS, GC = I["s5_b_re"].shape[1:]
        L5 = 8
        NC5 = T // L5
        HALF = G5 // 2
        BG = 4
        BATCHES = G5 // BG
        M5 = L5 + 1
        s5a = Arena(sbuf, base, pe_words)
        WA, WB = [s5a.take(2 * G5 * L5).rearrange("p (d g m) -> p d g m", d=2, g=G5) for _ in range(2)]
        PA, PB = [s5a.take(2 * G5 * M5).rearrange("p (d g m) -> p d g m", d=2, g=G5) for _ in range(2)]
        s5k = Arena(kept_mem, kept.at - 1024, kept.at)
        Yb = s5k.take(L5 * BG * GC).rearrange("p (t n) -> p t n", t=L5)
        LR = s5k.take(2 * G5).rearrange("p (d g) -> p d g", d=2)
        LI = s5k.take(4 * G5).rearrange("p (d e g) -> p d e g", d=2, e=2)
        Bst, Bsw = [s5a.take(G5 * GC).rearrange("p (g c) -> p g c", g=G5) for _ in range(2)]
        s5_work = s5a.at
        ZS = 2 * HALF
        z_at = [s5a.at, s5a.at + (NC5 + 1) * ZS]
        Z = [s5a.take((NC5 + 1) * ZS) for _ in range(2)]
        BBk = s5a.take(HALF * 2 * GC).rearrange("p (d g c) -> p d g c", d=2, g=HALF)
        W1, W2 = [s5a.take(2 * BG * M5 * GC) for _ in range(2)]
        BP = W1[:, 0:2 * BG * L5 * GC].rearrange("p (d g m c) -> p d g (m c)", d=2, g=BG, m=L5)
        BQ = W2[:, 0:2 * BG * L5 * GC].rearrange("p (d g m c) -> p d g (m c)", d=2, g=BG, m=L5)
        CP = W1.rearrange("p (d g m c) -> p d g (m c)", d=2, g=BG, m=M5)
        CQ = W2.rearrange("p (d g m c) -> p d g (m c)", d=2, g=BG, m=M5)
        big_at = s5a.at
        BigB = s5a.take(2 * BG * 192).rearrange("p (d g n) -> p d g n", d=2, g=BG)
        s5a.at = big_at
        KJ = s5a.take(BG * 15 * GC).rearrange("p (g j c) -> p g j c", g=BG, j=15)
        Kbig = s5a.take(BG * P).rearrange("p (g n) -> p g n", g=BG)
        s5a.at = max(s5a.at, big_at + 2 * BG * 192)
        assert s5a.at <= hn_at
        UN = sbuf[0:NC5, s5_work:s5_work + L5 * D].rearrange("p (t n) -> p t n", t=L5)
        UP = (W1, W2)
        U = hnT.rearrange("p k t -> p (k t)").rearrange("p (g n) -> p g n", g=G5)
        Cst, Csw = [mixT.rearrange("p k t -> p (k t)")[:, 2048 * n:2048 * (n + 1)].rearrange("p (d g c) -> p d g c", d=2, g=G5)
                    for n in range(2)]
        rwa = Arena(sbuf, s5_work, hn_at + 1024)
        srow = lambda n: rwa.take(n)
        r_are, r_aim, r_x, r_th, r_k, r_r, r_s, r_c, r_den, r_t0, r_t1, r_nr, r_cr, r_ci = [srow(NS) for _ in range(14)]
        r_ls = srow(1)
        PR, PI = [rwa.take(M5 * NS).rearrange("p (m n) -> p m n", m=M5) for _ in range(2)]
        WR, WI = [rwa.take(L5 * NS).rearrange("p (m n) -> p m n", m=L5) for _ in range(2)]
        rowt = rwa.take(5 * 2 * NS * M5).rearrange("p (k m q n) -> p k m q n", k=5, m=M5, q=2)
        C3 = rwa.take(16 * 3 * NS).rearrange(
            "p (b q n) -> p b q n", b=16, q=3)
        ytok = sbuf[:, base:base + 4 * D].rearrange("p (c n) -> p c n", c=4)
        skip_w = sbuf[:, base + 4 * D:base + 5 * D]
        gtmp = sbuf[:, base + 5 * D:base + 5 * D + 2048].rearrange(v4, a=4)
        hn_dram = nc.dram_tensor("hn_by_token", (T, D), F32, kind="Internal").ap()
        y_dram = nc.dram_tensor("s5_y_by_token", (T, D), F32, kind="Internal").ap()


        lnb4 = lnb.rearrange("p c n -> p (c n)")[:, 0:4 * T].rearrange(v4, a=4)
        h_ready = {
            0: lambda e, c: e.wait_ge(s_x, 16),
            1: lambda e, c: e.wait_ge(s_drD, cumD[gidx["o1"]] - 3 + c),
            2: lambda e, c: e.wait_ge(s_fd, 2 * (c + 1)),
            3: lambda e, c: e.wait_ge(s_ph, c + 1),
            4: lambda e, c: e.wait_ge(s_drD, cumD[gidx["go1"]] - 3 + c),
            5: lambda e, c: e.wait_ge(s_mc, c + 1),
            6: lambda e, c: e.wait_ge(s_ph, 4 + c + 1),
        }

        def ssd_squares(act, c):
            act.wait_ge(s_yz, c + 1)
            for g in range(GROUPS):
                m = act.activation(zs[:, c, g * 256:(g + 1) * 256], yst[:, c, g * 256:(g + 1) * 256], ACT.Square,
                                   accum_out=ssy[:, 0, 2 * c + g:2 * c + g + 1])
            m.then_inc(s_ysq, 1)

        SSD_STATES = [(0, 0), (1, 3), (0, 1), (1, 2), (0, 2), (1, 1)]
        LE_, GE_, GT_, LT_ = LE, GE, GT, LT
        def scan(eng, chain, d, half_, done):
            scratch = (W1, W2)[d]
            a = scratch[:, 0:ZS]
            b = scratch[:, ZS:2 * ZS]
            g0 = HALF * half_
            LRv = LR[:, d, g0:g0 + HALF].unsqueeze(1).broadcast_to([P, 2, HALF])
            LIv = LI[:, d, :, g0:g0 + HALF]
            kinds = lambda ap: ap.rearrange("p (e g) -> p e g", e=2)
            for n in range(NC5):
                last, new = (n, n + 1) if d == 0 else (NC5 - n, NC5 - 1 - n)
                at = last * ZS
                old = Z[d][:, at:at + ZS]
                swapped = bass.AP(sbuf, z_at[d] + at + HALF, [[words, P], [-HALF, 2], [1, HALF]])
                chain.link(eng.tensor_tensor(kinds(a), kinds(old), LRv, ALU.mult))
                chain.link(eng.tensor_tensor(kinds(b), swapped, LIv, ALU.mult))
                v = Z[d][:, new * ZS:(new + 1) * ZS]
                eng.wait_ge(chain.sem, chain.n - 1)
                chain.link(eng.tensor_tensor(a, a, v, ALU.add))
                chain.settle()
                m = eng.tensor_tensor(v, a, b, ALU.add)
                if n < NC5 - 1:
                    chain.link(m)
                    chain.settle()
                else:
                    m.then_inc(done, 1)
            eng.wait_ge(done, half_ + 1)

        TURN = {0: 0, 1: 1, 2: 2, 4: 3, 5: 4}
        ROW_TABLES = [(k, m) for k in range(4) for m in range(M5 if k < 2 else L5)] + [(4, 0), (4, 1)]
        s5_tile0 = groups[gidx["gg0"]][4]

        def s5_moves(sp):
            for c in range(TC):
                sp.wait_ge(s_hn, 12 + c + 1)
                sp.dma_start(hn_dram[c * P:(c + 1) * P, :], hn[:, c, :]).then_inc(s_hnd, 16)
            sp.wait_ge(s_hnd, 64)
            sp.wait_ge(s_tabD, 1)
            sp.dma_start(UN, hn_dram.rearrange("(n t) d -> n t d", t=L5)).then_inc(s_un, 16)
            for b in range(BATCHES):
                sp.wait_ge(s_kj, b + 1)
                if b:
                    sp.wait_ge(s_yy, b)
                for t in range(L5):
                    sp.dma_start(Kbig[GC * t:GC * (t + 1), :, :],
                                 KJ[0:GC, :, :, :].rearrange("p g j c -> p g (j c)")[:, :, GC * (L5 - 1 - t):GC * (2 * L5 - 1 - t)]
                                 ).then_inc(s_kb, 16)
                sp.wait_ge(s_yb, b + 1)
                sp.dma_start(y_dram.rearrange("(n t) d -> n t d", t=L5)[:, :, BG * GC * b:BG * GC * (b + 1)],
                             Yb[0:NC5, :, :]).then_inc(s_ydr, 16)
            sp.wait_ge(s_ydr, 16 * BATCHES)
            sp.dma_start(ytok, y_dram.rearrange("(c p) d -> p c d", p=P)).then_inc(s_yin, 16)

        releases = dict(used=s_used, group=s_grp, down=s_ffd, proj=s_pp)

        @block.sync
        def _(sp):
            sp.dma_start(h, x[0].rearrange("(c p) n -> p c n", p=P)).then_inc(s_x, 16)
            for src, r0, n in ((I["m2_conv_w"][0], 0, CONV * CB), (I["m2_conv_b"], 40, CB), (I["hg_norm_w"], 48, 4),
                               (I["hg_lb_logits"], 52, 4), (I["m2_norm_w"], 56, 4), (I["s5_d"], 60, 8)):
                sp.dma_start(parR[r0:r0 + n, :], src.rearrange("a (b n) -> (a b) n", n=P)).then_inc(s_par, 16)
            for n, (src, width) in enumerate(stream):
                if n == s5_tile0 + RING:
                    s5_moves(sp)
                if n >= RING:
                    what, count = release[n - RING]
                    sp.wait_ge(releases[what], count)
                dst = ring[:, n % RING, :]
                if width == -1:
                    dst = dst.rearrange("p (k n) -> p k n", k=2)
                else:
                    dst = dst.rearrange("p (k n) -> p k n", k=4)[:, :, 0:width]
                sp.dma_start(dst, src).then_inc(s_ring[n % RING], 16)
            for c in range(TC):
                sp.wait_ge(s_hn, 16 + c + 1)
                sp.dma_start(moe_dram[c * P:(c + 1) * P, :], hn[:, c, :]).then_inc(s_hnm, 16)
            for n in range(N0 - RING, N0):
                what, count = release[n]
                sp.wait_ge(releases[what], count)
            sp.wait_ge(s_plan, 1)
            units_sp = sp.value_load(plan_u[0:1, :], min_val=TC, max_val=MAXU)
            with sp.Fori(0, MAXU) as u:
                with sp.If(u < units_sp):
                    e = sp.value_load(plan_e[0:1, bass.ds(u, 1)], min_val=0, max_val=NE - 1)
                    for n, src in enumerate(moe_sources(e)):
                        sp.wait_ge(s_mt, u * PER + (n + 1))
                        slot = (N0 + n) % RING
                        sp.dma_start(ring[:, slot, :].rearrange("p (k n) -> p k n", k=src.shape[1]), src).then_inc(s_ring[slot], 16)
            sp.wait_ge(s_mt, units_sp * PER + RING)
            for j in range(2):
                sp.dma_start(gw[:, j, :, :], I["ple_gate"][1][:, 512 * j:512 * (j + 1)].rearrange("(k p) n -> p k n", p=P)
                             ).then_inc(s_gw, 16)
            for c in range(TC):
                sp.wait_ge(s_hn, 24 + c + 1)
                sp.dma_start(out[0, c * P:(c + 1) * P, :], hn[:, c, :]).then_inc(s_out, 16)
            sp.wait_ge(s_out, 16 * TC)

        @block.gpsimd
        def _(pool):
            chain = Chain(pool, s_pc)
            for n, v in enumerate((I["m2_dt_bias"][0].rearrange("a b -> (a b)"), I["m2_a_log"][0].rearrange("a b -> (a b)"),
                                   I["m2_d"][0])):
                dst = (dtb, alog, dskip)[n]
                pool.dma_start(dst, row(v).broadcast_to([P, v.shape[0]])).then_inc(s_tokp, 16)
            for k in range(2):
                pool.dma_start(nw[:, k, :], row(norm_w[k]).broadcast_to([P, D])).then_inc(s_nw[k], 16)
            chain.link(pool.memset(ones, 1.0))
            chain.link(pool.memset(eps, EPS))
            chain.settle()
            for m, op, sign in ((ident, ALU.is_equal, 1), (LE, ALU.is_ge, -1), (GE, ALU.is_ge, 1), (GT, ALU.is_gt, 1),
                                (LT, ALU.is_gt, -1)):
                pool.affine_select(out=m, in_=ones, compare_op=op, fill=0.0, base=0, pattern=[[-sign, P]],
                                   channel_multiplier=sign).then_inc(s_const, 1)

            chain.link(pool.memset(mtmp, 0.0))
            chain.settle()
            for l in range(7):
                n = 1 << l
                for d in range(2):
                    m = mtmp[:, 2 * l + d, :]
                    view = half(m, n, 1 - d)
                    blocks, lo = [[-2 * n, P // (2 * n)], [0, n]], n * d
                    chain.link(pool.memset(view, 1.0))
                    chain.settle()
                    chain.link(pool.affine_select(out=view, in_=view, compare_op=ALU.is_ge, fill=0.0, base=-lo,
                                                  pattern=blocks, channel_multiplier=1))
                    chain.settle()
                    chain.link(pool.affine_select(out=view, in_=view, compare_op=ALU.is_gt, fill=0.0, base=lo + n,
                                                  pattern=[[2 * n, P // (2 * n)], [0, n]], channel_multiplier=-1))
            chain.settle()
            pool.tensor_copy(masks, mtmp).then_inc(s_const, 1)

            def zero_suffix(hd):
                if hd >= 2:
                    pool.wait_ge(s_exp, 18 * (hd - 1))
                for d in range(2):
                    m = pool.memset(Rs[hd % 2][d], 0.0)
                m.then_inc(s_rz, 1)

            pool.wait_ge(s_hn, 4)
            for r0 in range(2 * TC * P, (MAXB + 1) * P, T):
                n = min(T, (MAXB + 1) * P - r0)
                pool.dma_start(y_rows[r0:r0 + n, :], x[0, 0:n, :]).then_inc(s_mys, 16)
            pool.wait_ge(s_tp, 8)
            pool.wait_ge(s_k, 8)
            pool.wait_ge(s_lf, 2)
            for hd in range(HEADS):
                zero_suffix(hd)
                if hd >= 1:
                    pool.wait_ge(s_dg, hd)
                pool.tensor_tensor(ksum, kT[0][:, hd, :], kT[1][:, hd, :], ALU.add).then_inc(s_ks, 1)
                pool.wait_ge(s_lf, 2)
                pool.wait_ge(s_rz, hd + 1)
                for l in range(LEVELS - 1):
                    for d in range(2):
                        n = hd * 18 + 2 * l + d
                        pool.wait_ge(s_exp, n + 1)
                        if l:
                            pool.wait_ge(s_upd, hd * 16 + 2 * (l - 1) + d + 1)
                        Pd, Rd = lf[d][:, hd, :], Rs[hd % 2][d]
                        hs = 1 << l
                        near, far = (0, 1) if d == 0 else (1, 0)
                        edge = hs - 1 if d == 0 else 0
                        shape = [P, T // (2 * hs), hs]
                        chain.link(pool.tensor_tensor(half(Rd, hs, near), half(Rd, hs, near),
                                                      half(Pd, hs, far)[:, :, edge:edge + 1].broadcast_to(shape), ALU.add))
                        chain.settle()
                        pool.tensor_tensor(half(Pd, hs, far), half(Pd, hs, far),
                                           half(Pd, hs, near)[:, :, edge:edge + 1].broadcast_to(shape),
                                           ALU.add).then_inc(s_upd, 1)

            pool.wait_ge(s_mix, HEADS)
            for c in (0, T + 2):
                m = pool.memset(raw[:, :, c:c + 2], 0.0)
            m.then_inc(s_pad, 1)
            pool.wait_ge(s_parTd, 1)
            for cb in range(CB):
                if cb >= 2:
                    pool.wait_ge(s_conv, cb - 1)
                for k in range(CONV):
                    m = pool.tensor_scalar(diag[:, cb % 2, k, :], ident, parT[:, k * CB + cb:k * CB + cb + 1], None, ALU.mult)
                m.then_inc(s_diag, 1)
            pool.wait_ge(s_dt, 1)
            pool.wait_ge(s_ex, 1)
            R = ex[:, 64:128].rearrange("p (d c k) -> p d c k", d=2, c=4)
            pool.tensor_tensor(toend.rearrange("p d c k -> p (d c k)"), ex[:, 64:128], dts.rearrange("p d c k -> p (d c k)"),
                               ALU.mult).then_inc(s_te, 1)
            pool.wait_ge(s_te, 1)
            for m, (d, c) in enumerate(SSD_STATES):
                pool.wait_ge(s_xtd, c + 1)
                if m >= 2:
                    pool.wait_ge(s_st, m - 1)
                pool.tensor_tensor(xe[:, m % 2, :].rearrange("p (k n) -> p k n", k=MH),
                                   xst[:, c, :].rearrange("p (k n) -> p k n", k=MH),
                                   toend[:, d, c, :].unsqueeze(2).broadcast_to([P, MH, MP]), ALU.mult).then_inc(s_xe, 1)
            for c in range(TC):
                if c >= 1:
                    pool.wait_ge(s_seg, c)
                for d in range(2):
                    m = pool.tensor_tensor(dtaU[:, d, :, :], (LE_, GE_)[d].unsqueeze(1).broadcast_to([P, MH, P]),
                                           dta[:, d, c, :].unsqueeze(2).broadcast_to([P, MH, P]), ALU.mult)
                m.then_inc(s_dtau, 1)
                if c >= 1:
                    pool.wait_ge(s_y, c)
                for d in range(2):
                    m = pool.tensor_tensor(xdt[:, d, :].rearrange("p (k n) -> p k n", k=MH),
                                           xst[:, c, :].rearrange("p (k n) -> p k n", k=MH),
                                           dts[:, d, c, :].unsqueeze(2).broadcast_to([P, MH, MP]), ALU.mult)
                m.then_inc(s_xdt, 1)
            for k in range(2, 4):
                pool.wait_ge(s_hn, 4 * (k - 1))
                pool.dma_start(nw[:, k % 2, :], row(norm_w[k]).broadcast_to([P, D])).then_inc(s_nw[k % 2], 16)
                if k == 2:
                    pool.wait_ge(s_ffd, 8)
                    pool.dma_start(ptok, p_in[0, 0].rearrange("(c p) n -> p c n", p=P)).then_inc(s_p, 16)
            pool.wait_ge(s_ph, 4)
            pool.dma_start(nw[:, 0, :], row(norm_w[4]).broadcast_to([P, D])).then_inc(s_nw[0], 16)
            for v, dst in ((I["s5_a_re"], r_are), (I["s5_a_im"], r_aim)):
                pool.dma_start(dst, v[0].rearrange("d g n -> (d g) n")).then_inc(s_s5in, 16)
            pool.dma_start(r_ls, I["s5_log_step"][0].rearrange("d (g a) -> (d g) a", a=1)).then_inc(s_s5in, 16)
            for n, v in enumerate((I["s5_c_re"], I["s5_c_im"], I["s5_c_re"])):
                pool.dma_start(C3[:, :, n, :], v[0].rearrange("d (b g) c n -> (g c) (d b) n", b=8)).then_inc(s_s5in, 16)
            for dst, top, low in ((Bst, I["s5_b_re"], I["s5_b_im"]), (Bsw, I["s5_b_im"], I["s5_b_re"])):
                for q, v in ((0, top), (1, low)):
                    pool.dma_start(dst[NS * q:NS * (q + 1), :, :], v[0].rearrange("g n c -> n g c")).then_inc(s_s5in, 16)
            pool.wait_ge(s_u, 8)
            pool.dma_start(nw[:, 1, :], row(norm_w[5]).broadcast_to([P, D])).then_inc(s_nw[1], 16)
            for hf in range(2):
                for b in range(8 * hf, 8 * hf + 8):
                    if b % 8:
                        pool.wait_ge(s_bp, b)
                    elif b:
                        pool.wait_ge(s_cp, b)
                    for d in range(2):
                        m = pool.tensor_tensor(BQ[:, d, :, :].rearrange("p g (m c) -> p g m c", m=L5),
                                               Bsw[:, BG * b:BG * (b + 1), :].unsqueeze(2).broadcast_to([P, BG, L5, GC]),
                                               WB[:, d, BG * b:BG * (b + 1), :].unsqueeze(3).broadcast_to([P, BG, L5, GC]),
                                               ALU.mult)
                    m.then_inc(s_t2, 1)
                pool.wait_ge(s_vd, 8 * (hf + 1))
                pool.wait_ge(s_z0, hf + 1)
                scan(pool, chain, 1, hf, s_zb)
                for b in range(8 * hf, 8 * hf + 8):
                    if b % 8:
                        pool.wait_ge(s_cp, b)
                    else:
                        pool.wait_ge(s_bp, 8 * (hf + 1))
                    for d in range(2):
                        m = pool.tensor_tensor(CQ[:, d, :, :].rearrange("p g (m c) -> p g m c", m=M5),
                                               Csw[:, d, BG * b:BG * (b + 1), :].unsqueeze(2).broadcast_to([P, BG, M5, GC]),
                                               PB[:, d, BG * b:BG * (b + 1), :].unsqueeze(3).broadcast_to([P, BG, M5, GC]),
                                               ALU.mult)
                    m.then_inc(s_t2, 1)
            pool.wait_ge(s_yy, BATCHES)
            pool.dma_start(skip_w, row(I["s5_d"][0]).broadcast_to([P, D])).then_inc(s_dw, 16)
            pool.dma_start(ptok1, p_in[1, 0].rearrange("(c p) n -> p c n", p=P)).then_inc(s_p, 16)
            pool.dma_start(pw1, I["ple_proj"][1].rearrange("(k p) n -> p k n", p=P)).then_inc(s_pw, 16)

            pool.wait_ge(s_drD, cumD[gidx["go1"]])
            pool.dma_start(router, I["moe_router"][0].rearrange("(k p) e -> p k e", p=P)).then_inc(s_rtr, 16)
            pool.wait_ge(s_hn, 20)
            pool.dma_start(nw[:, 0, :], row(norm_w[6]).broadcast_to([P, D])).then_inc(s_nw[0], 16)
            pool.wait_ge(s_mys, 16 * 2)
            pool.wait_ge(s_plan, 1)
            pool.wait_ge(s_hnm, 16 * TC)

            def hold(n):
                return pool.tensor_tensor(slot_junk[:, n:n + 1], ident[:, 0:1], ident[:, 1:2], ALU.add)

            def gather_unit(first, count):
                for n in range(2):
                    pool.tensor_copy(slot_now[:, n:n + 1], slot_tok[:, first + n:first + n + 1] if isinstance(first, int) else
                                     slot_tok[:, bass.ds(first + n, 1)]).then_inc(s_ix, 1)
                pool.wait_ge(s_ix, count)
                hold(1).then_inc(s_ix, 1)
                for n in range(2):
                    pool.indirect_dma_start(xblk[:, n, :], None, moe_dram,
                                            bass.IndirectOffsetOnAxis(slot_now[:, n:n + 1], 0)).then_inc(s_xg, 16)

            gather_unit(0, 2)
            units_pool = pool.value_load(plan_u[0:1, :], min_val=TC, max_val=MAXU)
            with pool.Fori(0, MAXU) as u:
                with pool.If(u < units_pool):
                    pool.wait_ge(s_xtp, u + 1)
                    hold(0).then_inc(s_ix, 1)
                    following = pool.value_load(plan_b[0:1, bass.ds(u + 1, 1)], min_val=0, max_val=MAXB)
                    gather_unit(following, 5 * u + 6)
                    pool.wait_ge(s_myA, u + 1)
                    pool.wait_ge(s_myd, u + 2)
                    hold(2).then_inc(s_ix, 1)
                    here = pool.value_load(plan_b[0:1, bass.ds(u, 1)], min_val=0, max_val=MAXB - 1)
                    pool.dma_start(y_rows[bass.ds(here * P, 2 * P), :].rearrange("(a p) n -> p a n", p=P), yblk).then_inc(s_mys, 16)
            pool.wait_ge(s_mys, units_pool * 16 + 32)
            pool.wait_ge(s_xg, units_pool * 32 + 32)
            hold(3)
            for c in range(TC):
                for k in range(2):
                    pool.indirect_dma_start(yg[k][:, c, :], None, y_rows,
                                            bass.IndirectOffsetOnAxis(desti[:, k, c:c + 1], 0)).then_inc(s_yg[c], 16)


        @block.tensor
        def _(pe):
            def tile(n):
                pe.wait_ge(s_ring[n % RING], 16 * (n // RING + 1))
                return ring[:, n % RING, :].rearrange("p (k n) -> p k n", k=2 if stream[n][1] == -1 else 4)

            def all_drained(name):
                g = gidx[name]
                if cumA[g]:
                    pe.wait_ge(s_drA, cumA[g])
                if cumD[g]:
                    pe.wait_ge(s_drD, cumD[g])

            def transpose_norm(k):
                for c in range(TC):
                    pe.wait_ge(s_hn, 4 * k + c + 1)
                    for g in range(2):
                        for q in range(4):
                            m = pe.transpose(psum[:, 2 * c + g, q * P:(q + 1) * P],
                                             hn[:, c, (4 * g + q) * P:(4 * g + q + 1) * P], ident)
                        m.then_inc(s_tp, 1)
                pe.wait_ge(s_hA, 4 * (TURN[k] + 1))
                pe.wait_ge(s_hD, 4 * (TURN[k] + 1))

            def dense(name, act):
                g = gidx[name]
                _, layout, width, _, t0 = groups[g]
                if t0 is None:
                    pe.wait_ge(s_gw, 32)
                b0 = 4 * (g % 2)
                if g >= 2:
                    all_drained(groups[g - 2][0])
                for kk in range(2):
                    w = gw[:, int(name[-1]), 4 * kk:4 * kk + 4, :] if t0 is None else tile(t0 + kk)
                    for b in range(4):
                        for k in range(4):
                            at = dict(start=kk == 0 and k == 0, stop=kk == 1 and k == 3, skip_group_check=True)
                            if layout == "T":
                                m = pe.matmul(psum[:, b0 + b, :], w[:, k, b * P:(b + 1) * P], act[:, 4 * kk + k, :], **at)
                            else:
                                m = pe.matmul(psum[:, b0 + b, 0:width], act[:, 4 * kk + k, b * P:(b + 1) * P],
                                              w[:, k, 0:width], **at)
                        if kk == 1:
                            m.then_inc(s_grp, 1)
                    if kk == 0 and t0 is not None:
                        m.then_inc(s_used, 1)

            pe.wait_ge(s_const, 6)
            pe.wait_ge(s_par, 16 * 6)
            pe.transpose(psum[:, 7, 0:68], parR[0:68, :], ident[0:68, 0:68]).then_inc(s_parT, 1)
            pe.wait_ge(s_parTd, 1)
            transpose_norm(0)
            for name in ("q", "ff", "fb", "v", "g"):
                dense(name, hnT)

            def hg_out(hd):
                pe.wait_ge(s_gdr, 18 * (hd + 1))
                if hd >= 2:
                    pe.wait_ge(s_mix, hd - 1)
                for c in range(TC):
                    m = pe.matmul(psum[:, 5 + hd % 2, :], vtok[:, c, hd * P:(hd + 1) * P], S_main[:, c, :],
                                  start=c == 0, stop=c == TC - 1)
                m.then_inc(s_o, 1)

            def hg_squares(hd):
                pe.wait_ge(s_osq, hd + 1)
                if hd >= 1:
                    pe.wait_ge(s_orms, hd)
                pe.matmul(psum[:, 7, :], ones, osq, start=True, stop=True).then_inc(s_oss, 1)

            all_drained("g")
            for hd in range(HEADS):
                pe.wait_ge(s_ks, hd + 1)
                if hd >= 1:
                    pe.wait_ge(s_sd, hd)
                for c in range(TC):
                    at = slice(c * P, (c + 1) * P)
                    m = pe.matmul(psum[:, 4, at], ksum[:, at], qT[:, hd, at], start=True, stop=True)
                m.then_inc(s_dg, 1)
                for j in range(18):
                    n, l, d = hd * 18 + j, j // 2, j % 2
                    X, bank = Xb[n % 4], psum[:, n % 4, :]
                    pe.wait_ge(s_X, n + 1)
                    if n >= 4:
                        pe.wait_ge(s_gdr, n - 3)
                    if l < 7:
                        for c in range(TC):
                            at = slice(c * P, (c + 1) * P)
                            m = pe.matmul(bank[:, at], X[:, at], X[:, at], start=True, stop=True)
                    elif l == 7:
                        for i in range(2):
                            s0, t0 = (2 * i, 2 * i + 1) if d == 0 else (2 * i + 1, 2 * i)
                            m = pe.matmul(bank[:, i * P:(i + 1) * P], X[:, s0 * P:(s0 + 1) * P],
                                          X[:, t0 * P:(t0 + 1) * P], start=True, stop=True)
                    else:
                        for i in range(2):
                            s0, t0 = (i, 2) if d == 0 else (2 + i, 0)
                            m = pe.matmul(bank[:, i * 256:(i + 1) * 256], X[:, s0 * P:(s0 + 1) * P],
                                          X[:, t0 * P:(t0 + 2) * P], start=True, stop=True)
                    m.then_inc(s_gram, 1)
                    if hd and j == 2:
                        hg_out(hd - 1)
                    if hd and j == 6:
                        hg_squares(hd - 1)
            hg_out(HEADS - 1)
            hg_squares(HEADS - 1)

            pe.wait_ge(s_mix, HEADS)
            pe.wait_ge(s_gdr, 18 * HEADS)
            for name in ("z", "xs", "bc", "dt"):
                dense(name, hnT)
            all_drained("dt")
            for cb in range(CB):
                pe.wait_ge(s_diag, cb + 1)
                if cb >= 2:
                    pe.wait_ge(s_cact, cb - 1)
                for k in range(CONV):
                    m = pe.matmul(psum[:, cb % 2, :], diag[:, cb % 2, k, :], raw[:, cb, k:k + T], start=k == 0,
                                  stop=k == CONV - 1)
                m.then_inc(s_conv, 1)
            pe.wait_ge(s_cact, CB)
            for c in range(TC):
                b = 4 + 2 * (c % 2)
                if c >= 2:
                    pe.wait_ge(s_xtd, c - 1)
                for q in range(6):
                    m = pe.transpose(psum[:, b + q // 4, (q % 4) * P:(q % 4 + 1) * P], xc[:, q, c * P:(c + 1) * P], ident)
                m.then_inc(s_xt, 1)
            pe.wait_ge(s_dt, 1)
            df = [dta[:, d, :, :].rearrange("p c k -> p (c k)") for d in range(2)]
            for n, (w, d) in enumerate(((LE_, 0), (GE_, 1), (GT_, 0), (LT_, 1))):
                pe.matmul(psum[:, 3, 32 * n:32 * n + 32], w, df[d], start=True, stop=True)
            pe.matmul(psum[:, 3, 128:192], ones, dta.rearrange("p d c k -> p (d c k)"), start=True,
                      stop=True).then_inc(s_cum, 1)
            for m_, (d, c) in enumerate(SSD_STATES):
                pe.wait_ge(s_xe, m_ + 1)
                if m_ >= 2:
                    pe.wait_ge(s_H, m_ - 1)
                for g in range(GROUPS):
                    m = pe.matmul(psum[:, m_ % 2, g * 256:(g + 1) * 256], btok[:, c, g * P:(g + 1) * P],
                                  xe[:, m_ % 2, g * 256:(g + 1) * 256], start=True, stop=True)
                m.then_inc(s_st, 1)
            pe.wait_ge(s_H, 6)
            pe.wait_ge(s_xtd, TC)
            pe.wait_ge(s_ex, 1)
            for c in range(TC):
                at = slice(c * P, (c + 1) * P)
                if c >= 1:
                    pe.wait_ge(s_cbm, c)
                for g in range(GROUPS):
                    m = pe.matmul(psum[:, 2, g * P:(g + 1) * P], xc[:, 4 + g, at], xc[:, 6 + g, at], start=True, stop=True)
                m.then_inc(s_cb, 1)
                pe.wait_ge(s_dtau, c + 1)
                if c >= 1:
                    pe.wait_ge(s_E, c)
                for n in range(4):
                    d = n // 2
                    m = pe.matmul(psum[:, 4 + n, :], (GT_, LT_)[d],
                                  dtaU[:, d, 4 * (n % 2):4 * (n % 2) + 4, :].rearrange("p k t -> p (k t)"),
                                  start=True, stop=True)
                m.then_inc(s_seg, 1)
                pe.wait_ge(s_w, c + 1)
                pe.wait_ge(s_xdt, c + 1)
                if c >= 1:
                    pe.wait_ge(s_yd, c)
                for k in range(MH):
                    for d in range(2):
                        m = pe.matmul(psum[:, 3, k * MP:(k + 1) * MP], Ew[:, d, k, :], xdt[:, d, k * MP:(k + 1) * MP],
                                      start=d == 0, stop=d == 1, skip_group_check=True)
                for d in range(2):
                    if c == (0, TC - 1)[d]:
                        continue
                    for g in range(GROUPS):
                        m = pe.matmul(psum[:, d, g * 256:(g + 1) * 256], xc[:, 6 + g, at],
                                      Hst[d][:, c - 1 + d, g * 256:(g + 1) * 256], start=True, stop=True)
                m.then_inc(s_y, 1)
            for c in range(TC):
                pe.wait_ge(s_yn, c + 1)
                if c >= 2:
                    pe.wait_ge(s_ym, c - 1)
                for q in range(4):
                    m = pe.transpose(psum[:, 4 + c % 2, q * P:(q + 1) * P], yst[:, c, q * P:(q + 1) * P], ident)
                m.then_inc(s_yt, 1)
            pe.wait_ge(s_ym, TC)
            dense("o0", mixT)
            dense("o1", mixT)

            all_drained("o1")
            transpose_norm(1)
            for j in range(FJ):
                dense(f"fg{j}", hnT)
                dense(f"fu{j}", hnT)
            all_drained(f"fu{FJ - 1}")
            for j in range(FJ):
                for hf in range(2):
                    n = down_tile0 + 2 * j + hf
                    w = tile(n)
                    for c in range(TC):
                        for k in range(4):
                            m = pe.matmul(psum[:, 2 * c + hf, :], hT[:, 4 * j + k, c * P:(c + 1) * P], w[:, k, :],
                                          start=j == 0 and k == 0, stop=j == FJ - 1 and k == 3, skip_group_check=True)
                        if j == FJ - 1:
                            m.then_inc(s_ffd, 1)
                    if j < FJ - 1:
                        m.then_inc(s_used, 1)

            def embed(layer):
                ptok_, pT_ = ((ptok, pT), (ptok1, pT1))[layer]
                pe.wait_ge(s_p, 16 * (layer + 1))
                for c in range(TC):
                    for q in range(2):
                        m = pe.transpose(psum[:, 0, c * P:(c + 1) * P] if q == 0 else psum[:, 1, c * P:(c + 1) * P],
                                         ptok_[:, c, q * P:(q + 1) * P], ident)
                m.then_inc(s_pT, 1)
                pe.wait_ge(s_pTd, layer + 1)
                if layer:
                    pe.wait_ge(s_pw, 16)
                w = pw1 if layer else tile(ple_tile)
                for c in range(TC):
                    for hf in range(2):
                        for k in range(2):
                            m = pe.matmul(psum[:, 2 * c + hf, :], pT_[:, k, c * P:(c + 1) * P],
                                          w[:, k, hf * 512:(hf + 1) * 512], start=k == 0, stop=k == 1)
                        m.then_inc(s_pp, 1)
                pe.wait_ge(s_ppd, 8 * (layer + 1))

            pe.wait_ge(s_fd, 8)
            embed(0)
            transpose_norm(2)
            dense("pg00", hnT)
            dense("pg01", hnT)

            all_drained("pg01")
            pe.wait_ge(s_s5in, 16 * 10)
            for n in range(16):
                if n >= 4:
                    pe.wait_ge(s_cst, n - 3)
                for v in range(2):
                    m = pe.transpose(psum[:, n % 4, v * P:(v + 1) * P], C3[:, n, v:v + 2, :].rearrange("p q n -> p (q n)"), ident)
                m.then_inc(s_rt, 1)
            pe.wait_ge(s_rowt, 1)
            for n, (k, m_) in enumerate(ROW_TABLES):
                if n >= 4:
                    pe.wait_ge(s_cst, 16 + n - 3)
                m = pe.transpose(psum[:, 4 + n % 4, 0:P], rowt[:, k, m_, :, :].rearrange("p q n -> p (q n)"), ident)
                m.then_inc(s_rt, 1)
            pe.wait_ge(s_cst, 16 + len(ROW_TABLES))
            pe.wait_ge(s_un, 16)
            for n in range(8):
                pe.wait_ge(s_up, n + 1)
                for q in range(8):
                    m = pe.transpose(psum[:, n, NC5 * q:NC5 * (q + 1)], UP[n % 2][0:NC5, P * q:P * (q + 1)], ident[0:NC5, 0:NC5])
                m.then_inc(s_ut, 1)
            pe.wait_ge(s_u, 8)
            for hf in range(2):
                for b in range(8 * hf, 8 * hf + 8):
                    pe.wait_ge(s_bp, b + 1)
                    for d in range(2):
                        for g in range(BG):
                            m = pe.transpose(psum[:, d, g * P:(g + 1) * P], BP[:, d, g, :], ident)
                    m.then_inc(s_bt, 1)
                    pe.wait_ge(s_bigA, b + 1)
                    pe.wait_ge(s_bigD, b + 1)
                    if b % 8:
                        pe.wait_ge(s_vd, b)
                    for d in range(2):
                        for e in range(2):
                            for g in range(BG):
                                m = pe.matmul(psum[:, 2 + d, (e * BG + g) * NC5:(e * BG + g + 1) * NC5],
                                              BigB[:, d, g, NS - NS * e:NS - NS * e + P], U[:, BG * b + g, :],
                                              start=True, stop=True)
                    m.then_inc(s_v, 1)
                pe.wait_ge(s_vd, 8 * (hf + 1))
                for b in range(8 * hf, 8 * hf + 8):
                    gl = BG * (b - 8 * hf)
                    pe.wait_ge(s_cp, b + 1)
                    for d in range(2):
                        for g in range(BG):
                            m = pe.matmul(psum[0:GC, 4 + d, g * P:(g + 1) * P], BBk[:, d, gl + g, :],
                                          CP[:, d, g, GC * d:GC * d + P], start=True, stop=True)
                    m.then_inc(s_kk, 1)
                    if b % 8 == 0:
                        pe.wait_ge(s_zf, hf + 1)
                        pe.wait_ge(s_zb, hf + 1)
                    pe.wait_ge(s_kb, 16 * L5 * (b + 1))
                    if b:
                        pe.wait_ge(s_yb, b)
                    for g in range(BG):
                        o = psum[0:NC5, 6, g * P:(g + 1) * P]
                        pe.matmul(o, U[:, BG * b + g, :], Kbig[:, g, :], start=True, stop=False, skip_group_check=True)
                        for d in range(2):
                            first = z_at[d] + d * ZS + gl + g
                            states = bass.AP(sbuf, first, [[words, P], [ZS, NC5]])
                            m = pe.matmul(o, states, CP[:, d, g, GC * (1 - d):GC * (1 - d) + P], start=False, stop=d == 1,
                                          skip_group_check=True)
                    m.then_inc(s_yy, 1)
            pe.wait_ge(s_yb, BATCHES)
            for c in range(TC):
                pe.wait_ge(s_gl, c + 1)
                for g in range(2):
                    for q in range(4):
                        m = pe.transpose(psum[:, 2 * c + g, q * P:(q + 1) * P],
                                         ytok[:, c, (4 * g + q) * P:(4 * g + q + 1) * P], ident)
                    m.then_inc(s_glt, 1)
            pe.wait_ge(s_glA, 4)
            pe.wait_ge(s_glD, 4)
            for j in range(2):
                dense(f"gg{j}", hnT)
                dense(f"go{j}", hnT)

            all_drained("go1")
            embed(1)
            transpose_norm(4)
            pe.matmul(psum[:, 1, 128:256], ones, LT, start=True, stop=True)
            pe.matmul(psum[:, 1, 64:65], LT, ones[:, 0:1], start=True, stop=True)
            pe.wait_ge(s_rtr, 16)
            for c in range(TC):
                for k in range(8):
                    m = pe.matmul(psum[:, 0, NE * c:NE * (c + 1)], hnT[:, k, c * P:(c + 1) * P], router[:, k, :],
                                  start=k == 0, stop=k == 7)
                    if (c, k) == (0, 0):
                        m.then_inc(s_mt, RING)
            m.then_inc(s_lg, 1)
            pe.wait_ge(s_hot, 1)
            for c in range(TC):
                for c0 in range(c + 1):
                    pe.matmul(psum[:, 1, NE * c:NE * (c + 1)], LT if c0 == c else ones, hot[:, 2, c0, :], start=c0 == 0,
                              stop=c0 == c, skip_group_check=True)
            for c in range(TC):
                m = pe.matmul(psum[:, 1, 32:32 + NE], ones, hot[:, 2, c, :], start=c == 0, stop=c == TC - 1,
                              skip_group_check=True)
            m.then_inc(s_rank, 1)
            pe.wait_ge(s_slot, 1)
            for n in range(2 * TC):
                k, c = n // TC, n % TC
                m = pe.matmul(psum[:, 2, 0:SLOTC], moe_hotR[:, k, c, :], moe_hotB[:, k, c, :], start=n == 0,
                              stop=n == 2 * TC - 1)
            m.then_inc(s_tok, 1)
            pe.wait_ge(s_plan, 1)

            def unit_pe(u, two):
                toks = 2 * P if two else P

                def ready(n):
                    if two:
                        pe.wait_ge(s_ws, u * PER + (n + 1))
                    else:
                        tile_wait(pe, u, n)

                def product(out_, w, act_, weights_move, start, stop):
                    pairs = ((w[0], act_[0]), (w[1], act_[0]), (w[0], act_[1])) if two else ((w[0], act_[0]),)
                    for n, (a, b) in enumerate(pairs):
                        a, b = (b, a) if weights_move else (a, b)
                        m = pe.matmul(out_, a, b, start=start and n == 0, stop=stop and n == len(pairs) - 1, skip_group_check=True)
                    return m

                def weights(n, k):
                    return [ap.rearrange("p (k n) -> p k n", k=k)
                            for ap in ((w_high[n % WSLOTS], w_low[n % WSLOTS]) if two else (unit_tile(n),))]

                def down(s_):
                    ready(down_at(s_))
                    pe.wait_ge(s_mh, u * (3 * STEPS) + (3 * s_ + 3))
                    if s_ == 0:
                        pe.wait_ge(s_myd, u + 1)
                        pe.wait_ge(s_myA, u)
                    w = weights(down_at(s_), 2)
                    for blk in range(2 if two else 1):
                        for hf in range(2):
                            at = slice(512 * hf, 512 * (hf + 1))
                            tk = slice(P * blk, P * (blk + 1))
                            for k in range(2):
                                m = product(psum[:, 4 + 2 * blk + hf, :], [ap[:, k, at] for ap in w],
                                            [ap[:, s_ % 2, k, tk] for ap in ((ehH, ehL) if two else (ehid,))], True,
                                            s_ == 0 and k == 0, s_ == STEPS - 1 and k == 1)
                    m.then_inc(s_mt, 1)

                pe.wait_ge(s_xg, u * 32 + 32)
                for blk in range(2 if two else 1):
                    for g in range(2):
                        for q in range(4):
                            m = pe.transpose(psum[:, 2 * blk + g, q * P:(q + 1) * P],
                                             xblk[:, blk, (4 * g + q) * P:(4 * g + q + 1) * P], ident)
                m.then_inc(s_xtp, 1)
                pe.wait_ge(s_xtA, u * 4 + 4)
                pe.wait_ge(s_xtD, u + 1)
                for s_ in range(STEPS):
                    for part in range(2):
                        n = gate_at(s_) + part
                        ready(n)
                        w = weights(n, 8)
                        for fb in range(2):
                            fs = slice(P * fb, P * (fb + 1))
                            for k in range(8):
                                m = product(psum[:, 2 * part + s_ % 2, 256 * fb:256 * fb + toks], [ap[:, k, fs] for ap in w],
                                            [ap[:, k, 0:toks] for ap in ((xbH, xbL) if two else (xbT,))], False, k == 0, k == 7)
                        m.then_inc(s_mt, 1)
                    if s_:
                        down(s_ - 1)
                down(STEPS - 1)

            units_pe = pe.value_load(plan_u[0:1, :], min_val=TC, max_val=MAXU)
            with pe.Fori(0, MAXU) as u:
                with pe.If(u < units_pe):
                    blocks_pe = pe.value_load(plan_n[0:1, bass.ds(u, 1)], min_val=1, max_val=2)
                    with pe.If(blocks_pe > 1):
                        unit_pe(u, True)
                    with pe.If(blocks_pe < 2):
                        unit_pe(u, False)
            transpose_norm(5)
            dense("pg10", hnT)
            dense("pg11", hnT)

        @block.scalar
        def _(act):
            def norm(k, ready, turn=True):
                for c in range(TC):
                    ready(act, c)
                    act.activation(hn[:, c, :], h[:, c, :], ACT.Square, accum_out=stat[:, k, 0, c:c + 1]).then_inc(s_sq, 1)
                act.wait_ge(s_sq, 4 * (k + 1))
                act.activation(stat[:, k, 1, :], stat[:, k, 0, :], ACT.Sqrt, bias=eps, scale=1.0 / D).then_inc(s_rms, 1)
                for c in range(TC if turn else 0):
                    act.wait_ge(s_tp, 8 * TURN[k] + 2 * c + 1)
                    act.activation(hnT[:, 0:4, c * P:(c + 1) * P], psum[:, 2 * c, :].rearrange("p (q t) -> p q t", q=4),
                                   ACT.Copy).then_inc(s_hA, 1)

            def drain(name, out_of, func):
                g = gidx[name]
                for b in range(4):
                    act.wait_ge(s_grp, 4 * g + b + 1)
                    act.activation(out_of(b), psum[:, 4 * (g % 2) + b, :], func).then_inc(s_drA, 1)

            act.wait_ge(s_const, 1)
            norm(0, h_ready[0])
            act.wait_ge(s_lb, 1)
            act.activation(hgc[:, 1, :], hgc[:, 0, :], ACT.Exp).then_inc(s_lbc, 1)
            drain("q", lambda b: qT[:, b, :], ACT.Silu)
            for name, d in (("ff", 0), ("fb", 1)):
                g = gidx[name]
                for b in range(4):
                    bank = psum[:, 4 * (g % 2) + b, :]
                    act.wait_ge(s_grp, 4 * g + b + 1)
                    act.activation(lf[d][:, b, :], bank, ACT.Sigmoid)
                    act.activation(kT[d][:, b, :], bank, ACT.Sigmoid, scale=-1.0).then_inc(s_drA, 1)
            drain("g", lambda b: gT[:, b, :], ACT.Sigmoid)
            for d in range(2):
                act.wait_ge(s_lnin, d + 1)
                act.activation(lf[d], lf[d], ACT.Ln)
                act.activation(lnb4, lnb4, ACT.Ln).then_inc(s_lnout, 1)

            def hg_square(hd):
                act.wait_ge(s_o, hd + 1)
                if hd == HEADS - 1:
                    pass
                act.activation(osq, psum[:, 5 + hd % 2, :], ACT.Square).then_inc(s_osq, 1)

            def hg_rms(hd):
                act.wait_ge(s_oss, hd + 1)
                if hd:
                    act.wait_ge(s_mix, hd)
                act.activation(orms, psum[:, 7, :], ACT.Sqrt, bias=eps, scale=1.0 / P).then_inc(s_orms, 1)

            act.wait_ge(s_lf, 2)
            for hd in range(HEADS):
                act.wait_ge(s_rz, hd + 1)
                for j in range(18):
                    n, l, d = hd * 18 + j, j // 2, j % 2
                    if n >= 4:
                        act.wait_ge(s_gram, n - 3)
                    if l:
                        act.wait_ge(s_upd, hd * 16 + 2 * (l - 1) + d + 1)
                    hs = 1 << l
                    near, far = (0, 1) if d == 0 else (1, 0)
                    act.activation(half(Xb[n % 4], hs, far), half(lf[d][:, hd, :], hs, far), ACT.Exp)
                    act.activation(half(Xb[n % 4], hs, near), half(Rs[hd % 2][d], hs, near), ACT.Exp).then_inc(s_exp, 1)
                    if hd and j == 5:
                        hg_square(hd - 1)
                    if hd and j == 9:
                        hg_rms(hd - 1)
            hg_square(HEADS - 1)
            hg_rms(HEADS - 1)

            act.wait_ge(s_mix, HEADS)
            drain("z", lambda b: zs[:, b, :], ACT.Silu)
            act.wait_ge(s_parTd, 1)
            for cb in range(CB):
                act.wait_ge(s_conv, cb + 1)
                act.activation(xc[:, cb, :], psum[:, cb % 2, :], ACT.Silu, bias=parT[:, 40 + cb:41 + cb]).then_inc(s_cact, 1)
            act.wait_ge(s_sp, 2)
            act.activation(dtt, dtt, ACT.Exp, scale=-1.0).then_inc(s_ac, 1)
            act.wait_ge(s_ac, 1)
            act.activation(dtt, dtt, ACT.Ln, bias=1.0).then_inc(s_ac, 1)
            act.activation(aneg, alog, ACT.Exp).then_inc(s_ac, 1)
            act.wait_ge(s_cum, 1)
            act.activation(ex, psum[:, 3, 0:192], ACT.Exp).then_inc(s_ex, 1)
            for c in range(TC):
                act.wait_ge(s_seg, c + 1)
                if c:
                    act.wait_ge(s_y, c)
                act.activation(Ew.rearrange("p d k t -> p (d k t)"), psum[:, 4:8, :].rearrange("p b n -> p (b n)"),
                               ACT.Exp).then_inc(s_E, 1)
                if c:
                    ssd_squares(act, c - 1)
            ssd_squares(act, TC - 1)
            act.wait_ge(s_ysq, TC)
            act.activation(ssy[:, 1, :], ssy[:, 0, :], ACT.Sqrt, bias=eps, scale=1.0 / (INNER // GROUPS)).then_inc(s_yrms, 1)

            norm(1, h_ready[1])
            for j in range(FJ):
                g = gidx[f"fg{j}"]
                for b in range(4):
                    act.wait_ge(s_grp, 4 * g + b + 1)
                    if j:
                        act.wait_ge(s_drD, cumD[gidx[f"fu{j - 1}"]] - 3 + b)
                    act.activation(silT[:, b, :], psum[:, 4 * (g % 2) + b, :], ACT.Silu).then_inc(s_drA, 1)
            act.wait_ge(s_pT, 1)
            act.activation(pT[:, 0, :], psum[:, 0, :], ACT.Copy).then_inc(s_ac, 1)
            norm(2, h_ready[2])

            def gate_ple(layer):
                gates = pgate.rearrange("p k t -> p (k t)").rearrange("p (c n) -> p c n", c=4)
                for j in range(2):
                    g = gidx[f"pg{layer}{j}"]
                    for b in range(4):
                        act.wait_ge(s_grp, 4 * g + b + 1)
                        act.activation(gates[:, b, 512 * j:512 * (j + 1)], psum[:, 4 * (g % 2) + b, :],
                                       ACT.Sigmoid).then_inc(s_drA, 1)

            gate_ple(0)

            act.wait_ge(s_s5in, 16 * 10)
            act.activation(r_ls, r_ls, ACT.Exp).then_inc(s_sin, 1)
            act.wait_ge(s_ang, 1)
            act.activation(r_x, r_x, ACT.Exp).then_inc(s_sin, 1)
            act.wait_ge(s_ang, 2)
            act.activation(r_s, r_r, ACT.Sin)
            act.activation(r_c, r_r, ACT.Sin, scale=0.5).then_inc(s_sin, 1)
            norm(3, h_ready[3], False)
            act.wait_ge(s_un, 16)
            for n in range(8):
                if n >= 2:
                    act.wait_ge(s_ut, n - 1)
                act.activation(UP[n % 2][0:NC5, 0:8 * P].rearrange("p (g t c) -> p t g c", g=8, t=L5),
                               UN[:, :, P * n:P * (n + 1)].rearrange("p t (g c) -> p t g c", g=8), ACT.Copy).then_inc(s_up, 1)
            for b in range(BATCHES):
                act.wait_ge(s_bt, b + 1)
                if b % 8:
                    act.wait_ge(s_v, b)
                src = psum[:, 0, :].rearrange("p (g n) -> p g n", g=BG)
                act.activation(BigB[:, 0, :, NS:192], src, ACT.Copy)
                act.activation(BigB[:, 0, :, 0:NS], src[:, :, NS:P], ACT.Copy, scale=-1.0).then_inc(s_bigA, 1)
                if b % 8 == 7:
                    for bb in range(b - 7, b + 1):
                        act.wait_ge(s_yy, bb + 1)
                        if bb:
                            act.wait_ge(s_ydr, 16 * bb)
                        for g in range(BG):
                            m = act.activation(Yb[0:NC5, :, GC * g:GC * (g + 1)],
                                               psum[0:NC5, 6, g * P:(g + 1) * P].rearrange("p (t c) -> p t c", t=L5), ACT.Copy)
                        m.then_inc(s_yb, 1)
            for c in range(TC):
                act.wait_ge(s_gin, c + 1)
                act.activation(ytok[:, c, :], ytok[:, c, :], ACT.Gelu_apprx_tanh).then_inc(s_gl, 1)
            for c in range(TC):
                act.wait_ge(s_glt, 2 * c + 1)
                act.activation(hnT[:, 0:4, c * P:(c + 1) * P], psum[:, 2 * c, :].rearrange("p (q t) -> p q t", q=4),
                               ACT.Copy).then_inc(s_glA, 1)
            for j in range(2):
                g = gidx[f"gg{j}"]
                for b in range(4):
                    act.wait_ge(s_grp, 4 * g + b + 1)
                    if j:
                        act.wait_ge(s_drD, cumD[gidx[f"go{j - 1}"]] - 3 + b)
                    act.activation(gtmp[:, b, :], psum[:, 4 * (g % 2) + b, :], ACT.Sigmoid).then_inc(s_drA, 1)

            act.wait_ge(s_pT, 2)
            act.activation(pT1[:, 0, :], psum[:, 0, :], ACT.Copy).then_inc(s_ac, 1)
            norm(4, h_ready[4])
            act.wait_ge(s_top, 1)
            act.activation(gate[:, 2, :], gate[:, 0, :], ACT.Exp).then_inc(s_gexp, 1)
            act.wait_ge(s_plan, 1)

            def unit_act(u, two):
                toks = 2 * P if two else P

                def split(n):
                    tile_wait(act, u, n)
                    act.wait_ge(s_mt, tiles_done(u, n + 1 - WSLOTS))
                    act.activation(w_high[n % WSLOTS], unit_tile(n), ACT.Copy).then_inc(s_wh, 1)

                if two:
                    split(0)
                act.wait_ge(s_xtp, u + 1)
                for bank in range(4 if two else 1):
                    blk, g = bank // 2, bank % 2
                    m = act.activation((xbH if two else xbT)[:, 4 * g:4 * g + 4, P * blk:P * (blk + 1)],
                                       psum[:, bank, :].rearrange("p (q t) -> p q t", q=4), ACT.Copy)
                    if two:
                        m.then_inc(s_xtA, 1)
                    else:
                        m.then_inc(s_xtA, 4)
                if two:
                    split(1)
                else:
                    act.activation(spare[:, 0:1], eps, ACT.Copy).then_inc(s_wh, PER)
                for s_ in range(STEPS):
                    if two and s_ + 1 < STEPS:
                        split(gate_at(s_ + 1))
                    act.wait_ge(s_mt, tiles_done(u, gate_at(s_) + 1))
                    act.activation(esil[:, s_ % 2, :, 0:toks],
                                   psum[:, s_ % 2, :].rearrange("p (f t) -> p f t", f=2)[:, :, 0:toks], ACT.Silu).then_inc(s_msl, 1)
                    if two:
                        if s_ + 1 < STEPS:
                            split(gate_at(s_ + 1) + 1)
                        split(down_at(s_))
                act.wait_ge(s_mt, tiles_done(u, PER))
                act.wait_ge(s_mys, u * 16 + 32)
                act.activation(yblk[:, 0, :], psum[:, 4:6, :].rearrange("p b n -> p (b n)"), ACT.Copy).then_inc(s_myA, 1)

            units_act = act.value_load(plan_u[0:1, :], min_val=TC, max_val=MAXU)
            with act.Fori(0, MAXU) as u:
                with act.If(u < units_act):
                    blocks_act = act.value_load(plan_n[0:1, bass.ds(u, 1)], min_val=1, max_val=2)
                    with act.If(blocks_act > 1):
                        unit_act(u, True)
                    with act.If(blocks_act < 2):
                        unit_act(u, False)
            norm(5, h_ready[5])
            gate_ple(1)
            norm(6, h_ready[6], False)

        @block.vector
        def _(dve):
            chain = Chain(dve, s_vc)

            def norm(k, turn=True):
                dve.wait_ge(s_rms, k + 1)
                chain.link(dve.reciprocal(stat[:, k, 2, :], stat[:, k, 1, :]))
                chain.settle()
                dve.wait_ge(s_nw[k % 2], 16 * (k // 2 + 1))
                for c in range(TC):
                    dve.scalar_tensor_tensor(out=hn[:, c, :], in0=h[:, c, :], scalar=stat[:, k, 2, c:c + 1],
                                             in1=nw[:, k % 2, :], op0=ALU.mult, op1=ALU.mult).then_inc(s_hn, 1)
                for c in range(TC if turn else 0):
                    dve.wait_ge(s_tp, 8 * TURN[k] + 2 * c + 2)
                    dve.tensor_copy(hnT[:, 4:8, c * P:(c + 1) * P],
                                    psum[:, 2 * c + 1, :].rearrange("p (q t) -> p q t", q=4)).then_inc(s_hD, 1)

            def drain(name, out_of):
                g = gidx[name]
                width = groups[g][2]
                for b in range(4):
                    dve.wait_ge(s_grp, 4 * g + b + 1)
                    dve.tensor_copy(out_of(b), psum[:, 4 * (g % 2) + b, 0:width]).then_inc(s_drD, 1)

            dve.wait_ge(s_parT, 1)
            dve.tensor_copy(parT, psum[:, 7, 0:68]).then_inc(s_parTd, 1)
            norm(0)
            lbl = parT[:, 52:56]
            chain.settle()
            dve.wait_ge(s_parTd, 1)
            dve.tensor_tensor(hgc[:, 0, :], lbl, lbl, ALU.subtract).then_inc(s_lb, 1)
            dve.wait_ge(s_lbc, 1)
            chain.link(dve.reciprocal(hgc[:, 2, :], hgc[:, 1, :]))
            chain.settle()
            chain.link(dve.tensor_tensor(hgc[:, 3, :], hgc[:, 1, :], hgc[:, 2, :], ALU.mult))
            chain.settle()
            chain.link(dve.tensor_tensor(hgc[:, 4, :], hgc[:, 3, :], hgc[:, 3, :], ALU.subtract))
            chain.settle()
            chain.link(dve.tensor_scalar(hgc[:, 5, :], hgc[:, 4, :], LB_FLOOR, None, ALU.max))
            chain.link(dve.tensor_scalar(hgc[:, 6, :], hgc[:, 4, :], -1.0, 1.0, ALU.mult, ALU.add))
            chain.settle()
            chain.link(dve.tensor_tensor(hgc[:, 7, :], hgc[:, 4, :], hgc[:, 5, :], ALU.subtract))
            chain.settle()
            drain_v = lambda: drain("v", lambda b: vtok[:, b, :])
            drain_v()
            for d, name in enumerate(("ff", "fb")):
                dve.wait_ge(s_drA, cumA[gidx[name]])
                for b in range(4):
                    dve.tensor_scalar(kT[d][:, b, :], kT[d][:, b, :], hgc[:, 6, b:b + 1], hgc[:, 7, b:b + 1],
                                      ALU.mult, ALU.add).then_inc(s_k, 1)
                    chain.link(dve.tensor_scalar(lf[d][:, b, :], lf[d][:, b, :], hgc[:, 6, b:b + 1], hgc[:, 5, b:b + 1],
                                                 ALU.mult, ALU.add))
                chain.settle()
                chain.link(dve.tensor_scalar(lnb4, lf[d], 1.0 / LN_SPLIT, 1.0, ALU.mult, ALU.min))
                chain.settle()
                dve.tensor_scalar(lf[d], lf[d], LN_SPLIT, None, ALU.max).then_inc(s_lnin, 1)
                dve.wait_ge(s_lnout, d + 1)
                dve.tensor_tensor(lf[d], lf[d], lnb4, ALU.add).then_inc(s_lf, 1)

            def scores(n):
                hd, l, d = n // 18, (n % 18) // 2, n % 2
                dve.wait_ge(s_gram, n + 1)
                bank = psum[:, n % 4, :]
                if l < 7:
                    if (l, d) == (0, 0):
                        dve.wait_ge(s_sd, hd + 1)
                    else:
                        dve.wait_ge(s_gdr, n)
                    m = dve.copy_predicated(S_diag, masks[:, 2 * l + d, :].unsqueeze(1).broadcast_to([P, TC, P]),
                                            bank.rearrange("p (c t) -> p c t", c=TC))
                elif l == 7:
                    out_ = S_main.rearrange("p (i s) (a e t) -> p i s a e t", s=2, a=2, e=2)
                    for i in range(2):
                        s0, t0 = (2 * i, 2 * i + 1) if d == 0 else (2 * i + 1, 2 * i)
                        m = dve.tensor_copy(S_main[:, s0, t0 * P:(t0 + 1) * P], bank[:, i * P:(i + 1) * P])
                else:
                    s0, t0 = (0, 2) if d == 0 else (2, 0)
                    m = dve.tensor_copy(S_main[:, s0:s0 + 2, t0 * P:(t0 + 2) * P], bank.rearrange("p (i t) -> p i t", i=2))
                m.then_inc(s_gdr, 1)

            def hg_finish(hd):
                dve.wait_ge(s_orms, hd + 1)
                chain.link(dve.reciprocal(orms, orms))
                chain.settle()
                chain.link(dve.tensor_tensor(orms, psum[:, 5 + hd % 2, :], orms, ALU.mult))
                chain.settle()
                dve.scalar_tensor_tensor(out=mixT[:, hd, :], in0=orms, scalar=parT[:, 48 + hd:49 + hd], in1=gT[:, hd, :],
                                         op0=ALU.mult, op1=ALU.mult).then_inc(s_mix, 1)

            dve.wait_ge(s_drA, cumA[gidx["g"]])
            for hd in range(HEADS):
                for j in range(18):
                    n, l, d = hd * 18 + j, j // 2, j % 2
                    hs = 1 << l
                    near, far = (0, 1) if d == 0 else (1, 0)
                    X = Xb[n % 4]
                    dve.wait_ge(s_exp, n + 1)
                    dve.tensor_tensor(half(X, hs, far), half(X, hs, far), half(qT[:, hd, :], hs, far), ALU.mult)
                    dve.tensor_tensor(half(X, hs, near), half(X, hs, near), half(kT[d][:, hd, :], hs, near),
                                      ALU.mult).then_inc(s_X, 1)
                    if j == 2:
                        dve.wait_ge(s_dg, hd + 1)
                        if hd:
                            dve.wait_ge(s_o, hd)
                        dve.tensor_tensor(S_diag, psum[:, 4, :].rearrange("p (c t) -> p c t", c=TC),
                                          ident.unsqueeze(1).broadcast_to([P, TC, P]), ALU.mult).then_inc(s_sd, 1)
                    if j >= 3:
                        scores(n - 3)
                    if hd and j == 13:
                        hg_finish(hd - 1)
                for n in range(hd * 18 + 15, hd * 18 + 18):
                    scores(n)
            hg_finish(HEADS - 1)

            dve.wait_ge(s_pad, 1)
            drain("xs", lambda b: raw[:, b, 2:2 + T])
            drain("bc", lambda b: raw[:, 4 + b, 2:2 + T])
            drain("dt", lambda b: dtr[:, :, b, :])
            dve.wait_ge(s_tokp, 48)
            dve.wait_ge(s_drD, cumD[gidx["dt"]])
            chain.link(dve.tensor_tensor(dtr, dtr, dtb.rearrange("p (d k) -> p d k", d=2).unsqueeze(2).broadcast_to([P, 2, 4, 8]),
                                         ALU.add))
            chain.settle()
            chain.link(dve.tensor_scalar(dts, dtr, -1.0, None, ALU.mult))
            chain.settle()
            dve.tensor_tensor(dtt, dtr, dts, ALU.max).then_inc(s_sp, 1)
            dve.tensor_scalar(dtr, dtr, 0.0, None, ALU.max).then_inc(s_sp, 1)
            dve.wait_ge(s_ac, 3)
            dve.wait_ge(s_sp, 2)
            chain.link(dve.tensor_tensor(dts, dtr, dtt, ALU.add))
            chain.settle()
            chain.link(dve.tensor_tensor(dta, dts, aneg.rearrange("p (d k) -> p d k", d=2).unsqueeze(2).broadcast_to([P, 2, 4, 8]),
                                         ALU.mult))
            chain.settle()
            dve.tensor_scalar(dta, dta, -1.0, None, ALU.mult).then_inc(s_dt, 1)
            for c in range(TC):
                b = 4 + 2 * (c % 2)
                dve.wait_ge(s_xt, c + 1)
                dve.tensor_copy(xst[:, c, :], psum[:, b, :])
                dve.tensor_copy(btok[:, c, :], psum[:, b + 1, 0:256]).then_inc(s_xtd, 1)
            dve.wait_ge(s_ex, 1)
            exA = ex[:, 0:64].rearrange("p (d c k) -> p d c k", d=2, c=4)
            tot = ex[:, 128:192].rearrange("p (d c k) -> p d c k", d=2, c=4)
            heads = lambda ap: ap.rearrange("p (k n) -> p k n", k=MH)
            for m_, (d, c) in enumerate(SSD_STATES):
                dve.wait_ge(s_st, m_ + 1)
                bank = psum[:, m_ % 2, :]
                slot = c if d == 0 else c - 1
                new = Hst[d][:, slot, :]
                if m_ < 2:
                    dve.tensor_copy(new, bank).then_inc(s_H, 1)
                else:
                    old = Hst[d][:, slot - 1 if d == 0 else slot + 1, :]
                    dve.wait_ge(s_H, m_ - 1)
                    chain.link(dve.tensor_tensor(heads(new), heads(old), tot[:, d, c, :].unsqueeze(2).broadcast_to([P, MH, MP]), ALU.mult))
                    chain.settle()
                    dve.tensor_tensor(new, new, bank, ALU.add).then_inc(s_H, 1)
            for c in range(TC):
                dve.wait_ge(s_cb, c + 1)
                for d in range(2):
                    m = dve.tensor_tensor(cbm[:, d, :, :], psum[:, 2, 0:256].rearrange("p (g t) -> p g t", g=2),
                                          (LE_, GE_)[d].unsqueeze(1).broadcast_to([P, GROUPS, P]), ALU.mult)
                m.then_inc(s_cbm, 1)
                dve.wait_ge(s_cbm, c + 1)
                dve.wait_ge(s_E, c + 1)
                for d in range(2):
                    for g in range(GROUPS):
                        e = Ew[:, d, HPG * g:HPG * (g + 1), :]
                        m = dve.tensor_tensor(e, e, cbm[:, d, g, :].unsqueeze(1).broadcast_to([P, HPG, P]), ALU.mult)
                m.then_inc(s_w, 1)
                y = yst[:, c, :]
                dve.wait_ge(s_xtd, c + 1)
                chain.link(dve.tensor_tensor(heads(y), heads(xst[:, c, :]), dskip.unsqueeze(2).broadcast_to([P, MH, MP]), ALU.mult))
                dve.wait_ge(s_y, c + 1)
                dirs = [d for d in range(2) if c != (0, TC - 1)[d]]
                for d in dirs:
                    chain.settle()
                    chain.link(dve.tensor_tensor(heads(ytmp), heads(psum[:, d, :]), exA[:, d, c, :].unsqueeze(2).broadcast_to([P, MH, MP]), ALU.mult))
                    chain.settle()
                    chain.link(dve.tensor_tensor(y, y, ytmp, ALU.add))
                chain.settle()
                dve.tensor_tensor(y, y, psum[:, 3, :], ALU.add).then_inc(s_yd, 1)
                dve.wait_ge(s_yd, c + 1)
                dve.wait_ge(s_drA, cumA[gidx["z"]])
                dve.tensor_tensor(y, y, zs[:, c, :], ALU.mult).then_inc(s_yz, 1)
            dve.wait_ge(s_yrms, 1)
            chain.link(dve.reciprocal(ssy[:, 2, :], ssy[:, 1, :]))
            chain.settle()
            for c in range(TC):
                for g in range(GROUPS):
                    y = yst[:, c, g * 256:(g + 1) * 256]
                    m = dve.tensor_scalar(y, y, ssy[:, 2, 2 * c + g:2 * c + g + 1], None, ALU.mult)
                m.then_inc(s_yn, 1)
            for c in range(TC):
                dve.wait_ge(s_yt, c + 1)
                dve.tensor_tensor(mixT[:, 4:8, c * P:(c + 1) * P], psum[:, 4 + c % 2, :].rearrange("p (q t) -> p q t", q=4),
                                  parT[:, 56:60].unsqueeze(2).broadcast_to([P, 4, P]), ALU.mult).then_inc(s_ym, 1)

            def add_to_h(name, half_):
                g = gidx[name]
                for b in range(4):
                    dve.wait_ge(s_grp, 4 * g + b + 1)
                    hh = h[:, b, 512 * half_:512 * (half_ + 1)]
                    dve.tensor_tensor(hh, hh, psum[:, 4 * (g % 2) + b, :], ALU.add).then_inc(s_drD, 1)

            add_to_h("o0", 0)
            add_to_h("o1", 1)
            norm(1)
            for j in range(FJ):
                g = gidx[f"fu{j}"]
                for b in range(4):
                    dve.wait_ge(s_grp, 4 * g + b + 1)
                    dve.wait_ge(s_drA, cumA[gidx[f"fg{j}"]] - 3 + b)
                    dve.tensor_tensor(hT[:, 4 * j + b, :], silT[:, b, :], psum[:, 4 * (g % 2) + b, :],
                                      ALU.mult).then_inc(s_drD, 1)
            for c in range(TC):
                for hf in range(2):
                    dve.wait_ge(s_ffd, 4 * hf + c + 1)
                    hh = h[:, c, 512 * hf:512 * (hf + 1)]
                    dve.tensor_tensor(hh, hh, psum[:, 2 * c + hf, :], ALU.add).then_inc(s_fd, 1)

            def embed_parts(layer):
                pT_, pp_ = ((pT, pp), (pT1, pp1))[layer]
                dve.wait_ge(s_pT, layer + 1)
                dve.wait_ge(s_ac, 4 + layer)
                dve.tensor_copy(pT_[:, 1, :], psum[:, 1, :]).then_inc(s_pTd, 1)
                for c in range(TC):
                    for hf in range(2):
                        dve.wait_ge(s_pp, 8 * layer + 2 * c + hf + 1)
                        dve.tensor_copy(pp_[:, c, 512 * hf:512 * (hf + 1)], psum[:, 2 * c + hf, :]).then_inc(s_ppd, 1)

            def embed_add(layer):
                pp_ = (pp, pp1)[layer]
                gates = pgate.rearrange("p k t -> p (k t)").rearrange("p (c n) -> p c n", c=4)
                for c in range(TC):
                    dve.wait_ge(s_drA, cumA[gidx[f"pg{layer}1"]] - 3 + c)
                    dve.wait_ge(s_ppd, 8 * (layer + 1))
                    chain.link(dve.tensor_tensor(pp_[:, c, :], pp_[:, c, :], gates[:, c, :], ALU.mult))
                    chain.settle()
                    dve.tensor_tensor(h[:, c, :], h[:, c, :], pp_[:, c, :], ALU.add).then_inc(s_ph, 1)

            embed_parts(0)
            norm(2)
            embed_add(0)

            tt = lambda o, a, b, op: chain.link(dve.tensor_tensor(o, a, b, op))
            ts = lambda o, a, s1, s2, op0, op1=ALU.bypass: chain.link(dve.tensor_scalar(o, a, s1, s2, op0, op1))
            dve.wait_ge(s_s5in, 16 * 10)
            dve.wait_ge(s_sin, 1)
            dve.tensor_scalar(r_x, r_are, r_ls, None, ALU.mult).then_inc(s_ang, 1)
            ts(r_th, r_aim, r_ls, None, ALU.mult)
            chain.settle()
            ts(r_k, r_th, 1.0 / TWO_PI, ROUND, ALU.mult, ALU.add)
            chain.settle()
            ts(r_k, r_k, ROUND, None, ALU.subtract)
            chain.settle()
            r = r_th
            for part in PI_PARTS:
                chain.link(dve.scalar_tensor_tensor(out=r_r, in0=r_k, scalar=-part, in1=r, op0=ALU.mult, op1=ALU.add))
                chain.settle()
                r = r_r
            dve.tensor_scalar(r_r, r_r, PI_MAX, -PI_MAX, ALU.min, ALU.max).then_inc(s_ang, 1)
            dve.wait_ge(s_sin, 3)
            tt(r_t0, r_c, r_c, ALU.mult)
            chain.settle()
            ts(r_t0, r_t0, -2.0, 1.0, ALU.mult, ALU.add)
            chain.settle()
            chain.link(dve.memset(PR[:, 0, :], 1.0))
            chain.link(dve.memset(PI[:, 0, :], 0.0))
            tt(PR[:, 1, :], r_x, r_t0, ALU.mult)
            tt(PI[:, 1, :], r_x, r_s, ALU.mult)
            tt(r_den, r_are, r_are, ALU.mult)
            tt(r_t1, r_aim, r_aim, ALU.mult)
            chain.settle()
            tt(r_den, r_den, r_t1, ALU.add)
            ts(r_nr, PR[:, 1, :], -1.0, None, ALU.add)
            chain.settle()
            chain.link(dve.reciprocal(r_den, r_den))
            for o, u1, w1, u2, w2, op in ((r_cr, r_nr, r_are, PI[:, 1, :], r_aim, ALU.add),
                                          (r_ci, PI[:, 1, :], r_are, r_nr, r_aim, ALU.subtract)):
                tt(r_t0, u1, w1, ALU.mult)
                tt(r_t1, u2, w2, ALU.mult)
                chain.settle()
                tt(o, r_t0, r_t1, op)
                chain.settle()
                tt(o, o, r_den, ALU.mult)
                chain.settle()

            def complex_product(zr, zi, ar, ai, br, bi, s0, s1):
                tt(s0, ar, br, ALU.mult)
                tt(s1, ai, bi, ALU.mult)
                chain.settle()
                tt(zr, s0, s1, ALU.subtract)
                chain.settle()
                tt(s0, ar, bi, ALU.mult)
                tt(s1, ai, br, ALU.mult)
                chain.settle()
                tt(zi, s0, s1, ALU.add)
                chain.settle()

            s0, s1 = WR, WI
            for n in (1, 2, 4):
                many = lambda ap: ap[:, n:n + 1, :].broadcast_to([P, n, NS])
                complex_product(PR[:, n + 1:2 * n + 1, :], PI[:, n + 1:2 * n + 1, :], PR[:, 1:n + 1, :], PI[:, 1:n + 1, :],
                                many(PR), many(PI), s0[:, 0:n, :], s1[:, 0:n, :])
            scr = rowt.rearrange("p k m q n -> p (k m q n)")
            sc = [scr[:, n * L5 * NS:(n + 1) * L5 * NS].rearrange("p (m n) -> p m n", m=L5) for n in range(2)]
            rows = lambda ap: ap.unsqueeze(1).broadcast_to([P, L5, NS])
            complex_product(WR, WI, PR[:, 0:L5, :], PI[:, 0:L5, :], rows(r_cr), rows(r_ci), sc[0], sc[1])
            for k, (src, sign0, sign1, m) in enumerate(((PR, 1, -1, M5), (PI, -1, -1, M5), (WR, 1, 1, L5), (WI, -1, 1, L5))):
                for q, sign in enumerate((sign0, sign1)):
                    ts(rowt[:, k, 0:m, q, :], src[:, 0:m, :], float(sign), None, ALU.mult)
            for q in range(2):
                ts(rowt[:, 4, 0, q, :], PR[:, L5, :], 1.0, None, ALU.mult)
                ts(rowt[:, 4, 1, q, :], PI[:, L5, :], 1.0, None, ALU.mult)
            chain.settle()
            dve.tensor_copy(r_t0, r_t1).then_inc(s_rowt, 1)
            for n in range(16):
                dve.wait_ge(s_rt, n + 1)
                d, b = n // 8, n % 8
                bank = psum[:, n % 4, :]
                dve.tensor_copy(Cst[:, d, 8 * b:8 * b + 8, :], bank[:, 0:P].rearrange("p (g c) -> p g c", g=8))
                dve.tensor_copy(Csw[:, d, 8 * b:8 * b + 8, :], bank[:, P:2 * P].rearrange("p (g c) -> p g c", g=8)).then_inc(s_cst, 1)
            for n, (k, m_) in enumerate(ROW_TABLES):
                dve.wait_ge(s_rt, 16 + n + 1)
                bank = psum[:, 4 + n % 4, 0:P]
                fwd, bwd = bank[:, 0:G5], bank[:, G5:2 * G5]
                if k < 4:
                    table = (PA, PB, WA, WB)[k]
                    mf, mb = (m_, L5 - m_) if k < 2 else (L5 - 1 - m_, m_)
                    dve.tensor_copy(table[:, 0, :, mf], fwd)
                    m = dve.tensor_copy(table[:, 1, :, mb], bwd)
                elif m_ == 0:
                    m = dve.tensor_copy(LR.rearrange("p d g -> p (d g)"), bank)
                else:
                    pair = bank.rearrange("p (d g) -> p d g", d=2)
                    dve.tensor_copy(LI[:, :, 0, :], pair)
                    m = dve.tensor_scalar(LI[:, :, 1, :], pair, -1.0, None, ALU.mult)
                m.then_inc(s_cst, 1)
            norm(3, False)
            dve.wait_ge(s_cst, 16 + len(ROW_TABLES))
            chain.settle()
            dve.tensor_copy(stat[:, 3, 1, 0:1], stat[:, 3, 2, 0:1]).then_inc(s_tabD, 1)
            for n in range(8):
                dve.wait_ge(s_ut, n + 1)
                dve.tensor_copy(U[:, 8 * n:8 * n + 8, :], psum[:, n, :].rearrange("p (g n) -> p g n", g=8)).then_inc(s_u, 1)
            dve.wait_ge(s_ut, 8)
            for hf in range(2):
                if hf:
                    dve.wait_ge(s_yy, 8)
                dve.memset(Z[0][:, 0:ZS], 0.0)
                dve.memset(Z[1][:, NC5 * ZS:], 0.0).then_inc(s_z0, 1)
                for b in range(8 * hf, 8 * hf + 8):
                    g0 = BG * b
                    if b % 8:
                        dve.wait_ge(s_bt, b)
                    for d in range(2):
                        chain.link(dve.tensor_tensor(BP[:, d, :, :].rearrange("p g (m c) -> p g m c", m=L5),
                                                     Bst[:, g0:g0 + BG, :].unsqueeze(2).broadcast_to([P, BG, L5, GC]),
                                                     WA[:, d, g0:g0 + BG, :].unsqueeze(3).broadcast_to([P, BG, L5, GC]), ALU.mult))
                    chain.settle()
                    dve.wait_ge(s_t2, 16 * hf + (b - 8 * hf) + 1)
                    dve.tensor_tensor(BP, BP, BQ, ALU.add).then_inc(s_bp, 1)
                    dve.wait_ge(s_bp, b + 1)
                    gl = g0 - HALF * hf
                    for d in range(2):
                        at = GC * (L5 - 1) * (1 - d)
                        dve.tensor_copy(BBk[:, d, gl:gl + BG, :], BP[:, d, :, at:at + GC])
                    dve.wait_ge(s_bt, b + 1)
                    if b % 8:
                        dve.wait_ge(s_v, b)
                    src = psum[:, 1, :].rearrange("p (g n) -> p g n", g=BG)
                    dve.tensor_copy(BigB[:, 1, :, NS:192], src)
                    dve.tensor_scalar(BigB[:, 1, :, 0:NS], src[:, :, NS:P], -1.0, None, ALU.mult).then_inc(s_bigD, 1)
                    dve.wait_ge(s_v, b + 1)
                    for d in range(2):
                        z = Z[d][:, (1 - d) * ZS:(1 - d) * ZS + NC5 * ZS].rearrange("p (n e g) -> p n e g", e=2, g=HALF)
                        for e in range(2):
                            m = dve.tensor_copy(z[:, :, e, gl:gl + BG],
                                                psum[:, 2 + d, e * 256:(e + 1) * 256].rearrange("p (g n) -> p n g", g=BG))
                    m.then_inc(s_vd, 1)
                dve.wait_ge(s_vd, 8 * (hf + 1))
                dve.wait_ge(s_z0, hf + 1)
                dve.wait_ge(s_bt, 8 * (hf + 1))
                scan(dve, chain, 0, hf, s_zf)
                for b in range(8 * hf, 8 * hf + 8):
                    g0 = BG * b
                    if b % 8:
                        dve.wait_ge(s_yy, b)
                    for d in range(2):
                        chain.link(dve.tensor_tensor(CP[:, d, :, :].rearrange("p g (m c) -> p g m c", m=M5),
                                                     Cst[:, d, g0:g0 + BG, :].unsqueeze(2).broadcast_to([P, BG, M5, GC]),
                                                     PA[:, d, g0:g0 + BG, :].unsqueeze(3).broadcast_to([P, BG, M5, GC]), ALU.mult))
                    chain.settle()
                    dve.wait_ge(s_t2, 16 * hf + 8 + (b - 8 * hf) + 1)
                    dve.tensor_tensor(CP, CP, CQ, ALU.add).then_inc(s_cp, 1)
                    dve.wait_ge(s_kk, b + 1)
                    if b % 8:
                        dve.wait_ge(s_kb, 16 * L5 * b)
                    kf = psum[0:GC, 4, :].rearrange("p (g j c) -> p g j c", g=BG, j=L5)
                    kb = psum[0:GC, 5, :].rearrange("p (g j c) -> p g j c", g=BG, j=L5)
                    KJ_ = KJ[0:GC, :, :, :]
                    chain.link(dve.tensor_copy(KJ_[:, :, L5 - 1:2 * L5 - 1, :], kf))
                    dve.tensor_copy(KJ_[:, :, 0:L5 - 1, :], kb[:, :, 0:L5 - 1, :])
                    chain.settle()
                    dve.tensor_tensor(KJ_[:, :, L5 - 1, :], KJ_[:, :, L5 - 1, :], kb[:, :, L5 - 1, :], ALU.add).then_inc(s_kj, 1)
            dve.wait_ge(s_yin, 16)
            dve.wait_ge(s_dw, 16)
            for c in range(TC):
                chain.link(dve.tensor_tensor(hn[:, c, :], hn[:, c, :], skip_w, ALU.mult))
                chain.settle()
                dve.tensor_tensor(ytok[:, c, :], ytok[:, c, :], hn[:, c, :], ALU.add).then_inc(s_gin, 1)
            for c in range(TC):
                dve.wait_ge(s_glt, 2 * c + 2)
                dve.tensor_copy(hnT[:, 4:8, c * P:(c + 1) * P],
                                psum[:, 2 * c + 1, :].rearrange("p (q t) -> p q t", q=4)).then_inc(s_glD, 1)
            for j in range(2):
                g = gidx[f"go{j}"]
                for b in range(4):
                    dve.wait_ge(s_grp, 4 * g + b + 1)
                    dve.wait_ge(s_drA, cumA[gidx[f"gg{j}"]] - 3 + b)
                    chain.link(dve.tensor_tensor(gtmp[:, b, :], gtmp[:, b, :], psum[:, 4 * (g % 2) + b, :], ALU.mult))
                    chain.settle()
                    hh = h[:, b, 512 * j:512 * (j + 1)]
                    dve.tensor_tensor(hh, hh, gtmp[:, b, :], ALU.add).then_inc(s_drD, 1)

            embed_parts(1)
            norm(4)
            dve.wait_ge(s_lg, 1)
            chain.link(dve.tensor_copy(lg.rearrange("p c e -> p (c e)"), psum[:, 0, 0:TC * NE]))
            chain.settle()
            for c in range(TC):
                chain.link(dve.max(out=top[:, c, :], in_=lg[:, c, :]))
            chain.settle()
            dve.tensor_tensor(gate[:, 0, :], top[:, :, 1], top[:, :, 0], ALU.subtract).then_inc(s_top, 1)
            for c in range(TC):
                chain.link(dve.max_index(out=topi[:, c, :], in_max=top[:, c, :], in_values=lg[:, c, :]))
            chain.link(dve.tensor_copy(rowi, psum[:, 1, 128:256]))
            for c in range(TC):
                chain.link(dve.tensor_scalar(parti[:, c:c + 1], psum[:, 1, 64:65], float(c * P), None, ALU.add))
            chain.settle()
            chain.link(dve.tensor_copy(topf, topi[:, :, 0:2]))
            chain.settle()
            for k in range(2):
                chain.link(dve.tensor_tensor(hot[:, k, :, :], rowi[:, 0:NE].unsqueeze(1).broadcast_to([P, TC, NE]),
                                             topf[:, :, k:k + 1].broadcast_to([P, TC, NE]), ALU.is_equal))
            chain.settle()
            dve.tensor_tensor(hot[:, 2, :, :], hot[:, 0, :, :], hot[:, 1, :, :], ALU.add).then_inc(s_hot, 1)
            dve.wait_ge(s_gexp, 1)
            chain.link(dve.tensor_scalar(gate[:, 1, :], gate[:, 2, :], 1.0, None, ALU.add))
            chain.settle()
            chain.link(dve.reciprocal(gate[:, 0, :], gate[:, 1, :]))
            chain.settle()
            chain.link(dve.tensor_tensor(gate[:, 1, :], gate[:, 0, :], gate[:, 2, :], ALU.mult))
            dve.wait_ge(s_rank, 1)
            chain.link(dve.tensor_copy(rk.rearrange("p c e -> p (c e)"), psum[:, 1, 0:TC * NE]))
            chain.link(dve.tensor_copy(cnt, psum[:, 1, 32:32 + NE]))
            chain.settle()

            def blocks_above(out_, in_, op):
                first = 0 if op == ALU.is_gt else 1
                chain.link(dve.tensor_scalar(out_, in_, float(first * P), None, op))
                chain.settle()
                for m_ in range(first + 1, TC):
                    chain.link(dve.scalar_tensor_tensor(out=out_, in0=in_, scalar=float(m_ * P), in1=out_, op0=op, op1=ALU.add))
                    chain.settle()

            blocks_above(nblk, cnt, ALU.is_gt)
            blocks_above(rq, rk, ALU.is_ge)

            def running_sum(a, pair):
                for n, step in enumerate((1, 2, 4)):
                    b = pair[:, n % 2, :]
                    chain.link(dve.tensor_copy(b[:, 0:step], a[:, 0:step]))
                    chain.link(dve.tensor_tensor(b[:, step:NE], a[:, step:NE], a[:, 0:NE - step], ALU.add))
                    chain.settle()
                    a = b
                return a

            end = running_sum(nblk, ends)
            chain.link(dve.tensor_scalar(nun, nblk, 0.0, None, ALU.is_gt))
            chain.settle()
            chain.link(dve.scalar_tensor_tensor(out=nun, in0=nblk, scalar=2.0, in1=nun, op0=ALU.is_gt, op1=ALU.add))
            chain.settle()
            last_unit = running_sum(nun, uend)
            chain.link(dve.scalar_tensor_tensor(out=rk, in0=rq, scalar=-float(P), in1=rk, op0=ALU.mult, op1=ALU.add))
            chain.link(dve.tensor_tensor(nblk, end, nblk, ALU.subtract))
            chain.settle()
            chain.link(dve.tensor_tensor(rq, rq, nblk.unsqueeze(1).broadcast_to([P, TC, NE]), ALU.add))
            chain.settle()
            for src, dst in ((rq, bsel), (rk, rsel)):
                for k in range(2):
                    chain.link(dve.tensor_tensor(rtmp[:, k, :, :], hot[:, k, :, :], src, ALU.mult))
                chain.settle()
                chain.link(dve.tensor_reduce(out=dst, in_=rtmp, axis=AX_X, op=ALU.add))
                chain.settle()
            for k in range(2):
                for c in range(TC):
                    chain.link(dve.tensor_scalar(moe_hotR[:, k, c, :], rowi, rsel[:, k, c:c + 1], None, ALU.is_equal))
                    m = dve.tensor_scalar(moe_hotB[:, k, c, :], rowi[:, 0:SLOTC], bsel[:, k, c:c + 1], parti[:, c:c + 1],
                                          ALU.is_equal, ALU.mult)
            m.then_inc(s_slot, 1)
            chain.link(dve.scalar_tensor_tensor(out=destf, in0=bsel, scalar=float(P), in1=rsel, op0=ALU.mult, op1=ALU.add))
            chain.settle()
            dve.tensor_copy(desti, destf).then_inc(s_myd, 1)
            units = MAXU + 1
            number = rowi[:, 0:units].unsqueeze(2).broadcast_to([P, units, NE])
            each = lambda ap: ap.unsqueeze(1).broadcast_to([P, units, NE])
            chain.link(dve.tensor_tensor(nun, last_unit, nun, ALU.subtract))
            chain.link(dve.tensor_tensor(ecmp[:, 0:units, :], number, each(last_unit), ALU.is_ge))
            chain.settle()
            chain.link(dve.tensor_reduce(out=ef[:, 0:units], in_=ecmp[:, 0:units, :], axis=AX_X, op=ALU.add))
            chain.link(dve.scalar_tensor_tensor(out=usel, in0=nun, scalar=-2.0, in1=nblk, op0=ALU.mult, op1=ALU.add))
            chain.link(dve.tensor_tensor(eown, number, each(nun), ALU.is_ge))
            chain.settle()
            chain.link(dve.tensor_tensor(eown, eown, ecmp[:, 0:units, :], ALU.subtract))
            chain.settle()
            for n, v in enumerate((usel, end)):
                chain.link(dve.tensor_tensor(ecmp[:, 0:units, :], eown, each(v), ALU.mult))
                chain.settle()
                chain.link(dve.tensor_reduce(out=ublk[:, n, :], in_=ecmp[:, 0:units, :], axis=AX_X, op=ALU.add))
                chain.settle()
            chain.link(dve.scalar_tensor_tensor(out=ublk[:, 0, :], in0=rowi[:, 0:units], scalar=2.0, in1=ublk[:, 0, :],
                                                op0=ALU.mult, op1=ALU.add))
            chain.link(dve.tensor_scalar(ef[:, 0:units], ef[:, 0:units], float(NE - 1), None, ALU.min))
            chain.settle()
            chain.link(dve.tensor_tensor(ublk[:, 2, :], ublk[:, 1, :], ublk[:, 0, :], ALU.subtract))
            chain.link(dve.tensor_scalar(ublk[:, 0, :], ublk[:, 0, :], float(MAXB), None, ALU.min))
            chain.settle()
            chain.link(dve.tensor_scalar(ublk[:, 2, :], ublk[:, 2, :], 2.0, 1.0, ALU.is_ge, ALU.add))
            chain.link(dve.tensor_copy(plan_e, ef[:, 0:units]))
            chain.link(dve.tensor_copy(plan_b, ublk[:, 0, :]))
            chain.link(dve.tensor_copy(plan_u, last_unit[:, NE - 1:NE]))
            chain.settle()
            chain.link(dve.tensor_copy(plan_n, ublk[:, 2, :]))
            chain.settle()
            dve.wait_ge(s_tok, 1)
            dve.tensor_copy(slot_tok, psum[:, 2, 0:SLOTC]).then_inc(s_plan, 1)
            dve.wait_ge(s_plan, 1)

            def unit_dve(u, two):
                if not two:
                    dve.memset(spare[:, 1:2], 0.0).then_inc(s_ws, PER)
                toks = 2 * P if two else P

                def split(n):
                    dve.wait_ge(s_wh, u * PER + (n + 1))
                    dve.tensor_tensor(w_low[n % WSLOTS], unit_tile(n), w_high[n % WSLOTS], ALU.subtract).then_inc(s_ws, 1)

                def hidden(s_):
                    dve.wait_ge(s_mt, tiles_done(u, gate_at(s_) + 2))
                    dve.wait_ge(s_msl, u * STEPS + (s_ + 1))
                    hid = ehid[:, s_ % 2, :, 0:toks]
                    dve.tensor_tensor(hid, esil[:, s_ % 2, :, 0:toks],
                                      psum[:, 2 + s_ % 2, :].rearrange("p (f t) -> p f t", f=2)[:, :, 0:toks],
                                      ALU.mult).then_inc(s_mh, 1 if two else 3)
                    if two:
                        done = lambda n: u * (3 * STEPS) + (3 * s_ + n)
                        dve.wait_ge(s_mh, done(1))
                        dve.tensor_copy(ehH[:, s_ % 2, :, :], hid).then_inc(s_mh, 1)
                        dve.wait_ge(s_mh, done(2))
                        dve.tensor_tensor(ehL[:, s_ % 2, :, :], hid, ehH[:, s_ % 2, :, :], ALU.subtract).then_inc(s_mh, 1)

                if two:
                    split(0)
                    for bank in range(4):
                        blk, g = bank // 2, bank % 2
                        dve.wait_ge(s_xtA, u * 4 + (bank + 1))
                        at = (slice(None), slice(4 * g, 4 * g + 4), slice(P * blk, P * (blk + 1)))
                        m = dve.tensor_tensor(xbL[at], psum[:, bank, :].rearrange("p (q t) -> p q t", q=4), xbH[at], ALU.subtract)
                    m.then_inc(s_xtD, 1)
                    split(1)
                else:
                    dve.wait_ge(s_xtp, u + 1)
                    dve.tensor_copy(xbT[:, 4:8, 0:P], psum[:, 1, :].rearrange("p (q t) -> p q t", q=4)).then_inc(s_xtD, 1)
                for s_ in range(STEPS):
                    if two and s_ + 1 < STEPS:
                        split(gate_at(s_ + 1))
                    hidden(s_)
                    if two:
                        if s_ + 1 < STEPS:
                            split(gate_at(s_ + 1) + 1)
                        split(down_at(s_))
                dve.wait_ge(s_mt, tiles_done(u, PER))
                dve.wait_ge(s_mys, u * 16 + 32)
                if two:
                    dve.tensor_copy(yblk[:, 1, :], psum[:, 6:8, :].rearrange("p b n -> p (b n)")).then_inc(s_myd, 1)
                else:
                    dve.memset(yblk[:, 1, 0:1], 0.0).then_inc(s_myd, 1)

            units_dve = dve.value_load(plan_u[0:1, :], min_val=TC, max_val=MAXU)
            with dve.Fori(0, MAXU) as u:
                with dve.If(u < units_dve):
                    blocks_dve = dve.value_load(plan_n[0:1, bass.ds(u, 1)], min_val=1, max_val=2)
                    with dve.If(blocks_dve > 1):
                        unit_dve(u, True)
                    with dve.If(blocks_dve < 2):
                        unit_dve(u, False)
            for c in range(TC):
                dve.wait_ge(s_yg[c], 32)
                for k in range(2):
                    m = dve.scalar_tensor_tensor(out=h[:, c, :], in0=yg[k][:, c, :], scalar=gate[:, k, c:c + 1],
                                                 in1=h[:, c, :], op0=ALU.mult, op1=ALU.add)
                    if k:
                        m.then_inc(s_mc, 1)
                    else:
                        chain.link(m)
                        chain.settle()
            norm(5)
            embed_add(1)
            norm(6, False)

    return None


def kernel(**inputs):
    import numpy as _np
    import concourse.bacc as _bacc
    from concourse import mybir as _mybir
    from concourse.bass_utils import run_bass_kernel_spmd as _run

    nc = _bacc.Bacc("TRN2", target_bir_lowering=False, num_devices=1)
    arrays, args = {}, {}
    for name, v in inputs.items():
        a = _np.ascontiguousarray(v)
        arrays[f"in_{name}_dram"] = a
        args[name] = nc.dram_tensor(f"in_{name}_dram", a.shape, _mybir.dt.from_np(a.dtype), kind="ExternalInput").ap()
    out = nc.dram_tensor("out_0_dram", inputs["x"].shape, _mybir.dt.float32, kind="ExternalOutput").ap()
    build_program(nc, args, out)
    r = _run(nc, [arrays], core_ids=[0])
    return r.results[0]["out_0_dram"]
```
